# Optimizing a Trainium2 kernel written in Bass

```python
import math
import jax, jax.numpy as jnp
from jax import lax
import numpy as np

D_MODEL = 1024
BATCH = 1
SEQ = 256
DEPTH = 2

N_MIXERS = 2
SSM_GROUP = 16
SSM_GROUPS = D_MODEL // SSM_GROUP
SSM_STATE = 64
DT_MIN = 1e-3
DT_MAX = 1e-1
SSM_C_STD = 0.5
SB_HEADS = 16
SB_HEAD_DIM = D_MODEL // SB_HEADS
Q_BLOCK = 128
FFN_HIDDEN = -(-8 * D_MODEL // (3 * 256)) * 256
DEEPNORM_ALPHA = (2 * DEPTH) ** 0.25
DEEPNORM_BETA = (8 * DEPTH) ** -0.25
LN_EPS = 1e-5
N_SSM_LAYERS = (DEPTH + 1) // 2
N_SB_LAYERS = DEPTH // 2


def layer_norm(x, g, b):
    xf = x.astype(jnp.float32)
    mu = jnp.mean(xf, axis=-1, keepdims=True)
    var = jnp.mean(jnp.square(xf - mu), axis=-1, keepdims=True)
    y = (xf - mu) * lax.rsqrt(var + LN_EPS) * g.astype(jnp.float32) + b.astype(jnp.float32)
    return y.astype(x.dtype)

def _cmul(ar, ai, br, bi):
    return ar * br - ai * bi, ar * bi + ai * br

def _ssm_combine(left, right):
    alr, ali, blr, bli = left
    arr, ari, brr, bri = right
    ar, ai = _cmul(arr, ari, alr, ali)
    br, bi = _cmul(arr, ari, blr, bli)
    return ar, ai, br + brr, bi + bri

def s5_mixer(x, a_re, a_im, log_dt, b_re, b_im, c_re, c_im, d_skip, w_glu, w_out):
    bsz, seq, _ = x.shape
    f32 = jnp.float32
    u = x.astype(f32).reshape(bsz, seq, SSM_GROUPS, SSM_GROUP)
    dt = jnp.exp(log_dt.astype(f32))[:, None]
    lam_re = jnp.minimum(a_re.astype(f32), -1e-4)
    lam_im = a_im.astype(f32)
    mag = jnp.exp(lam_re * dt)
    lbar_re = mag * jnp.cos(lam_im * dt)
    lbar_im = mag * jnp.sin(lam_im * dt)
    den = lam_re * lam_re + lam_im * lam_im
    num_re = lbar_re - 1.0
    num_im = lbar_im
    coef_re = (num_re * lam_re + num_im * lam_im) / den
    coef_im = (num_im * lam_re - num_re * lam_im) / den
    bb_re, bb_im = _cmul(coef_re[..., None], coef_im[..., None],
                         b_re.astype(f32), b_im.astype(f32))
    bu_re = jnp.einsum('blgh,gph->lbgp', u, bb_re)
    bu_im = jnp.einsum('blgh,gph->lbgp', u, bb_im)
    a_seq_re = jnp.broadcast_to(lbar_re, (seq, 1, SSM_GROUPS, SSM_STATE))
    a_seq_im = jnp.broadcast_to(lbar_im, (seq, 1, SSM_GROUPS, SSM_STATE))
    _, _, s_re, s_im = lax.associative_scan(
        _ssm_combine, (a_seq_re, a_seq_im, bu_re, bu_im), axis=0)
    y = (jnp.einsum('lbgp,ghp->blgh', s_re, c_re.astype(f32))
         - jnp.einsum('lbgp,ghp->blgh', s_im, c_im.astype(f32)))
    y = y.reshape(bsz, seq, D_MODEL) + d_skip.astype(f32) * x.astype(f32)
    h = jax.nn.gelu(y).astype(x.dtype)
    val, gate = jnp.split(h @ w_glu, 2, axis=-1)
    z = val * jax.nn.sigmoid(gate)
    return (z @ w_out).astype(x.dtype)

def stick_breaking_mixer(x, w_qkv, w_o):
    bsz, seq, _ = x.shape
    f32 = jnp.float32
    q, k, v = jnp.split(x @ w_qkv, 3, axis=-1)
    to_heads = lambda t: t.reshape(bsz, seq, SB_HEADS, SB_HEAD_DIM).transpose(0, 2, 1, 3)
    q, k, v = to_heads(q), to_heads(k), to_heads(v)
    scale = SB_HEAD_DIM ** -0.5
    outs = []
    for blk in range(seq // Q_BLOCK):
        q0 = blk * Q_BLOCK
        kv_len = q0 + Q_BLOCK
        qb = q[:, :, q0:kv_len].astype(f32)
        kb = k[:, :, :kv_len].astype(f32)
        vb = v[:, :, :kv_len]
        z = jnp.einsum('bhqd,bhkd->bhqk', qb, kb) * scale
        t_idx = q0 + jnp.arange(Q_BLOCK)[:, None]
        s_idx = jnp.arange(kv_len)[None, :]
        past = s_idx < t_idx
        log_beta = jax.nn.log_sigmoid(z)
        log_1m_beta = jnp.where(past, jax.nn.log_sigmoid(-z), 0.0)
        between = lax.cumsum(log_1m_beta, axis=3, reverse=True) - log_1m_beta
        weights = jnp.where(past, jnp.exp(log_beta + between), 0.0)
        outs.append(jnp.einsum('bhqk,bhkd->bhqd', weights.astype(vb.dtype), vb))
    o = jnp.concatenate(outs, axis=2)
    o = o.transpose(0, 2, 1, 3).reshape(bsz, seq, D_MODEL)
    return (o @ w_o).astype(x.dtype)

def swiglu_ffn(x, w_gu, w_down):
    g, u = jnp.split(x @ w_gu, 2, axis=-1)
    return (jax.nn.silu(g) * u) @ w_down

def first_inputs(seed: int = 0) -> dict:
    key = jax.random.key(seed)
    ks = jax.random.split(key, 24)
    f32 = jnp.float32
    nrm = lambda k, shape, std: jax.random.normal(k, shape, f32) * std
    G, P, H, D, F = SSM_GROUPS, SSM_STATE, SSM_GROUP, D_MODEL, FFN_HIDDEN
    x = jax.random.normal(ks[0], (BATCH, SEQ, D), f32)
    ssm_a_re = -0.5 + nrm(ks[1], (N_SSM_LAYERS, G, P), 0.01)
    ssm_a_im = (math.pi * jnp.arange(P, dtype=f32))[None, None, :] + nrm(ks[2], (N_SSM_LAYERS, G, P), 0.01)
    ssm_log_dt = jax.random.uniform(ks[3], (N_SSM_LAYERS, G), f32,
                                    minval=math.log(DT_MIN), maxval=math.log(DT_MAX))
    ssm_b_re = nrm(ks[4], (N_SSM_LAYERS, G, P, H), (2 * H) ** -0.5)
    ssm_b_im = nrm(ks[5], (N_SSM_LAYERS, G, P, H), (2 * H) ** -0.5)
    ssm_c_re = nrm(ks[6], (N_SSM_LAYERS, G, H, P), SSM_C_STD)
    ssm_c_im = nrm(ks[7], (N_SSM_LAYERS, G, H, P), SSM_C_STD)
    ssm_d = nrm(ks[8], (N_SSM_LAYERS, D), 1.0)
    ssm_w_glu = nrm(ks[9], (N_SSM_LAYERS, D, 2 * D), D ** -0.5)
    ssm_w_out = nrm(ks[10], (N_SSM_LAYERS, D, D), D ** -0.5 * DEEPNORM_BETA)
    sb_w_qkv = nrm(ks[11], (N_SB_LAYERS, D, 3 * D), D ** -0.5)
    sb_w_o = nrm(ks[12], (N_SB_LAYERS, D, D), D ** -0.5 * DEEPNORM_BETA)
    ffn_w_gu = nrm(ks[13], (DEPTH, D, 2 * F), D ** -0.5)
    ffn_w_down = nrm(ks[14], (DEPTH, F, D), F ** -0.5 * DEEPNORM_BETA)
    ln_mix_g = 1.0 + nrm(ks[15], (DEPTH, D), 0.02)
    ln_mix_b = nrm(ks[16], (DEPTH, D), 0.02)
    ln_ffn_g = 1.0 + nrm(ks[17], (DEPTH, D), 0.02)
    ln_ffn_b = nrm(ks[18], (DEPTH, D), 0.02)
    return {"x": x,
            "ssm_a_re": ssm_a_re, "ssm_a_im": ssm_a_im, "ssm_log_dt": ssm_log_dt,
            "ssm_b_re": ssm_b_re, "ssm_b_im": ssm_b_im,
            "ssm_c_re": ssm_c_re, "ssm_c_im": ssm_c_im, "ssm_d": ssm_d,
            "ssm_w_glu": ssm_w_glu, "ssm_w_out": ssm_w_out,
            "sb_w_qkv": sb_w_qkv, "sb_w_o": sb_w_o,
            "ffn_w_gu": ffn_w_gu, "ffn_w_down": ffn_w_down,
            "ln_mix_g": ln_mix_g, "ln_mix_b": ln_mix_b,
            "ln_ffn_g": ln_ffn_g, "ln_ffn_b": ln_ffn_b}

def first_block(x, ssm_a_re, ssm_a_im, ssm_log_dt, ssm_b_re, ssm_b_im, ssm_c_re, ssm_c_im,
              ssm_d, ssm_w_glu, ssm_w_out, sb_w_qkv, sb_w_o, ffn_w_gu, ffn_w_down,
              ln_mix_g, ln_mix_b, ln_ffn_g, ln_ffn_b):
    h = x
    for i in range(DEPTH):
        j = i // N_MIXERS
        if i % N_MIXERS == 0:
            mix = s5_mixer(h, ssm_a_re[j], ssm_a_im[j], ssm_log_dt[j], ssm_b_re[j], ssm_b_im[j],
                           ssm_c_re[j], ssm_c_im[j], ssm_d[j], ssm_w_glu[j], ssm_w_out[j])
        else:
            mix = stick_breaking_mixer(h, sb_w_qkv[j], sb_w_o[j])
        h = layer_norm(DEEPNORM_ALPHA * h + mix, ln_mix_g[i], ln_mix_b[i])
        h = layer_norm(DEEPNORM_ALPHA * h + swiglu_ffn(h, ffn_w_gu[i], ffn_w_down[i]),
                       ln_ffn_g[i], ln_ffn_b[i])
    return h


ATT_HEADS = 8
ATT_KV_HEADS = 2
ATT_HEAD_DIM = 64
ATT_GROUP = ATT_HEADS // ATT_KV_HEADS
WINDOW = 128
ATT_BLOCK = 128
ROPE_DIM = ATT_HEAD_DIM // 4
ROPE_THETA = 500000.0
M_HEADS = 4
M_QK_DIM = 64
M_V_DIM = 128
M_CHUNK = 64
D_FF = 4 * D_MODEL
EPS = 1e-6

ATT_Q_W = ATT_HEADS * ATT_HEAD_DIM
ATT_KV_W = ATT_KV_HEADS * ATT_HEAD_DIM
M_QK_W = M_HEADS * M_QK_DIM
M_V_W = M_HEADS * M_V_DIM
IN_WIDTHS = (ATT_Q_W, ATT_KV_W, ATT_KV_W, M_QK_W, M_QK_W, M_V_W, M_V_W, 2 * M_HEADS, 2 * D_MODEL)
D_IN = sum(IN_WIDTHS)


def rmsnorm(x, gain):
    x32 = x.astype(jnp.float32)
    inv = lax.rsqrt(jnp.mean(x32 * x32, axis=-1, keepdims=True) + EPS)
    return (x32 * inv).astype(x.dtype) * gain

def rope_tables(seq_len):
    pos = jnp.arange(seq_len, dtype=jnp.float32)
    inv_freq = ROPE_THETA ** (-jnp.arange(0, ROPE_DIM, 2, dtype=jnp.float32) / ROPE_DIM)
    ang = pos[:, None] * inv_freq[None, :]
    return jnp.cos(ang), jnp.sin(ang)

def partial_rope(x, cos, sin):
    half = ROPE_DIM // 2
    x1 = x[..., :half].astype(jnp.float32)
    x2 = x[..., half:ROPE_DIM].astype(jnp.float32)
    c = cos[None, :, None, :]
    s = sin[None, :, None, :]
    return jnp.concatenate([(x1 * c - x2 * s).astype(x.dtype),
                            (x2 * c + x1 * s).astype(x.dtype),
                            x[..., ROPE_DIM:]], axis=-1)

def sliding_window_attention(q, k, v, sinks):
    B, S, _, hd = q.shape
    nb = S // ATT_BLOCK
    qb = q.reshape(B, nb, ATT_BLOCK, ATT_KV_HEADS, ATT_GROUP, hd)

    def with_prev(t):
        tb = t.reshape(B, nb, ATT_BLOCK, ATT_KV_HEADS, hd)
        prev = jnp.pad(tb, ((0, 0), (1, 0), (0, 0), (0, 0), (0, 0)))[:, :-1]
        return jnp.concatenate([prev, tb], axis=2)

    kb, vb = with_prev(k), with_prev(v)
    scores = jnp.einsum('bnqhgd,bnkhd->bnhgqk', qb, kb).astype(jnp.float32) * (hd ** -0.5)
    blk = jnp.arange(nb)[:, None, None]
    qpos = blk * ATT_BLOCK + jnp.arange(ATT_BLOCK)[None, :, None]
    kpos = (blk - 1) * ATT_BLOCK + jnp.arange(2 * ATT_BLOCK)[None, None, :]
    valid = (kpos >= 0) & (kpos <= qpos) & (qpos - kpos < WINDOW)
    scores = jnp.where(valid[None, :, None, None], scores, -jnp.inf)
    sink = sinks.astype(jnp.float32).reshape(ATT_KV_HEADS, ATT_GROUP)[None, None, :, :, None, None]
    m = jnp.maximum(jnp.max(scores, axis=-1, keepdims=True), sink)
    p = jnp.exp(scores - m)
    probs = (p / (jnp.sum(p, axis=-1, keepdims=True) + jnp.exp(sink - m))).astype(v.dtype)
    out = jnp.einsum('bnhgqk,bnkhd->bnqhgd', probs, vb)
    return out.reshape(B, S, ATT_HEADS * hd)

def mlstm_chunkwise(q, k, v, i_pre, f_pre):
    f32 = jnp.float32
    B, S, H, dk = q.shape
    dv = v.shape[-1]
    L = M_CHUNK
    nc = S // L

    def chunks(t):
        return t.astype(f32).reshape(B, nc, L, H, -1).transpose(0, 1, 3, 2, 4)

    q = chunks(q) * (dk ** -0.5)
    k = chunks(k)
    v = chunks(v)
    log_f = jax.nn.log_sigmoid(f_pre.astype(f32)).reshape(B, nc, L, H).transpose(0, 1, 3, 2)
    log_i = i_pre.astype(f32).reshape(B, nc, L, H).transpose(0, 1, 3, 2)
    b = jnp.cumsum(log_f, axis=-1)
    g = b[..., -1]

    w_end = g[..., None] - b + log_i
    m_loc = jnp.max(w_end, axis=-1)
    e = jnp.exp(w_end - m_loc[..., None])
    dC = jnp.einsum('bnhlv,bnhlk->bnhvk', v * e[..., None], k)
    dn = jnp.einsum('bnhl,bnhlk->bnhk', e, k)

    def step(carry, inp):
        C, n, m = carry
        dC_c, dn_c, g_c, m_loc_c = inp
        m_new = jnp.maximum(g_c + m, m_loc_c)
        a = jnp.exp(g_c + m - m_new)
        s = jnp.exp(m_loc_c - m_new)
        C_new = a[..., None, None] * C + s[..., None, None] * dC_c
        n_new = a[..., None] * n + s[..., None] * dn_c
        return (C_new, n_new, m_new), (C, n, m)

    init = (jnp.zeros((B, H, dv, dk), f32), jnp.zeros((B, H, dk), f32), jnp.zeros((B, H), f32))
    xs = (jnp.moveaxis(dC, 1, 0), jnp.moveaxis(dn, 1, 0), jnp.moveaxis(g, 1, 0), jnp.moveaxis(m_loc, 1, 0))
    _, (C_prev, n_prev, m_prev) = lax.scan(step, init, xs)
    C_prev = jnp.moveaxis(C_prev, 0, 1)
    n_prev = jnp.moveaxis(n_prev, 0, 1)
    m_prev = jnp.moveaxis(m_prev, 0, 1)

    causal = jnp.tril(jnp.ones((L, L), dtype=bool))
    log_d = jnp.where(causal, b[..., :, None] - b[..., None, :] + log_i[..., None, :], -jnp.inf)
    log_inter = b + m_prev[..., None]
    m_t = jnp.maximum(log_inter, jnp.max(log_d, axis=-1))
    w = jnp.exp(log_d - m_t[..., None]) * jnp.einsum('bnhlk,bnhsk->bnhls', q, k)
    a_inter = jnp.exp(log_inter - m_t)
    num = jnp.einsum('bnhls,bnhsv->bnhlv', w, v) + a_inter[..., None] * jnp.einsum('bnhvk,bnhlk->bnhlv', C_prev, q)
    den = jnp.sum(w, axis=-1) + a_inter * jnp.einsum('bnhk,bnhlk->bnhl', n_prev, q)
    h = num / jnp.maximum(jnp.abs(den), jnp.exp(-m_t))[..., None]
    return h.transpose(0, 1, 3, 2, 4).reshape(B, S, H, dv)

def hybrid_layer(x, cos, sin, norm_mix, w_in, att_q_norm, att_k_norm, att_sinks, m_gate_bias,
                 m_head_norm, w_att_branch, w_m_branch, w_out, norm_ffn, w_ff1, w_ff2):
    B, S, _ = x.shape
    h = rmsnorm(x, norm_mix)
    z = h @ w_in
    splits = [int(s) for s in np.cumsum(IN_WIDTHS)[:-1]]
    q_a, k_a, v_a, q_m, k_m, v_m, o_m, if_m, gates = jnp.split(z, splits, axis=-1)

    q_a = partial_rope(rmsnorm(q_a.reshape(B, S, ATT_HEADS, ATT_HEAD_DIM), att_q_norm), cos, sin)
    k_a = partial_rope(rmsnorm(k_a.reshape(B, S, ATT_KV_HEADS, ATT_HEAD_DIM), att_k_norm), cos, sin)
    v_a = v_a.reshape(B, S, ATT_KV_HEADS, ATT_HEAD_DIM)
    att = sliding_window_attention(q_a, k_a, v_a, att_sinks)

    i_pre, f_pre = jnp.split(if_m + m_gate_bias, 2, axis=-1)
    hm = mlstm_chunkwise(q_m.reshape(B, S, M_HEADS, M_QK_DIM),
                         k_m.reshape(B, S, M_HEADS, M_QK_DIM),
                         v_m.reshape(B, S, M_HEADS, M_V_DIM), i_pre, f_pre).astype(x.dtype)
    hm = rmsnorm(hm, m_head_norm.reshape(M_HEADS, M_V_DIM)).reshape(B, S, M_V_W)
    hm = hm * jax.nn.sigmoid(o_m)

    g_a, g_m = jnp.split(gates, 2, axis=-1)
    mixed = jax.nn.sigmoid(g_a) * (att @ w_att_branch) + jax.nn.sigmoid(g_m) * (hm @ w_m_branch)
    x = x + mixed @ w_out

    u = jax.nn.relu(rmsnorm(x, norm_ffn) @ w_ff1)
    return x + (u * u) @ w_ff2

def second_inputs(seed: int = 0) -> dict:
    key = jax.random.key(seed)
    ks = jax.random.split(key, 16)
    nrm = jax.random.normal
    f32 = jnp.float32
    x = nrm(ks[0], (BATCH, SEQ, D_MODEL), f32)
    norm_mix = 1.0 + 0.02 * nrm(ks[1], (DEPTH, D_MODEL), f32)
    w_in = nrm(ks[2], (DEPTH, D_MODEL, D_IN), f32) * D_MODEL ** -0.5
    att_q_norm = 1.0 + 0.02 * nrm(ks[3], (DEPTH, ATT_HEAD_DIM), f32)
    att_k_norm = 1.0 + 0.02 * nrm(ks[4], (DEPTH, ATT_HEAD_DIM), f32)
    att_sinks = 0.5 * nrm(ks[5], (DEPTH, ATT_HEADS), f32)
    i_bias = -1.0 + 0.1 * nrm(ks[6], (DEPTH, M_HEADS), f32)
    f_bias = 3.0 + 0.5 * nrm(ks[7], (DEPTH, M_HEADS), f32)
    m_gate_bias = jnp.concatenate([i_bias, f_bias], axis=-1)
    m_head_norm = 1.0 + 0.02 * nrm(ks[8], (DEPTH, M_V_W), f32)
    w_att_branch = nrm(ks[9], (DEPTH, ATT_Q_W, D_MODEL), f32) * ATT_Q_W ** -0.5
    w_m_branch = nrm(ks[10], (DEPTH, M_V_W, D_MODEL), f32) * M_V_W ** -0.5
    w_out = nrm(ks[11], (DEPTH, D_MODEL, D_MODEL), f32) * D_MODEL ** -0.5
    norm_ffn = 1.0 + 0.02 * nrm(ks[12], (DEPTH, D_MODEL), f32)
    w_ff1 = nrm(ks[13], (DEPTH, D_MODEL, D_FF), f32) * D_MODEL ** -0.5
    w_ff2 = nrm(ks[14], (DEPTH, D_FF, D_MODEL), f32) * D_FF ** -0.5
    return {"x": x, "norm_mix": norm_mix, "w_in": w_in, "att_q_norm": att_q_norm,
            "att_k_norm": att_k_norm, "att_sinks": att_sinks, "m_gate_bias": m_gate_bias,
            "m_head_norm": m_head_norm, "w_att_branch": w_att_branch, "w_m_branch": w_m_branch,
            "w_out": w_out, "norm_ffn": norm_ffn, "w_ff1": w_ff1, "w_ff2": w_ff2}

def second_block(x, norm_mix, w_in, att_q_norm, att_k_norm, att_sinks, m_gate_bias, m_head_norm,
              w_att_branch, w_m_branch, w_out, norm_ffn, w_ff1, w_ff2):
    cos, sin = rope_tables(x.shape[1])
    for layer in range(DEPTH):
        x = hybrid_layer(x, cos, sin, norm_mix[layer], w_in[layer], att_q_norm[layer],
                         att_k_norm[layer], att_sinks[layer], m_gate_bias[layer],
                         m_head_norm[layer], w_att_branch[layer], w_m_branch[layer],
                         w_out[layer], norm_ffn[layer], w_ff1[layer], w_ff2[layer])
    return x


def setup_inputs(seed=0):
    out = dict(first_inputs(seed))
    for name, value in second_inputs(seed + 1).items():
        if name != "x":
            out[name + "_2"] = value
    return out


def reference(
    x, ssm_a_re, ssm_a_im, ssm_log_dt, ssm_b_re, ssm_b_im, ssm_c_re, ssm_c_im, ssm_d, ssm_w_glu,
    ssm_w_out, sb_w_qkv, sb_w_o, ffn_w_gu, ffn_w_down, ln_mix_g, ln_mix_b, ln_ffn_g, ln_ffn_b,
    norm_mix_2, w_in_2, att_q_norm_2, att_k_norm_2, att_sinks_2, m_gate_bias_2, m_head_norm_2,
    w_att_branch_2, w_m_branch_2, w_out_2, norm_ffn_2, w_ff1_2, w_ff2_2,
):
    x = first_block(
        x, ssm_a_re, ssm_a_im, ssm_log_dt, ssm_b_re, ssm_b_im, ssm_c_re, ssm_c_im, ssm_d,
        ssm_w_glu, ssm_w_out, sb_w_qkv, sb_w_o, ffn_w_gu, ffn_w_down, ln_mix_g, ln_mix_b,
        ln_ffn_g, ln_ffn_b,
    )
    return second_block(
        x, norm_mix_2, w_in_2, att_q_norm_2, att_k_norm_2, att_sinks_2, m_gate_bias_2,
        m_head_norm_2, w_att_branch_2, w_m_branch_2, w_out_2, norm_ffn_2, w_ff1_2, w_ff2_2,
    )


_drawn_inputs = setup_inputs


def setup_inputs(seed=0):
    import zlib

    import numpy as np

    out = dict(_drawn_inputs(seed))
    spreads = {}
    factors = {'ssm_a_re': 8.0,
     'norm_mix_2': 2.983,
     'att_q_norm_2': 8.0,
     'att_k_norm_2': 8.0,
     'att_sinks_2': 5.766,
     'm_head_norm_2': 6.953}
    for name, (base, spread) in spreads.items():
        noise = np.random.default_rng([zlib.crc32(name.encode()), seed]).standard_normal(out[name].shape)
        drawn = base * np.exp(spread * noise) if base else spread * noise
        out[name] = __import__('jax').numpy.asarray(drawn.astype(out[name].dtype))
    for name, factor in factors.items():
        out[name] = (out[name] * factor).astype(out[name].dtype)
    return out
```

```python
from contextlib import ExitStack

import numpy as np

import concourse.bass as bass
from concourse import mybir

F32 = mybir.dt.float32
F32R = mybir.dt.float32r
I32 = mybir.dt.int32
ACT = mybir.ActivationFunctionType
ALU = mybir.AluOpType
AX = mybir.AxisListType.X

P = 128
T = 256
D = 1024
KT = D // P
FFN = 2816
FF = 4096
ALPHA = 4.0 ** 0.25
LN_EPS, RMS_EPS = 1e-5, 1e-6
RING = 3
CH = 2048
HALF = CH // 2

SG, SH, SP, SL = 64, 16, 64, 8
SC = T // SL
SB_HEADS, HD = 16, 64
AH, AKV = 8, 2
MH = 4
IN_QKVO = 2304
IN_IF = 8
BIG = -1.0e30

_WIDTHS = [("ident", P), ("mean_d", P), ("negtri", P), ("negones", P), ("sb_keep", P), ("sb_mask", P),
           ("win_prev", P), ("win_diag", P), ("m_mask", P), ("tri", P), ("ones", P), ("mean_h", P), ("mean_v", P),
           ("rot", P), ("cos", T), ("sin", T), ("sel_neg", MH * P), ("sel_pos", MH * P), ("sgn", 8)]
CONST = {}
_at = 0
for _n, _w in _WIDTHS:
    CONST[_n] = (_at, _w)
    _at += _w
N_CONST = _at


def constants():
    c = np.zeros((P, N_CONST), np.float32)

    def put(name, value):
        at, w = CONST[name]
        c[:value.shape[0], at:at + w] = value

    i, j = np.arange(P)[:, None], np.arange(P)[None, :]
    put("ident", (i == j).astype(np.float32))
    put("mean_d", np.full((P, P), 1.0 / D, np.float32))
    put("negtri", -(i >= j).astype(np.float32))
    put("negones", np.full((P, P), -1.0, np.float32))
    put("sb_keep", (i < j).astype(np.float32))
    put("sb_mask", np.where(i < j, 0.0, BIG).astype(np.float32))
    put("win_prev", np.where(j > i, 0.0, BIG).astype(np.float32))
    put("win_diag", np.where(j <= i, 0.0, BIG).astype(np.float32))
    put("m_mask", np.where(i <= j, 0.0, BIG).astype(np.float32))
    put("tri", (i <= j).astype(np.float32))
    put("ones", np.ones((P, P), np.float32))
    put("mean_h", (i // HD == j // HD).astype(np.float32) / HD)
    put("mean_v", np.full((P, P), 1.0 / P, np.float32))
    rd = HD // 4
    half = rd // 2
    rot = np.zeros((P, P), np.float32)
    cos, sin = np.ones((P, T), np.float32), np.zeros((P, T), np.float32)
    inv_freq = np.float32(500000.0) ** (-np.arange(0, rd, 2, dtype=np.float32) / np.float32(rd))
    ang = np.arange(T, dtype=np.float32)[None, :] * inv_freq[:, None]
    for b in (0, HD):
        for f in range(half):
            rot[b + half + f, b + f] = -1.0
            rot[b + f, b + half + f] = 1.0
        cos[b:b + half], cos[b + half:b + rd] = np.cos(ang), np.cos(ang)
        sin[b:b + half], sin[b + half:b + rd] = np.sin(ang), np.sin(ang)
    put("rot", rot)
    put("cos", cos)
    put("sin", sin)
    sel = np.zeros((MH, MH * P), np.float32)
    for h in range(MH):
        sel[h, h * P:(h + 1) * P] = 1.0
    put("sel_neg", -sel)
    put("sel_pos", sel)
    sgn = np.ones((P, 8), np.float32)
    sgn[:SP, 0] = -1.0
    sgn[SP:, 1] = -1.0
    sgn[:, 2] = LN_EPS
    sgn[:, 3] = RMS_EPS
    put("sgn", sgn)
    return c


class Count:

    def __init__(self):
        self.n = 0

    def one(self):
        self.n += 1
        return self.n


class Gemm:

    def __init__(self, name, n, shape, evac, src, x=None, func=None, alpha=None, per=None, scale=None, layer=None,
                 half=False):
        self.name, self.n, self.shape, self.evac, self.src = name, n, shape, evac, src
        self.x, self.func, self.alpha, self.per = x, func, alpha, per
        self.scale, self.layer, self.half = scale, layer, half


def plan(w):

    def kt8(m, col=0):
        v = m.rearrange("(k p) n -> p k n", p=P)
        return lambda i: [v[:, :, bass.ds(i * 256 + col, 256)]]

    def pair(m, gate):
        v = m.rearrange("(k p) (two n) -> two p k n", p=P, two=2)
        return lambda i: [v[1 - gate, :, :, bass.ds(i * P, P)], v[gate, :, :, bass.ds(i * P, P)]]

    def kt2(m):
        v = m.rearrange("(c k p) n -> p c k n", k=2, p=P)
        return lambda i: [v[:, bass.ds(i, 1), :, :]]

    def branch(a, m):
        va = a.rearrange("(k p) n -> p k n", p=P)
        vm = m.rearrange("(k p) n -> p k n", p=P)
        return lambda i: [(va, vm)[i % 2][:, :, 512 * (i // 2):512 * (i // 2) + 512]]

    gs = [Gemm("glu", 8, "kt8", "gated", pair(w["ssm_w_glu"][0], 1), x=0, func=ACT.Sigmoid),
          Gemm("ssm_out", 4, "kt8", "resid", kt8(w["ssm_w_out"][0]), alpha=ALPHA),
          Gemm("gu0", 22, "kt8", "gated", pair(w["ffn_w_gu"][0], 0), x=1, func=ACT.Silu),
          Gemm("down0", 11, "kt2", "resid", kt2(w["ffn_w_down"][0]), alpha=ALPHA, per=1),
          Gemm("q", 4, "kt8", "copy", kt8(w["sb_w_qkv"][0]), x=2, scale=HD ** -0.5),
          Gemm("k", 4, "kt8", "copy", kt8(w["sb_w_qkv"][0], D), x=2, scale=1.0),
          Gemm("v", 4, "kt8", "copy", kt8(w["sb_w_qkv"][0], 2 * D), x=2, scale=1.0),
          Gemm("sb_out", 4, "kt8", "resid", kt8(w["sb_w_o"][0]), alpha=ALPHA),
          Gemm("gu1", 22, "kt8", "gated", pair(w["ffn_w_gu"][1], 0), x=3, func=ACT.Silu),
          Gemm("down1", 11, "kt2", "resid", kt2(w["ffn_w_down"][1]), alpha=ALPHA, per=1)]
    for l in range(2):
        win = w["w_in_2"][l]
        gs += [Gemm(f"in{l}", 7, "kt8", "copy", kt8(win), x=4 + 2 * l, scale=1.0),
               Gemm(f"o{l}", 2, "kt8", "sig_o", kt8(win, 1792), x=4 + 2 * l),
               Gemm(f"gates{l}", 8, "kt8", "sig_g", kt8(win, IN_QKVO + IN_IF), x=4 + 2 * l),
               Gemm(f"mix{l}", 4, "kt4", "mix", branch(w["w_att_branch_2"][l], w["w_m_branch_2"][l]), layer=l),
               Gemm(f"out{l}", 4, "kt8", "resid", kt8(w["w_out_2"][l]), alpha=1.0, half=True),
               Gemm(f"ff1_{l}", 16, "kt8", "relu2", kt8(w["w_ff1_2"][l]), x=5 + 2 * l),
               Gemm(f"ff2_{l}", 16, "kt2", "resid", kt2(w["w_ff2_2"][l]), alpha=1.0, per=2)]
    c = bank = 0
    cnt = {"gated": 0, "act": 0, "relu": 0, "resid": 0, "hid": 0, "seq": 0}
    prev = None
    for g in gs:
        g.c0, g.bank0 = c, bank
        g.gated0, g.act0, g.relu0, g.resid0 = cnt["gated"], cnt["act"], cnt["relu"], cnt["resid"]
        g.in_hid = prev_hid0 if prev else 0
        if g.evac in ("copy", "sig_o", "sig_g"):
            cnt["act"] += g.n
        elif g.evac == "gated":
            cnt["gated"] += g.n
        elif g.evac == "relu2":
            cnt["relu"] += g.n
        elif g.evac == "resid":
            cnt["resid"] += 4
        before = cnt["hid"]
        if g.evac in ("gated", "relu2"):
            cnt["hid"] += g.n
        elif g.evac == "mix":
            cnt["hid"] += 2
        g.hid0 = before
        if g.name == "v":
            cnt["hid"] += 8
        if g.name.startswith("gates"):
            cnt["hid"] += 8
        prev_hid0, prev = before, g
        g.run0 = 0
        c += g.n
        if g.shape == "kt8":
            bank += g.n
    for a, b in zip(gs, gs[1:]):
        if a.evac in ("copy", "sig_o", "sig_g") and b.evac in ("copy", "sig_o", "sig_g"):
            b.run0 = a.run0 + a.n
    return gs, c


def stack(nc, w, out):
    gemms, n_chunks = plan(w)
    G = {g.name: g for g in gemms}
    ctx = ExitStack()
    with ctx:
        base = 16512
        fence = ctx.enter_context(nc.sbuf_tensor("fence", [P, (229344 - base) // 4 - 16], F32))
        del fence
        place = {}
        at = base
        for name, size in [("const", 4 * N_CONST), ("vec", 512), ("misc", 3072), ("raw", 4 * CH * RING),
                           ("wh", 4 * CH * RING), ("wl", 4 * CH * RING), ("res", 8192), ("xh", 8192), ("xl", 8192),
                           ("hh", 32768), ("hl", 32768), ("xc", 8192), ("sq", 4096), ("sg", 6144), ("zt", 2048),
                           ("rstd", 1024), ("extra", 10240)]:
            place[name] = at
            at += size
        assert at <= 229344 - 64, at

        def sb(name, shape, region, off=0, dt=F32):
            return nc.alloc_sbuf_tensor_at(name, shape, dt, offset=place[region] + off)

        const = sb("const", [P, N_CONST], "const")
        raw = [sb(f"raw{s}", [P, CH], "raw", 4 * CH * s) for s in range(RING)]
        w_hi = [sb(f"w_hi{s}", [P, CH], "wh", 4 * CH * s, F32R) for s in range(RING)]
        w_lo = [sb(f"w_lo{s}", [P, CH], "wl", 4 * CH * s, F32R) for s in range(RING)]
        res = sb("res", [P, KT, T], "res")
        x_hi = sb("x_hi", [P, KT, T], "xh", 0, F32R)
        x_lo = sb("x_lo", [P, KT, T], "xl", 0, F32R)
        hid_hi = sb("hid_hi", [P, 32, T], "hh", 0, F32R)
        hid_lo = sb("hid_lo", [P, 32, T], "hl", 0, F32R)
        xn = sb("xn", [P, KT, T], "xc")
        sqr = sb("sqr", [P, 2, 512], "sq")
        gate_sb = sb("gate_sb", [P, RING, 512], "sg")
        prod = sb("prod", [P, 512], "zt")
        rstd = sb("rstd", [P, T], "rstd")
        vec_rows = sb("vec_rows", [108, P], "misc")
        vec = sb("vec", [P, 108], "vec")
        PS = ctx.enter_context(nc.psum_tensor("PS", [P, 8, 512], F32))
        acc = PS[:, 4:8, :]

        def C(name, rows=P):
            a, n = CONST[name]
            return const[0:rows, a:a + n]

        def column(kind, l, k):
            first = {"ln_mix_g": 0, "ln_mix_b": 16, "ln_ffn_g": 32, "ln_ffn_b": 48, "norm_mix": 64,
                     "norm_ffn": 80}
            if kind in first:
                c = first[kind] + 8 * l + k
            else:
                c = {"head": 96 + 4 * l + k, "q_norm": 104 + l, "k_norm": 106 + l}[kind]
            return vec[:, c:c + 1]

        ident = C("ident")

        a_count, v_count = Count(), Count()
        sems = {}

        def S(name):
            if name not in sems:
                sems[name] = ctx.enter_context(nc.semaphore(name))
            return sems[name]

        raw_ready = [S(f"raw_ready{s}") for s in range(RING)]
        act_step, dve_step = S("act_step"), S("dve_step")
        hi_done, lo_dve, lo_pool = S("hi_done"), S("lo_dve"), S("lo_pool")
        chunk_done = S("chunk_done")
        sig_done, z_done = S("sig_done"), S("z_done")
        act_done, relu_done, u_done = S("act_done"), S("relu_done"), S("u_done")
        resid_done, mix_done = S("resid_done"), S("mix_done")
        gated_hi, relu_hi, hid_done = S("gated_hi"), S("relu_hi"), S("hid_done")
        xh_done, xl_done = S("xh_done"), S("xl_done")

        def chunk_loop(eng, n, head, tail, body):
            for i in range(min(head, n)):
                body(i, i % RING, i // RING)
            mid = max(n - head - tail, 0)
            turns = mid // RING
            if turns >= 2:
                with eng.Fori(0, turns) as t:
                    for k in range(RING):
                        body(t * RING + (head + k), (head + k) % RING, t + (head + k) // RING)
                start = head + turns * RING
            else:
                start = head
            for i in range(start, n):
                body(i, i % RING, i // RING)

        def load_chunk(eng, g, idx, k):
            j = g.c0 + idx
            s = (g.c0 + k) % RING
            if not isinstance(j, int) or j >= RING:
                eng.wait_ge(lo_dve, j - (RING - 1))
                eng.wait_ge(lo_pool, j - (RING - 1))
            srcs = g.src(idx)
            if g.shape == "kt2":
                src = srcs[0].rearrange("p c k n -> p (c k) n")
                parts = [src[:, 0:1, :], src[:, 1:2, :]]
                dst = raw[s][:, :].rearrange("p (k n) -> p k n", k=2)
                dsts = [dst[:, 0:1, :], dst[:, 1:2, :]]
            elif g.evac == "gated":
                parts = srcs
                dst = raw[s][:, :].rearrange("p (k m n) -> p m k n", k=8, m=2)
                dsts = [dst[:, 0], dst[:, 1]]
            else:
                kt = 8 if g.shape == "kt8" else 4
                parts = [srcs[0][:, 0:kt // 2, :], srcs[0][:, kt // 2:kt, :]]
                dst = raw[s][:, :].rearrange("p (k n) -> p k n", k=kt)
                dsts = [dst[:, 0:kt // 2, :], dst[:, kt // 2:kt, :]]
            for d, q in zip(dsts, parts):
                eng.dma_start(d, q).then_inc(raw_ready[s], 16)

        def split_hi(act, c, k, turn):
            s = (c + k) % RING
            act.wait_ge(raw_ready[s], turn * 32 + ((c + k) // RING + 1) * 32)
            nc.scalar.activation(w_hi[s][:, :], raw[s][:, :], ACT.Copy).then_inc(hi_done, 1)

        def split_lo(eng, c, idx, k, half, done):
            s = (c + k) % RING
            e = nc.vector if half == 0 else nc.gpsimd
            eng.wait_ge(hi_done, idx + (c + 1))
            cols = slice(half * HALF, (half + 1) * HALF)
            e.tensor_tensor(w_lo[s][:, cols], raw[s][:, cols], w_hi[s][:, cols].bitcast(F32),
                              ALU.subtract).then_inc(done, 1)

        def base_of(g):
            return {"gated": (z_done, g.gated0), "relu2": (relu_done, g.relu0), "resid": (resid_done, g.resid0),
                    }.get(g.evac, (act_done, g.act0))

        def gemm_head(g):
            return 3 if base_of(g)[1] == 0 else 1

        def gemm_tensor(pe, g):
            drained, first = base_of(g)

            def three(dst, lhs_hi, lhs_lo, r_hi, r_lo, start, stop):
                nc.tensor.matmul(dst, lhs_hi, r_hi, start=start, stop=False, skip_group_check=True)
                nc.tensor.matmul(dst, lhs_hi, r_lo, start=False, stop=False, skip_group_check=True)
                return nc.tensor.matmul(dst, lhs_lo, r_hi, start=False, stop=stop, skip_group_check=True)

            def body(idx, k, turn):
                s = (g.c0 + k) % RING
                head = isinstance(idx, int)
                pe.wait_ge(lo_dve, idx + (g.c0 + 1))
                pe.wait_ge(lo_pool, idx + (g.c0 + 1))
                if g.shape == "kt8":
                    bank = (g.bank0 + k) % RING
                    if not head or idx + g.run0 >= RING:
                        pe.wait_ge(drained, idx + (first - 2))
                    hi = w_hi[s][:, :].rearrange("p (k m n) -> p k m n", k=8, m=2)
                    lo = w_lo[s][:, :].rearrange("p (k m n) -> p k m n", k=8, m=2)
                    for m in range(2):
                        for kt in range(KT):
                            if head and idx == 0 and m == 0:
                                if g.x is not None:
                                    pe.wait_ge(xl_done, KT * g.x + kt + 1)
                                else:
                                    pe.wait_ge(hid_done, g.in_hid + (kt // 4 if g.half else kt) + 1)
                            if g.x is not None:
                                a, b = x_hi[:, kt, :], x_lo[:, kt, :]
                            else:
                                t0 = 8 if g.half else 0
                                a, b = hid_hi[:, t0 + kt, :], hid_lo[:, t0 + kt, :]
                            last = three(PS[:, bank, m * T:(m + 1) * T], hi[:, kt, m, :], lo[:, kt, m, :], a, b,
                                         kt == 0, kt == KT - 1)
                elif g.shape == "kt4":
                    which, half = idx % 2, idx // 2
                    if half:
                        pe.wait_ge(mix_done, 4 * g.layer + 2)
                    hi = w_hi[s][:, :].rearrange("p (k m n) -> p k m n", k=4, m=4)
                    lo = w_lo[s][:, :].rearrange("p (k m n) -> p k m n", k=4, m=4)
                    for m in range(4):
                        for kt in range(4):
                            if m == 0 and half == 0:
                                pe.wait_ge(hid_done, g.in_hid + 4 * which + kt + 1)
                            dst = acc[:, 2 * which + m // 2, (m % 2) * T:(m % 2 + 1) * T]
                            last = three(dst, hi[:, kt, m, :], lo[:, kt, m, :], hid_hi[:, 4 * which + kt, :],
                                         hid_lo[:, 4 * which + kt, :], kt == 0, kt == 3)
                else:
                    pe.wait_ge(hid_done, idx * 2 + (g.in_hid + 2) if g.per == 1 else idx + (g.in_hid + 1))
                    hi = w_hi[s][:, :].rearrange("p (k m n) -> p k m n", k=2, m=8)
                    lo = w_lo[s][:, :].rearrange("p (k m n) -> p k m n", k=2, m=8)
                    for kt in range(2):
                        a = hid_hi[:, bass.ds(idx * 2 + kt, 1), :].rearrange("p a t -> p (a t)")
                        b = hid_lo[:, bass.ds(idx * 2 + kt, 1), :].rearrange("p a t -> p (a t)")
                        for m in range(8):
                            last = three(acc[:, m // 2, (m % 2) * T:(m % 2 + 1) * T], hi[:, kt, m, :], lo[:, kt, m, :],
                                         a, b, head and idx == 0 and kt == 0 and m % 2 == 0,
                                         head and idx == g.n - 1 and kt == 1)
                last.then_inc(chunk_done, 1)

            chunk_loop(pe, g.n, gemm_head(g) if g.shape == "kt8" else (4 if g.shape == "kt4" else 1),
                       1 if g.shape == "kt2" else 0, body)

        def gemm_scalar(act, g):
            def body(idx, k, turn):
                bank = (g.bank0 + k) % RING
                act.wait_ge(chunk_done, idx + (g.c0 + 1))
                if g.evac == "gated":
                    nc.scalar.activation(gate_sb[:, k, 0:T], PS[:, bank, T:2 * T], g.func).then_inc(sig_done, 1)
                elif g.evac == "relu2":
                    if not isinstance(idx, int) or g.relu0 + idx >= RING:
                        act.wait_ge(u_done, idx + (g.relu0 - 2))
                    nc.scalar.activation(gate_sb[:, k, :], PS[:, bank, :], ACT.Relu).then_inc(relu_done, 1)
                elif g.evac == "copy":
                    nc.scalar.activation(proj(g, idx), PS[:, bank, :], ACT.Copy, scale=g.scale).then_inc(act_done, 1)
                elif g.evac == "sig_o":
                    nc.scalar.activation(sig_o[:, bass.ds(idx * 2, 2), :].rearrange("p a t -> p (a t)"),
                                         PS[:, bank, :], ACT.Sigmoid).then_inc(act_done, 1)
                elif g.evac == "sig_g":
                    nc.scalar.activation(sig_g[:, bass.ds(idx * 2, 2), :].rearrange("p a t -> p (a t)"),
                                         PS[:, bank, :], ACT.Sigmoid).then_inc(act_done, 1)
                if not isinstance(idx, int) or g.c0 + idx + RING < n_chunks:
                    split_hi(act, g.c0 + RING, k, turn)

            chunk_loop(act, g.n, 3 if g.evac == "relu2" and g.relu0 == 0 else 0,
                       RING if g.c0 + g.n == n_chunks else 0, body)

        def gemm_vector(dve, g):
            def body(idx, k, turn):
                bank = (g.bank0 + k) % RING
                if g.evac == "gated":
                    n = idx + (g.gated0 + 1)
                    dve.wait_ge(sig_done, n)
                    if not isinstance(idx, int) or n > 1:
                        dve.wait_ge(hid_done, idx + g.hid0)
                    hi = hid_hi[:, bass.ds(idx, 1), :].rearrange("p a t -> p (a t)")
                    lo = hid_lo[:, bass.ds(idx, 1), :].rearrange("p a t -> p (a t)")
                    nc.vector.tensor_tensor(prod[:, 0:T], PS[:, bank, 0:T], gate_sb[:, k, 0:T],
                                            ALU.mult).then_inc(z_done, 1)
                    dve.wait_ge(z_done, n)
                    nc.vector.tensor_copy(hi, prod[:, 0:T]).then_inc(gated_hi, 1)
                    dve.wait_ge(gated_hi, n)
                    nc.vector.tensor_tensor(lo, prod[:, 0:T], hi.bitcast(F32), ALU.subtract).then_inc(hid_done, 1)
                elif g.evac == "relu2":
                    n = idx + (g.relu0 + 1)
                    dve.wait_ge(relu_done, n)
                    dve.wait_ge(hid_done, idx + g.hid0)
                    hi = hid_hi[:, bass.ds(idx * 2, 2), :].rearrange("p a t -> p (a t)")
                    lo = hid_lo[:, bass.ds(idx * 2, 2), :].rearrange("p a t -> p (a t)")
                    nc.vector.tensor_tensor(prod[:, :], gate_sb[:, k, :], gate_sb[:, k, :],
                                            ALU.mult).then_inc(u_done, 1)
                    dve.wait_ge(u_done, n)
                    nc.vector.tensor_copy(hi, prod[:, :]).then_inc(relu_hi, 1)
                    dve.wait_ge(relu_hi, n)
                    nc.vector.tensor_tensor(lo, prod[:, :], hi.bitcast(F32), ALU.subtract).then_inc(hid_done, 1)
                elif g.evac == "resid" and g.shape == "kt8":
                    dve.wait_ge(chunk_done, idx + (g.c0 + 1))
                    r = res[:, bass.ds(idx * 2, 2), :].rearrange("p a t -> p (a t)")
                    nc.vector.scalar_tensor_tensor(out=r, in0=r, scalar=g.alpha, in1=PS[:, bank, :], op0=ALU.mult,
                                                   op1=ALU.add).then_inc(resid_done, 1)
                elif g.evac == "mix" and idx % 2 == 1:
                    mix_vector(dve, g, idx // 2)
                if not isinstance(idx, int) or g.c0 + idx + RING < n_chunks:
                    if g.shape == "kt2" and isinstance(idx, int) and idx == g.n - 1:
                        sum_resid(dve, g)
                    split_lo(dve, g.c0 + RING, idx, k, 0, lo_dve)
                elif g.shape == "kt2" and idx == g.n - 1:
                    sum_resid(dve, g)

            chunk_loop(dve, g.n, 4 if g.shape == "kt4" else 0,
                       RING if g.c0 + g.n == n_chunks else (1 if g.shape == "kt2" else 0), body)

        def sum_resid(dve, g):
            dve.wait_ge(chunk_done, g.c0 + g.n)
            for q in range(4):
                r = res[:, 2 * q:2 * q + 2, :].rearrange("p a t -> p (a t)")
                nc.vector.scalar_tensor_tensor(out=r, in0=r, scalar=g.alpha, in1=acc[:, q, :], op0=ALU.mult,
                                               op1=ALU.add).then_inc(resid_done, 1)

        def mix_vector(dve, g, half):
            dve.wait_ge(chunk_done, g.c0 + 2 * half + 2)
            for q in range(2):
                if half or q:
                    dve.wait_ge(dve_step, v_count.n)
                t = 4 * half + 2 * q
                ga = sig_g[:, t:t + 2, :].rearrange("p a t -> p (a t)")
                gm = sig_g[:, 8 + t:10 + t, :].rearrange("p a t -> p (a t)")
                hi = hid_hi[:, 8 + t:10 + t, :].rearrange("p a t -> p (a t)")
                lo = hid_lo[:, 8 + t:10 + t, :].rearrange("p a t -> p (a t)")
                nc.vector.tensor_tensor(prod[:, :], acc[:, q, :], ga, ALU.mult).then_inc(dve_step, 1)
                v_count.one()
                nc.vector.tensor_tensor(gate_sb[:, 0, :], acc[:, 2 + q, :], gm, ALU.mult).then_inc(dve_step, 1)
                v_count.one()
                dve.wait_ge(dve_step, v_count.n)
                ins = nc.vector.tensor_tensor(prod[:, :], prod[:, :], gate_sb[:, 0, :], ALU.add)
                ins.then_inc(mix_done, 1)
                dve.wait_ge(mix_done, 4 * g.layer + 2 * half + q + 1)
                nc.vector.tensor_copy(hi, prod[:, :]).then_inc(dve_step, 1)
                v_count.one()
                dve.wait_ge(dve_step, v_count.n)
                ins = nc.vector.tensor_tensor(lo, prod[:, :], hi.bitcast(F32), ALU.subtract)
                if q == 0:
                    ins.then_inc(dve_step, 1)
                    v_count.one()
                else:
                    ins.then_inc(hid_done, 1)
                    dve.wait_ge(hid_done, g.hid0 + half + 1)

        mean_ready, var_ready, rstd_done = S("mean_ready"), S("var_ready"), S("rstd_done")
        centred, sq_done, sq_used = S("centred"), S("sq_done"), S("sq_used")
        scaled, res_normed = S("scaled"), S("res_normed")
        LN_VEC = [("ln_mix_g", "ln_mix_b", 0), ("ln_ffn_g", "ln_ffn_b", 0), ("ln_mix_g", "ln_mix_b", 1),
                  ("ln_ffn_g", "ln_ffn_b", 1)]
        RMS_VEC = [("norm_mix", 0), ("norm_ffn", 0), ("norm_mix", 1), ("norm_ffn", 1)]

        def x_index(n):
            return n + 1 if n < 3 else n

        def res_wait(eng, n, q):
            if n < 4:
                eng.wait_ge(resid_done, 4 * n + q + 1)
            elif n == 4:
                eng.wait_ge(res_normed, 8 * 3 + 2 * q + 2)
            else:
                eng.wait_ge(resid_done, 4 * (n - 1) + q + 1)

        def norm_tensor(pe, n):
            if n < 4:
                for kt in range(KT):
                    if kt % 2 == 0:
                        res_wait(pe, n, kt // 2)
                    last = nc.tensor.matmul(PS[:, 3, 0:T], C("mean_d"), res[:, kt, :], start=kt == 0, stop=kt == KT - 1)
                last.then_inc(mean_ready, 1)
            for kt in range(KT):
                if kt % 2 == 0:
                    pe.wait_ge(sq_done, 4 * n + kt // 2 + 1)
                last = nc.tensor.matmul(PS[:, 4, 0:T], C("mean_d"), sqr[:, kt // 2 % 2, (kt % 2) * T:(kt % 2 + 1) * T],
                                        start=kt == 0, stop=kt == KT - 1)
                if kt == KT - 1:
                    last.then_inc(var_ready, 1)
                elif kt % 2:
                    last.then_inc(sq_used, 1)

        def norm_scalar(act, n):
            src = xn if n < 4 else res
            for q in range(4):
                if n < 4:
                    act.wait_ge(centred, 4 * n + q + 1)
                else:
                    res_wait(act, n, q)
                if q >= 2:
                    act.wait_ge(sq_used, 3 * n + q - 1)
                nc.scalar.activation(sqr[:, q % 2, :], src[:, 2 * q:2 * q + 2, :].rearrange("p a t -> p (a t)"),
                                     ACT.Square).then_inc(sq_done, 1)
            act.wait_ge(var_ready, n + 1)
            eps = const[:, CONST["sgn"][0] + (2 if n < 4 else 3):][:, 0:1]
            nc.scalar.activation(rstd[:, :], PS[:, 4, 0:T], ACT.Ln, bias=eps).then_inc(act_step, 1)
            a_count.one()
            act.wait_ge(act_step, a_count.n)
            nc.scalar.activation(rstd[:, :], rstd[:, :], ACT.Exp, scale=-0.5).then_inc(rstd_done, 1)
            for kt in range(KT):
                act.wait_ge(scaled, KT * n + kt + 1)
                if n < 4:
                    nc.scalar.activation(res[:, kt, :], xn[:, kt, :], ACT.Identity,
                                         bias=column(LN_VEC[n][1], LN_VEC[n][2], kt)).then_inc(res_normed, 1)
                    if n == 3:
                        continue
                    act.wait_ge(res_normed, KT * n + kt + 1)
                nc.scalar.activation(x_hi[:, kt, :], (res if n < 4 else xn)[:, kt, :], ACT.Copy).then_inc(xh_done, 1)

        def norm_vector(dve, n):
            if n < 4:
                dve.wait_ge(mean_ready, n + 1)
                for q in range(4):
                    nc.vector.tensor_tensor(xn[:, 2 * q:2 * q + 2, :], res[:, 2 * q:2 * q + 2, :],
                                            PS[:, 3, 0:T].unsqueeze(1).to_broadcast([P, 2, T]),
                                            ALU.subtract).then_inc(centred, 1)
            dve.wait_ge(rstd_done, n + 1)
            if n < 4:
                dve.wait_ge(centred, 4 * n + 4)
            for kt in range(KT):
                gain = column(LN_VEC[n][0], LN_VEC[n][2], kt) if n < 4 else column(RMS_VEC[n - 4][0], RMS_VEC[n - 4][1], kt)
                nc.vector.scalar_tensor_tensor(out=xn[:, kt, :], in0=(xn if n < 4 else res)[:, kt, :], scalar=gain,
                                               in1=rstd[:, :], op0=ALU.mult, op1=ALU.mult).then_inc(scaled, 1)
            if n == 3:
                return
            for kt in range(KT):
                m = KT * x_index(n) + kt + 1
                dve.wait_ge(xh_done, m)
                nc.vector.tensor_tensor(x_lo[:, kt, :], (res if n < 4 else xn)[:, kt, :], x_hi[:, kt, :].bitcast(F32),
                                        ALU.subtract).then_inc(xl_done, 1)

        qkv = sb("qkv", [P, 16, T], "hh", 16 * 4 * T)
        v_feat = sb("v_feat", [P, 8, T], "hl", 16 * 4 * T)
        v_tok = sb("v_tok", [P, 2, D], "hl", 24 * 4 * T)
        sb_soft = [sb(f"sb_soft{i}", [P, 2, 384], "sg" if i == 0 else "extra", 0) for i in range(2)]
        sb_nl = [sb(f"sb_nl{i}", [P, 2, 384], "extra", 3072 * (i + 1)) for i in range(2)]
        sb_w = [sb(f"sb_w{i}", [P, 2, 384], "sg" if i == 0 else "sq", 3072 if i == 0 else 0) for i in range(2)]
        vt_ready, vt_done, z_ready, nl_done = S("vt_ready"), S("vt_done"), S("z_ready"), S("nl_done")
        soft_done, cum_ready, w_done, o_ready = S("soft_done"), S("cum_ready"), S("w_done"), S("o_ready")
        sb_hi, sb_raw = S("sb_hi"), S("sb_raw")
        PAIRS = SB_HEADS // 2

        def z_banks(hp):
            return PS[:, 2 * (hp % 2):2 * (hp % 2) + 2, :]

        def sb_tensor(pe):
            pe.wait_ge(act_done, G["v"].act0 + G["v"].n)
            for half in range(2):
                for f in range(8):
                    last = nc.tensor.transpose(PS[:, 4 + 2 * half + f // 4, (f % 4) * P:(f % 4 + 1) * P],
                                               v_feat[:, f, half * P:(half + 1) * P], ident)
                    if f % 4 == 3:
                        last.then_inc(vt_ready, 1)

            def scores(hp):
                if hp >= 2:
                    pe.wait_ge(w_done, hp - 1)
                for hd in range(2):
                    b = HD * hd
                    z = PS[:, 2 * (hp % 2) + hd, :]
                    q, k = qkv[b:b + HD, hp, :], qkv[b:b + HD, 8 + hp, :]
                    nc.tensor.matmul(z[:, 0:T], k[:, 0:P], q, start=True, stop=False, skip_group_check=True)
                    last = nc.tensor.matmul(z[:, T:T + P], k[:, P:T], q[:, P:T], start=False, stop=False,
                                            skip_group_check=True)
                last.then_inc(z_ready, 1)

            def running_sums(hp):
                pe.wait_ge(nl_done, hp + 1)
                for hd in range(2):
                    z = PS[:, 2 * (hp % 2) + hd, :]
                    nl = sb_nl[hp % 2][:, hd, :]
                    for dst, lhs, rhs in ((z[:, 0:T], C("negtri"), nl[:, 0:T]), (z[:, P:T], C("negones"), nl[:, T:T + P]),
                                          (z[:, T:T + P], C("negtri"), nl[:, T:T + P]), (z[:, 0:P], ident, C("sb_mask")),
                                          (z[:, T:T + P], ident, C("sb_mask"))):
                        last = nc.tensor.matmul(dst, lhs, rhs, start=False, stop=True, skip_group_check=True)
                last.then_inc(cum_ready, 1)

            def outputs(hp):
                pe.wait_ge(w_done, hp + 1)
                if hp == 0:
                    pe.wait_ge(vt_done, 4)
                if hp >= 2:
                    pe.wait_ge(hid_done, G["v"].hid0 + hp - 1)
                for hd in range(2):
                    o = PS[HD * hd:HD * hd + HD, 6 + hp % 2, 0:T]
                    h = 2 * hp + hd
                    wt = sb_w[hp % 2][:, hd, :]
                    nc.tensor.matmul(o, v_tok[:, 0, HD * h:HD * h + HD], wt[:, 0:T], start=True, stop=False,
                                     skip_group_check=True)
                    last = nc.tensor.matmul(o[:, P:T], v_tok[:, 1, HD * h:HD * h + HD], wt[:, T:T + P], start=False,
                                            stop=True, skip_group_check=True)
                last.then_inc(o_ready, 1)

            for it in range(PAIRS + 2):
                if it < PAIRS:
                    scores(it)
                if 1 <= it <= PAIRS:
                    running_sums(it - 1)
                if it >= 2:
                    outputs(it - 2)

        def sb_scalar(act):
            for i in range(4):
                act.wait_ge(vt_ready, i + 1)
                nc.scalar.activation(v_tok[:, i // 2, 512 * (i % 2):512 * (i % 2) + 512], PS[:, 4 + i, :],
                                     ACT.Copy).then_inc(vt_done, 1)
            for it in range(PAIRS + 1):
                if it < PAIRS:
                    a = sb_soft[it % 2]
                    act.wait_ge(z_ready, it + 1)
                    if it >= 2:
                        act.wait_ge(nl_done, it - 1)
                    nc.scalar.activation(a[:, :, :], z_banks(it)[:, :, 0:384], ACT.Abs).then_inc(act_step, 1)
                    a_count.one()
                    act.wait_ge(act_step, a_count.n)
                    nc.scalar.activation(a[:, :, :], a[:, :, :], ACT.Exp, scale=-1.0).then_inc(act_step, 1)
                    a_count.one()
                    act.wait_ge(act_step, a_count.n)
                    nc.scalar.activation(a[:, :, :], a[:, :, :], ACT.Ln, bias=1.0).then_inc(soft_done, 1)
                if it >= 1:
                    act.wait_ge(cum_ready, it)
                    if it >= 3:
                        act.wait_ge(o_ready, it - 2)
                    nc.scalar.activation(sb_w[(it - 1) % 2][:, :, :], z_banks(it - 1)[:, :, 0:384],
                                         ACT.Exp).then_inc(w_done, 1)

        def sb_vector(dve):
            keep = C("sb_keep").unsqueeze(1).to_broadcast([P, 2, P])
            for it in range(PAIRS + 2):
                if it < PAIRS:
                    nl = sb_nl[it % 2]
                    dve.wait_ge(soft_done, it + 1)
                    if it >= 2:
                        dve.wait_ge(cum_ready, it - 1)
                    nc.vector.scalar_tensor_tensor(out=nl[:, :, :], in0=z_banks(it)[:, :, 0:384], scalar=0.0,
                                                   in1=sb_soft[it % 2][:, :, :], op0=ALU.max, op1=ALU.add).then_inc(dve_step, 1)
                    v_count.one()
                    dve.wait_ge(dve_step, v_count.n)
                    nc.vector.tensor_tensor(nl[:, :, 0:P], nl[:, :, 0:P], keep, ALU.mult).then_inc(dve_step, 1)
                    v_count.one()
                    dve.wait_ge(dve_step, v_count.n)
                    nc.vector.tensor_tensor(nl[:, :, T:T + P], nl[:, :, T:T + P], keep, ALU.mult).then_inc(nl_done, 1)
                if it >= 2:
                    hp = it - 2
                    dve.wait_ge(o_ready, hp + 1)
                    o = PS[:, 6 + hp % 2, 0:T]
                    nc.vector.tensor_copy(hid_hi[:, hp, :], o).then_inc(sb_hi, 1)
                    dve.wait_ge(sb_hi, hp + 1)
                    nc.vector.tensor_tensor(hid_lo[:, hp, :], o, hid_hi[:, hp, :].bitcast(F32),
                                            ALU.subtract).then_inc(hid_done, 1)

        BQ = 16
        NB = SG // BQ
        x_chunk = sb("x_chunk", [SC, SL, D], "hl")
        y_chunk = sb("y_chunk", [SC, SL, D], "hl")
        toep = sb("toep", [P, SG, P], "hh")
        x_group = sb("x_group", [SC, SG, SL * SH], "hh")
        s_out = sb("s_out", [P, SG, SL + 1, SH], "wh")
        s_in = sb("s_in", [P, BQ, P], "wh", 36864)
        d_diag = sb("d_diag", [SH, SG, SH], "wh", 45056)
        b_rows = [sb(f"b_rows{i}", [SG, 2 * SP * SH], "wh", 8192 * i) for i in range(2)]
        c_rows = sb("c_rows", [P, 8, 4 * SP], "wh", 16384)
        a_rows = sb("a_rows", [SG, 4 * SP], "wh", 24576)
        tab_b = [sb(f"tab_b{i}", [P, SG, SH], "raw", 4096 * i) for i in range(2)]
        tab_c = [sb(f"tab_c{i}", [P, SG, SH], "raw", 8192 + 4096 * i) for i in range(2)]
        lag_b = sb("lag_b", [P, BQ, SL, SH], "raw", 16384)
        tmp_b = [sb(f"tmp_b{i}", [P, SG, SH], "raw", 16384 + 4096 * i) for i in range(2)]
        tmp = sb("tmp", [P, BQ * (SL + 1) * SH], "extra")
        kern = sb("kern", [SH, BQ, P], "xh")
        d_in = sb("d_in", [P, SC, 2, SG // 2], "xh")
        tb = sb("tb", [P, 24, SG], "xl")
        state = sb("state", [P, SG, SC], "xl")
        u_in = sb("u_in", [P, SG, SC], "xc")
        pow_re = sb("pow_re", [P, SL + 1, SG], "sq")
        pow_im = sb("pow_im", [P, SL + 1, SG], "sq", 2304)
        pow_is = sb("pow_is", [P, SL + 1, SG], "sq", 4608)
        rev_re = sb("rev_re", [P, SL, SG], "sq", 6912)
        rev_is = sb("rev_is", [P, SL, SG], "sq", 8960)
        run = sb("run", [P, SC + 1, 2, SG // 2], "extra")
        carry = sb("carry", [P, 2, 2, SG // 2], "misc", 512)
        scan_q = sb("scan_q", [P, 2, 2, SG // 2], "misc", 1024)
        scan_r = sb("scan_r", [P, 2, SG // 2], "misc", 1536)
        sinks = sb("sinks", [P, 2 * AH], "misc", 2304)
        gate_bias = sb("gate_bias", [P, 2 * IN_IF], "misc", 2368)
        gelu = sb("gelu", [P, 2, T], "sg")
        w_if = [sb(f"w_if{l}", [P, KT, IN_IF], "misc", 2560 + 256 * l) for l in range(2)]
        ld_if = S("ld_if")
        ld_const, ld_vec, ld_x, ld_ssm = S("ld_const"), S("ld_vec"), S("ld_x"), S("ld_ssm")
        N_VEC, N_SSM = 13, 14
        vec_t, vec_done = S("vec_t"), S("vec_done")
        xt_ready, xt_done, u_ready, u_done5 = S("xt_ready"), S("xt_done"), S("u_ready"), S("s5_u_done")
        a_ready, b_ready, c_ready, a_read = S("a_ready"), S("b_ready"), S("c_ready"), S("a_read")
        dt_done, mag_done, sin_done, cos_done = S("dt_done"), S("mag_done"), S("sin_done"), S("cos_done")
        arg_mag, arg_sin, arg_cos = S("arg_mag"), S("arg_sin"), S("arg_cos")
        tabs_done, lagb_done, sout_done = S("tabs_done"), S("lagb_done"), S("sout_done")
        e_t, e_done, ds_ready, k_ready, k_done, k_moved = (S("e_t"), S("e_done"), S("ds_ready"), S("k_ready"),
                                                           S("k_done"), S("k_moved"))
        toep_zero, din_act, din_dve, st_act, st_dve = (S("toep_zero"), S("din_act"), S("din_dve"), S("st_act"),
                                                       S("st_dve"))
        scan_p, scan_s, scan_n = S("scan_p"), S("scan_s"), S("scan_n")
        y_ready, yt_ready, gelu_done = S("y_ready"), S("yt_ready"), S("gelu_done")
        y_act, y_dve = S("y_act"), S("y_dve")
        diag_done, grouped = S("diag_done"), S("grouped")

        def s5_loads(sp):
            sp.dma_start(const[:, :], w["consts"]).then_inc(ld_const, 16)
            sp.dma_start(x_chunk[:, :, :], w["x"][0].rearrange("(c t) d -> c t d", t=SL)).then_inc(ld_x, 16)
            for i, name in enumerate(("ssm_a_re", "ssm_a_re", "ssm_a_im", "ssm_a_im")):
                sp.dma_start(a_rows[:, SP * i:SP * i + SP], w[name][0]).then_inc(ld_ssm, 16)
            sp.dma_start(tb[:, 0, :], w["ssm_log_dt"][0].partition_broadcast(P)).then_inc(ld_ssm, 16)
            for i, pair in enumerate((("ssm_b_re", "ssm_b_im"), ("ssm_b_im", "ssm_b_re"))):
                for j, name in enumerate(pair):
                    sp.dma_start(b_rows[i][:, SP * SH * j:SP * SH * (j + 1)],
                                 w[name][0].rearrange("g p h -> g (p h)")).then_inc(ld_ssm, 16)
            for i, name in enumerate(("ssm_c_re", "ssm_c_im", "ssm_c_im", "ssm_c_re")):
                sp.dma_start(c_rows[:, :, SP * i:SP * i + SP],
                             w[name][0].rearrange("(t g) h p -> (g h) t p", g=8)).then_inc(ld_ssm, 16)
            sp.dma_start(d_diag[:, :, :].rearrange("h g k -> h (g k)"),
                         w["ssm_d"][0].partition_broadcast(SH)).then_inc(ld_ssm, 16)
            at = 0
            for name in ("ln_mix_g", "ln_mix_b", "ln_ffn_g", "ln_ffn_b", "norm_mix_2", "norm_ffn_2"):
                sp.dma_start(vec_rows[at:at + 16, :], w[name].rearrange("l (k p) -> (l k) p", p=P)).then_inc(ld_vec, 16)
                at += 16
            sp.dma_start(vec_rows[at:at + 8, :], w["m_head_norm_2"].rearrange("l (k p) -> (l k) p", p=P)).then_inc(ld_vec, 16)
            at += 8
            for name in ("att_q_norm_2", "att_k_norm_2"):
                for b in (0, HD):
                    sp.dma_start(vec_rows[at:at + 2, b:b + HD], w[name]).then_inc(ld_vec, 16)
                at += 2
            sp.dma_start(sinks[:, :], w["att_sinks_2"].rearrange("l h -> (l h)").partition_broadcast(P)).then_inc(ld_vec, 16)
            sp.dma_start(gate_bias[:, :], w["m_gate_bias_2"].rearrange("l h -> (l h)").partition_broadcast(P)).then_inc(ld_vec, 16)
            for l in range(2):
                sp.dma_start(w_if[l][:, :, :], w["w_in_2"][l].rearrange("(k p) n -> p k n", p=P)[
                    :, :, IN_QKVO:IN_QKVO + IN_IF]).then_inc(ld_if, 16)

        def s5_toeplitz(sp):
            sp.wait_ge(toep_zero, 1)
            for b in range(NB):
                sp.wait_ge(k_done, 4 * b + 4)
                for t in range(SL):
                    sp.dma_start(toep[SH * t:SH * t + SH, BQ * b:BQ * b + BQ, SH * t:P],
                                 kern[:, :, 0:P - SH * t]).then_inc(k_moved, 16)

        def s5_tensor(pe):
            pe.wait_ge(ld_const, 16)
            pe.wait_ge(ld_x, 16)
            for f in range(KT):
                for t in range(SL):
                    last = nc.tensor.transpose(PS[:, 4 + f // 2, (f % 2) * T + SC * t:(f % 2) * T + SC * t + SC],
                                               x_chunk[:, t, P * f:P * f + P], ident[0:SC, 0:SC])
                last.then_inc(xt_ready, 1)
            pe.wait_ge(grouped, 2)
            for g in range(SG):
                last = nc.tensor.transpose(PS[:, g // 16, (g % 16) * SC:(g % 16 + 1) * SC],
                                           x_group[:, g, :], ident[0:SC, 0:SC])
                if g % 16 == 15:
                    last.then_inc(u_ready, 1)
            pe.wait_ge(ld_vec, 16 * N_VEC)
            pe.wait_ge(xt_done, KT)
            nc.tensor.transpose(PS[:, 4, 0:108], vec_rows[:, :], ident[0:108, 0:108]).then_inc(vec_t, 1)
            pe.wait_ge(ld_ssm, 16 * N_SSM)
            for i in range(2):
                last = nc.tensor.transpose(PS[:, 5, SG * i:SG * i + SG], a_rows[:, P * i:P * i + P], ident[0:SG, 0:SG])
            last.then_inc(a_ready, 1)
            pe.wait_ge(u_done5, 4)
            for i in range(2):
                rows = b_rows[i][:, :].rearrange("g (q h) -> g q h", h=SH)
                for h in range(SH):
                    last = nc.tensor.transpose(PS[:, 2 * i + h // 8, (h % 8) * SG:(h % 8 + 1) * SG], rows[:, :, h],
                                               ident[0:SG, 0:SG])
            last.then_inc(b_ready, 1)
            pe.wait_ge(a_read, 2)
            pe.wait_ge(vec_done, 1)
            for i in range(2):
                for t in range(8):
                    last = nc.tensor.transpose(PS[:, 4 + 2 * i + t // 4, (t % 4) * P:(t % 4 + 1) * P],
                                               c_rows[:, t, P * i:P * i + P], ident)
            last.then_inc(c_ready, 1)
            pe.wait_ge(tabs_done, 2)
            for b in range(NB):
                for q in range(4):
                    n = 4 * b + q
                    if q == 0:
                        pe.wait_ge(lagb_done, b + 1)
                    if n >= 2:
                        pe.wait_ge(e_done, n - 1)
                    for i in range(4):
                        last = nc.tensor.transpose(PS[:, 2 + n % 2, P * i:P * i + P],
                                                   lag_b[:, 4 * q + i, :, :].rearrange("p t h -> p (t h)"), ident)
                    last.then_inc(e_t, 1)
                for q in range(4):
                    n = 4 * b + q
                    pe.wait_ge(e_done, n + 1)
                    for i in range(4):
                        g = BQ * b + 4 * q + i
                        last = nc.tensor.matmul(PS[:, 4 + b, (g % 16) * SC:(g % 16 + 1) * SC], s_in[:, 4 * q + i, :],
                                                u_in[:, g, :], start=True, stop=True, skip_group_check=True)
                    last.then_inc(ds_ready, 1)
                for q in range(4):
                    n = 4 * b + q
                    if q == 0:
                        pe.wait_ge(sout_done, b + 1)
                    if n >= 2:
                        pe.wait_ge(k_done, n - 1)
                    for i in range(4):
                        g = BQ * b + 4 * q + i
                        last = nc.tensor.matmul(PS[0:SH, n % 2, P * i:P * i + P], tab_b[0][:, g, :],
                                                s_out[:, g, 0:SL, :].rearrange("p t h -> p (t h)"), start=True, stop=True,
                                                skip_group_check=True)
                    last.then_inc(k_ready, 1)
            pe.wait_ge(k_moved, 16 * SL * NB)
            pe.wait_ge(k_done, 16)
            pe.wait_ge(e_done, 16)
            pe.wait_ge(st_act, 2)
            pe.wait_ge(st_dve, 2)
            for q in range(16):
                if q >= 4:
                    pe.wait_ge((y_act, y_dve)[q % 2], q // 2 - 1)
                for i in range(4):
                    g = 4 * q + i
                    y = PS[0:SC, q % 4, P * i:P * i + P]
                    nc.tensor.matmul(y, u_in[:, g, :], toep[:, g, :], start=True, stop=False, skip_group_check=True)
                    last = nc.tensor.matmul(y, state[:, g, :], s_out[:, g, 1:SL + 1, :].rearrange("p t h -> p (t h)"),
                                            start=False, stop=True, skip_group_check=True)
                last.then_inc(y_ready, 1)
            for f in range(KT):
                pe.wait_ge(y_act, f + 1)
                pe.wait_ge(y_dve, f + 1)
                for t in range(SL):
                    last = nc.tensor.transpose(PS[:, 4 + f // 2, (f % 2) * T + SC * t:(f % 2) * T + SC * t + SC],
                                               y_chunk[:, t, P * f:P * f + P], ident[0:SC, 0:SC])
                last.then_inc(yt_ready, 1)

        def by_token(f):
            return PS[:, 4 + f // 2, (f % 2) * T:(f % 2 + 1) * T].rearrange("p (t c) -> p c t", t=SL)

        def s5_scalar(act):
            act.wait_ge(ld_ssm, 16 * N_SSM)
            nc.scalar.activation(tb[:, 1, :], tb[:, 0, :], ACT.Exp).then_inc(dt_done, 1)
            for f in range(KT):
                act.wait_ge(xt_ready, f // 2 * 2 + 2)
                nc.scalar.activation(res[:, f, :].rearrange("p (c t) -> p c t", t=SL), by_token(f), ACT.Copy).then_inc(xt_done, 1)
            for i in range(4):
                act.wait_ge(u_ready, i + 1)
                nc.scalar.activation(u_in[:, 16 * i:16 * i + 16, :].rearrange("p g c -> p (g c)"), PS[:, i, :],
                                     ACT.Copy).then_inc(u_done5, 1)
            act.wait_ge(vec_t, 1)
            nc.scalar.activation(vec[:, :], PS[:, 4, 0:108], ACT.Copy).then_inc(vec_done, 1)
            act.wait_ge(arg_mag, 1)
            nc.scalar.activation(tb[:, 8, :], tb[:, 4, :], ACT.Exp).then_inc(mag_done, 1)
            act.wait_ge(arg_sin, 1)
            nc.scalar.activation(tb[:, 9, :], tb[:, 7, :], ACT.Sin).then_inc(sin_done, 1)
            act.wait_ge(arg_cos, 1)
            nc.scalar.activation(tb[:, 10, :], tb[:, 11, :], ACT.Sin).then_inc(cos_done, 1)
            sgn = const[:, CONST["sgn"][0]:CONST["sgn"][0] + 2]
            act.wait_ge(c_ready, 1)
            nc.scalar.activation(tab_c[0][:, :, :].rearrange("p g h -> p (g h)").rearrange("p (a b) -> p a b", a=2),
                                 PS[:, 4:6, :], ACT.Identity, scale=sgn[:, 1:2]).then_inc(tabs_done, 1)
            nc.scalar.activation(tab_c[1][:, :, :].rearrange("p g h -> p (g h)").rearrange("p (a b) -> p a b", a=2),
                                 PS[:, 6:8, :], ACT.Copy, scale=-1.0).then_inc(tabs_done, 1)
            for b in range(NB):
                for q in range(4):
                    n = 4 * b + q
                    act.wait_ge(e_t, n + 1)
                    if b >= 1:
                        act.wait_ge(ds_ready, 4 * b - 3 + q)
                    nc.scalar.activation(s_in[:, 4 * q:4 * q + 4, :].rearrange("p g c -> p (g c)"), PS[:, 2 + n % 2, :],
                                         ACT.Copy).then_inc(e_done, 1)
            act.wait_ge(ds_ready, 16)
            act.wait_ge(k_moved, 16 * SL * NB)
            ds = PS[:, 4:8, :].rearrange("p b (g two c) -> p b g two c", two=2, c=SC)
            dv = d_in[:, :, :, :].rearrange("p c r (b g) -> p r b g c", b=4)
            for b in range(2):
                for two in range(2):
                    for ri in range(2):
                        ins = nc.scalar.activation(dv[SP * two:SP * two + SP, ri, b], ds[SP * ri:SP * ri + SP, b, :, two, :],
                                                   ACT.Copy)
            ins.then_inc(din_act, 1)
            act.wait_ge(scan_n, SC - 1)
            st = state[:, :, :].rearrange("p (g two) c -> p two g c", two=2)
            rn = run[:, 0:SC, :, :].rearrange("p c r g -> p r g c")
            nc.scalar.activation(st[0:SP, 0], rn[0:SP, 0], ACT.Copy).then_inc(st_act, 1)
            nc.scalar.activation(st[SP:P, 1], rn[SP:P, 1], ACT.Copy).then_inc(st_act, 1)
            for q in range(0, 16, 2):
                act.wait_ge(y_ready, q + 1)
                nc.scalar.activation(*y_places(q), ACT.Copy).then_inc(y_act, 1)
            act.wait_ge(y_ready, 16)
            split_hi(act, 0, 0, 0)
            for f in range(KT):
                act.wait_ge(yt_ready, f // 2 * 2 + 2)
                if f >= 2:
                    act.wait_ge(xl_done, f - 1)
                nc.scalar.activation(gelu[:, f % 2, :].rearrange("p (c t) -> p c t", t=SL), by_token(f),
                                     ACT.Gelu_apprx_tanh).then_inc(gelu_done, 1)
                act.wait_ge(gelu_done, f + 1)
                nc.scalar.activation(x_hi[:, f, :], gelu[:, f % 2, :], ACT.Copy).then_inc(xh_done, 1)
            for j in range(1, RING):
                split_hi(act, 0, j, 0)

        def y_places(q):
            src = PS[0:SC, q % 4, :].rearrange("c (g t h) -> c g t h", g=4, h=SH)
            dst = y_chunk[:, :, 4 * q * SH:4 * (q + 1) * SH].rearrange("c t (g h) -> c g t h", h=SH)
            return dst, src

        def s5_pool(pool):
            pool.wait_ge(u_ready, 4)
            nc.gpsimd.memset(toep[:, :, :], 0.0).then_inc(toep_zero, 1)

        def s5_vector(dve):
            V = nc.vector
            lr, li, dt, xm, th, kk, r = (tb[:, i, :] for i in (2, 3, 1, 4, 5, 6, 7))
            mag, sn, cs, ca, ar = (tb[:, i, :] for i in (8, 9, 10, 11, 12))


            dve.wait_ge(ld_x, 16)
            for i in range(2):
                V.tensor_copy(x_group[:, 32 * i:32 * i + 32, :].rearrange("c g (t h) -> c t g h", h=SH),
                              x_chunk[:, :, 512 * i:512 * i + 512].rearrange("c t (g h) -> c t g h", h=SH)).then_inc(grouped, 1)
            dve.wait_ge(a_ready, 1)
            V.tensor_scalar(lr, PS[:, 5, 0:SG], -1e-4, None, ALU.min).then_inc(a_read, 1)
            V.tensor_copy(li, PS[:, 5, SG:2 * SG]).then_inc(a_read, 1)
            dve.wait_ge(a_read, 2)
            dve.wait_ge(dt_done, 1)
            V.tensor_tensor(xm, lr, dt, ALU.mult).then_inc(arg_mag, 1)
            V.tensor_tensor(th, li, dt, ALU.mult).then_inc(dve_step, 1)
            dve.wait_ge(dve_step, v_count.one())
            magic = 1.5 * 2.0 ** 23
            two_pi_hi = float(np.float32(6.28125))
            two_pi_lo = float(2 * np.pi - 6.28125)
            V.tensor_scalar(kk, th, float(1 / (2 * np.pi)), magic, ALU.mult, ALU.add).then_inc(dve_step, 1)
            dve.wait_ge(dve_step, v_count.one())
            V.tensor_scalar(kk, kk, -magic, None, ALU.add).then_inc(dve_step, 1)
            dve.wait_ge(dve_step, v_count.one())
            V.scalar_tensor_tensor(out=r, in0=kk, scalar=-two_pi_hi, in1=th, op0=ALU.mult, op1=ALU.add).then_inc(dve_step, 1)
            dve.wait_ge(dve_step, v_count.one())
            V.scalar_tensor_tensor(out=r, in0=kk, scalar=-two_pi_lo, in1=r, op0=ALU.mult, op1=ALU.add).then_inc(dve_step, 1)
            dve.wait_ge(dve_step, v_count.one())
            pi = float(np.nextafter(np.float32(np.pi), np.float32(0)))
            V.tensor_scalar(r, r, pi, -pi, ALU.min, ALU.max).then_inc(arg_sin, 1)
            dve.wait_ge(arg_sin, 1)
            V.scalar_tensor_tensor(out=ar, in0=r, scalar=-1.0, in1=r, op0=ALU.mult, op1=ALU.max).then_inc(dve_step, 1)
            dve.wait_ge(dve_step, v_count.one())
            V.tensor_scalar(ca, ar, -1.0, float(np.pi / 2), ALU.mult, ALU.add).then_inc(arg_cos, 1)
            dve.wait_ge(mag_done, 1)
            dve.wait_ge(sin_done, 1)
            dve.wait_ge(cos_done, 1)
            V.memset(pow_re[:, 0, :], 1.0)
            V.memset(pow_im[:, 0, :], 0.0)
            V.tensor_tensor(pow_re[:, 1, :], mag, cs, ALU.mult).then_inc(dve_step, 1)
            dve.wait_ge(dve_step, v_count.one())
            V.tensor_tensor(pow_im[:, 1, :], mag, sn, ALU.mult).then_inc(dve_step, 1)
            dve.wait_ge(dve_step, v_count.one())
            nr, den, t0, t1, cr, ci = (tb[:, i, :] for i in (13, 14, 15, 16, 17, 18))
            cis = tb[:, 19, :]
            lb_im = pow_im[:, 1, :]
            V.tensor_scalar(nr, pow_re[:, 1, :], -1.0, None, ALU.add).then_inc(dve_step, 1)
            dve.wait_ge(dve_step, v_count.one())
            V.tensor_tensor(den, lr, lr, ALU.mult).then_inc(dve_step, 1)
            dve.wait_ge(dve_step, v_count.one())
            V.tensor_tensor(t0, li, li, ALU.mult).then_inc(dve_step, 1)
            dve.wait_ge(dve_step, v_count.one())
            V.tensor_tensor(den, den, t0, ALU.add).then_inc(dve_step, 1)
            dve.wait_ge(dve_step, v_count.one())
            V.reciprocal(den, den).then_inc(dve_step, 1)
            dve.wait_ge(dve_step, v_count.one())
            V.tensor_tensor(t0, nr, lr, ALU.mult).then_inc(dve_step, 1)
            dve.wait_ge(dve_step, v_count.one())
            V.tensor_tensor(t1, lb_im, li, ALU.mult).then_inc(dve_step, 1)
            dve.wait_ge(dve_step, v_count.one())
            V.tensor_tensor(t0, t0, t1, ALU.add).then_inc(dve_step, 1)
            dve.wait_ge(dve_step, v_count.one())
            V.tensor_tensor(cr, t0, den, ALU.mult).then_inc(dve_step, 1)
            dve.wait_ge(dve_step, v_count.one())
            V.tensor_tensor(t0, lb_im, lr, ALU.mult).then_inc(dve_step, 1)
            dve.wait_ge(dve_step, v_count.one())
            V.tensor_tensor(t1, nr, li, ALU.mult).then_inc(dve_step, 1)
            dve.wait_ge(dve_step, v_count.one())
            V.tensor_tensor(t0, t0, t1, ALU.subtract).then_inc(dve_step, 1)
            dve.wait_ge(dve_step, v_count.one())
            V.tensor_tensor(ci, t0, den, ALU.mult).then_inc(dve_step, 1)
            dve.wait_ge(dve_step, v_count.one())
            sgn = CONST["sgn"][0]
            minus_re = const[:, sgn:sgn + 1]
            V.tensor_scalar(cis, ci, minus_re, None, ALU.mult).then_inc(dve_step, 1)
            dve.wait_ge(dve_step, v_count.one())
            for lo, n in ((1, 1), (1, 2), (1, 4)):
                top = lo + n - 1
                src = slice(1, n + 1)
                dst = slice(top + 1, top + n + 1)
                br = pow_re[:, top:top + 1, :].to_broadcast([P, n, SG])
                bi = pow_im[:, top:top + 1, :].to_broadcast([P, n, SG])
                ta, tb2 = tmp[:, 0:n * SG].rearrange("p (n g) -> p n g", n=n), tmp[:, 512:512 + n * SG].rearrange(
                    "p (n g) -> p n g", n=n)
                V.tensor_tensor(ta, pow_re[:, src, :], br, ALU.mult).then_inc(dve_step, 1)
                dve.wait_ge(dve_step, v_count.one())
                V.tensor_tensor(tb2, pow_im[:, src, :], bi, ALU.mult).then_inc(dve_step, 1)
                dve.wait_ge(dve_step, v_count.one())
                V.tensor_tensor(pow_re[:, dst, :], ta, tb2, ALU.subtract).then_inc(dve_step, 1)
                dve.wait_ge(dve_step, v_count.one())
                V.tensor_tensor(ta, pow_re[:, src, :], bi, ALU.mult).then_inc(dve_step, 1)
                dve.wait_ge(dve_step, v_count.one())
                V.tensor_tensor(tb2, pow_im[:, src, :], br, ALU.mult).then_inc(dve_step, 1)
                dve.wait_ge(dve_step, v_count.one())
                V.tensor_tensor(pow_im[:, dst, :], ta, tb2, ALU.add).then_inc(dve_step, 1)
                dve.wait_ge(dve_step, v_count.one())
            V.tensor_scalar(pow_is[:, :, :], pow_im[:, :, :], minus_re, None, ALU.mult).then_inc(dve_step, 1)
            dve.wait_ge(dve_step, v_count.one())
            for j in range(SL):
                V.tensor_copy(rev_re[:, j, :], pow_re[:, SL - 1 - j, :])
                V.tensor_copy(rev_is[:, j, :], pow_is[:, SL - 1 - j, :]).then_inc(dve_step, 1)
                dve.wait_ge(dve_step, v_count.one())
            for half in range(2):
                ps = slice(SP * half, SP * half + SP)
                lre = pow_re[ps, SL, :].rearrange("p (g two) -> p two g", two=2)[:, half, :]
                lim = pow_im[ps, SL, :].rearrange("p (g two) -> p two g", two=2)[:, half, :]
                V.tensor_copy(carry[ps, 0, 0, :], lre)
                V.tensor_copy(carry[ps, 1, 1, :], lre)
                V.tensor_copy(carry[ps, 1, 0, :], lim)
                V.tensor_scalar(carry[ps, 0, 1, :], lim, -1.0, None, ALU.mult).then_inc(dve_step, 1)
                dve.wait_ge(dve_step, v_count.one())
            dve.wait_ge(b_ready, 1)
            pb = [PS[:, 2 * i:2 * i + 2, :].rearrange("p a (h g) -> p (a h) g", g=SG).rearrange("p h g -> p g h")
                  for i in range(2)]
            crb = cr.unsqueeze(2).to_broadcast([P, SG, SH])
            cib = cis.unsqueeze(2).to_broadcast([P, SG, SH])
            V.tensor_tensor(tmp_b[0][:, :, :], pb[0], crb, ALU.mult).then_inc(dve_step, 1)
            dve.wait_ge(dve_step, v_count.one())
            V.tensor_tensor(tmp_b[1][:, :, :], pb[1], cib, ALU.mult).then_inc(dve_step, 1)
            dve.wait_ge(dve_step, v_count.one())
            V.tensor_tensor(tab_b[0][:, :, :], tmp_b[0][:, :, :], tmp_b[1][:, :, :], ALU.add).then_inc(dve_step, 1)
            dve.wait_ge(dve_step, v_count.one())
            V.tensor_tensor(tmp_b[0][:, :, :], pb[1], crb, ALU.mult).then_inc(dve_step, 1)
            dve.wait_ge(dve_step, v_count.one())
            V.tensor_tensor(tmp_b[1][:, :, :], pb[0], cib, ALU.mult).then_inc(dve_step, 1)
            dve.wait_ge(dve_step, v_count.one())
            V.tensor_tensor(tab_b[1][:, :, :], tmp_b[0][:, :, :], tmp_b[1][:, :, :], ALU.subtract).then_inc(dve_step, 1)
            dve.wait_ge(dve_step, v_count.one())
            V.tensor_tensor(d_diag[:, :, :], d_diag[:, :, :], ident[0:SH, 0:SH].unsqueeze(1).to_broadcast([SH, SG, SH]),
                            ALU.mult).then_inc(diag_done, 1)
            dve.wait_ge(diag_done, 1)
            dve.wait_ge(tabs_done, 2)

            def kernels_drain(b):
                for q in range(4):
                    n = 4 * b + q
                    dve.wait_ge(k_ready, n + 1)
                    if q == 0 and b >= 1:
                        dve.wait_ge(k_moved, 16 * SL * b)
                    kv = kern[:, 4 * q:4 * q + 4, :]
                    V.tensor_copy(kv.rearrange("h g c -> h (g c)"), PS[0:SH, n % 2, :]).then_inc(dve_step, 1)
                    dve.wait_ge(dve_step, v_count.one())
                    V.tensor_tensor(kv[:, :, 0:SH], kv[:, :, 0:SH], d_diag[:, 4 * n:4 * n + 4, :],
                                    ALU.add).then_inc(k_done, 1)

            for b in range(NB):
                gs = slice(BQ * b, BQ * b + BQ)
                sh = [P, BQ, SL, SH]
                if b >= 1:
                    dve.wait_ge(e_t, 4 * b)
                lag_re = rev_re[:, :, gs].rearrange("p t g -> p g t").unsqueeze(3).to_broadcast(sh)
                lag_im = rev_is[:, :, gs].rearrange("p t g -> p g t").unsqueeze(3).to_broadcast(sh)
                tv = tmp[:, 0:BQ * SL * SH].rearrange("p (g t h) -> p g t h", g=BQ, h=SH)
                V.tensor_tensor(lag_b[:, :, :, :], tab_b[0][:, gs, :].unsqueeze(2).to_broadcast(sh), lag_re, ALU.mult).then_inc(dve_step, 1)
                dve.wait_ge(dve_step, v_count.one())
                V.tensor_tensor(tv, tab_b[1][:, gs, :].unsqueeze(2).to_broadcast(sh), lag_im, ALU.mult).then_inc(dve_step, 1)
                dve.wait_ge(dve_step, v_count.one())
                V.tensor_tensor(lag_b[:, :, :, :], lag_b[:, :, :, :], tv, ALU.add).then_inc(lagb_done, 1)
                dve.wait_ge(lagb_done, b + 1)
                sh = [P, BQ, SL + 1, SH]
                o_re = pow_re[:, :, gs].rearrange("p t g -> p g t").unsqueeze(3).to_broadcast(sh)
                o_im = pow_im[:, :, gs].rearrange("p t g -> p g t").unsqueeze(3).to_broadcast(sh)
                tv = tmp[:, :].rearrange("p (g t h) -> p g t h", g=BQ, h=SH)
                so = s_out[:, gs, :, :]
                V.tensor_tensor(so, tab_c[0][:, gs, :].unsqueeze(2).to_broadcast(sh), o_re, ALU.mult).then_inc(dve_step, 1)
                dve.wait_ge(dve_step, v_count.one())
                V.tensor_tensor(tv, tab_c[1][:, gs, :].unsqueeze(2).to_broadcast(sh), o_im, ALU.mult).then_inc(dve_step, 1)
                dve.wait_ge(dve_step, v_count.one())
                V.tensor_tensor(so, so, tv, ALU.add).then_inc(sout_done, 1)
                dve.wait_ge(sout_done, b + 1)
                if b >= 1:
                    kernels_drain(b - 1)
            kernels_drain(NB - 1)
            dve.wait_ge(ds_ready, 16)
            dve.wait_ge(k_moved, 16 * SL * NB)
            ds = PS[:, 4:8, :].rearrange("p b (g two c) -> p b g two c", two=2, c=SC)
            dv = d_in[:, :, :, :].rearrange("p c r (b g) -> p r b g c", b=4)
            for b in range(2, 4):
                for two in range(2):
                    for ri in range(2):
                        ins = V.tensor_copy(dv[SP * two:SP * two + SP, ri, b], ds[SP * ri:SP * ri + SP, b, :, two, :])
            ins.then_inc(din_dve, 1)
            V.memset(run[:, 0, :, :], 0.0).then_inc(din_dve, 1)
            dve.wait_ge(din_dve, 2)
            dve.wait_ge(din_act, 1)
            with dve.Fori(0, SC - 1) as c:
                now = run[:, bass.ds(c, 1), :, :].to_broadcast([P, 2, 2, SG // 2])
                V.tensor_tensor(scan_q[:, :, :, :], now, carry[:, :, :, :], ALU.mult).then_inc(scan_p, 1)
                dve.wait_ge(scan_p, c + 1)
                V.tensor_tensor(scan_r[:, :, :], scan_q[:, :, 0, :], scan_q[:, :, 1, :], ALU.add).then_inc(scan_s, 1)
                dve.wait_ge(scan_s, c + 1)
                V.tensor_tensor(run[:, bass.ds(c + 1, 1), :, :].rearrange("p a r g -> p (a r) g"), scan_r[:, :, :],
                                d_in[:, bass.ds(c, 1), :, :].rearrange("p a r g -> p (a r) g"),
                                ALU.add).then_inc(scan_n, 1)
                dve.wait_ge(scan_n, c + 1)
            st = state[:, :, :].rearrange("p (g two) c -> p two g c", two=2)
            rn = run[:, 0:SC, :, :].rearrange("p c r g -> p r g c")
            V.tensor_copy(st[SP:P, 0], rn[0:SP, 1]).then_inc(st_dve, 1)
            V.tensor_copy(st[0:SP, 1], rn[SP:P, 0]).then_inc(st_dve, 1)
            for q in range(1, 16, 2):
                dve.wait_ge(y_ready, q + 1)
                V.tensor_copy(*y_places(q)).then_inc(y_dve, 1)
            split_lo(dve, 0, 0, 0, 0, lo_dve)
            for f in range(KT):
                dve.wait_ge(xh_done, f + 1)
                V.tensor_tensor(x_lo[:, f, :], gelu[:, f % 2, :], x_hi[:, f, :].bitcast(F32), ALU.subtract).then_inc(xl_done, 1)
            for j in range(1, RING):
                split_lo(dve, 0, j, j, 0, lo_dve)

        ztile = sb("ztile", [P, 14, T], "hl", 16 * 4 * T)
        sig_g = sb("sig_g", [P, 16, T], "hh", 16 * 4 * T)
        sig_o = sb("sig_o", [P, MH, T], "extra", 4096)
        vm_tok = sb("vm_tok", [P, 2, 512], "extra", 0)
        hm_raw = sb("hm_raw", [P, 2, T], "extra", 8192)
        qk_rot = sb("qk_rot", [P, 5, T], "xc")
        k_dup = sb("k_dup", [P, 2, T], "xc", 5120)
        va_tok = sb("va_tok", [P, 2, P], "xc", 7168)
        qk_buf = sb("qk_buf", [P, 5, T], "sg")
        a_prob = [sb(f"a_prob{i}", [P, 2, 384], "sg", 3072 * i) for i in range(2)]
        a_probT = sb("a_probT", [P, 2, 384], "sq")
        m_exp = [sb(f"m_exp{i}", [P, 384], "sg", 1536 * i) for i in range(2)]
        m_w = [sb(f"m_w{i}", [P, 384], "sg", 3072 + 1536 * i) for i in range(2)]
        m_lim = [sb(f"m_lim{i}", [P, T], "zt", 1024 * i) for i in range(2)]
        m_den, m_sq, m_rs, m_out = (sb(n, [P, T], "sq", 1024 * i) for i, n in enumerate(("m_den", "m_sq", "m_rs", "m_out")))
        row_a = [sb(f"row_a{i}", [MH, P + T], "xh", 1536 * i) for i in range(2)]
        row_e = sb("row_e", [MH, T], "xh", 3072)
        gate_if = sb("gate_if", [P, 2, IN_IF], "xh", 4096)
        nlf = sb("nlf", [P, 2, MH], "xh", 4160)
        nlf_t = sb("nlf_t", [P, 2, MH], "xh", 4192)
        a_col = sb("a_col", [P, 2, MH], "xh", 4224)
        mx, neg_m, sink_e, p_sum, p_inv = (sb(n, [P, 4, 2, 2], "xh", 4288 + 64 * i) for i, n in enumerate(
            ("mx", "neg_m", "sink_e", "p_sum", "p_inv")))
        q_gain = sb("q_gain", [P, 2], "misc", 2432)
        gain_done = S("gain_done")
        if_ready, vtm_ready, va_done = S("if_ready"), S("vtm_ready"), S("va_done")
        qsq_done, qss_ready, qrs_done, qn_done, rot_ready, qr_done = (S("qsq_done"), S("qss_ready"), S("qrs_done"),
                                                                      S("qn_done"), S("rot_ready"), S("qr_done"))
        gi_done, nlf_done, rows_ready, rows_done, acol_done = (S("gi_done"), S("nlf_done"), S("rows_ready"),
                                                               S("rows_done"), S("acol_done"))
        s_ready, mx_done, p_done, pn_done, pt_ready, pt_done, ao_ready, ao_hi = (
            S("s_ready"), S("mx_done"), S("p_done"), S("pn_done"), S("pt_ready"), S("pt_done"), S("ao_ready"), S("ao_hi"))
        d_ready, x_done, w_ready, nd_ready, hm_done, hsq_done, hss_ready, hrs_done, hm_hi = (
            S("d_ready"), S("x_done"), S("w_ready"), S("nd_ready"), S("hm_done"), S("hsq_done"), S("hss_ready"),
            S("hrs_done"), S("hm_hi"))
        AP_ = AH // 2

        def proj(g, idx):
            if g.name == "q":
                t = qkv[:, bass.ds(idx * 2, 2), :]
            elif g.name == "k":
                t = qkv[:, bass.ds(idx * 2 + 8, 2), :]
            elif g.name == "v":
                t = v_feat[:, bass.ds(idx * 2, 2), :]
            else:
                t = ztile[:, bass.ds(idx * 2, 2), :]
            return t.rearrange("p a t -> p (a t)")

        def hyb_tensor(pe, l):
            g = G[f"gates{l}"]
            hid0 = g.hid0
            MMr = dict(skip_group_check=True)
            pe.wait_ge(act_done, g.act0 + g.n)
            if l == 0:
                pe.wait_ge(ld_if, 32)
            for t in range(2):
                for kt in range(KT):
                    last = nc.tensor.matmul(PS[:, 7, IN_IF * t:IN_IF * (t + 1)], xn[:, kt, P * t:P * t + P],
                                            w_if[l][:, kt, :], start=kt == 0, stop=kt == KT - 1, **MMr)
            last.then_inc(if_ready, 1)
            for t in range(2):
                nc.tensor.transpose(PS[:, 1, P * t:P * t + P], ztile[:, 5, P * t:P * t + P], ident)
                for h in range(MH):
                    last = nc.tensor.transpose(PS[:, 2 + t, P * h:P * h + P], ztile[:, 10 + h, P * t:P * t + P], ident)
            last.then_inc(vtm_ready, 1)
            pe.wait_ge(qsq_done, l + 1)
            flat = qk_buf[:, :, :].rearrange("p a t -> p (a t)")
            zflat = ztile[:, 0:5, :].rearrange("p a t -> p (a t)")
            for b, n in ((0, 512), (1, 512), (2, T)):
                last = nc.tensor.matmul(PS[:, 4 + b, 0:n], C("mean_h"), flat[:, 512 * b:512 * b + n], start=True, stop=True)
            last.then_inc(qss_ready, 1)
            pe.wait_ge(qn_done, 2 * l + 2)
            for b, n in ((0, 512), (1, 512), (2, T)):
                last = nc.tensor.matmul(PS[:, 4 + b, 0:n], C("rot"), zflat[:, 512 * b:512 * b + n], start=True, stop=True)
            last.then_inc(rot_ready, 1)
            pe.wait_ge(nlf_done, l + 1)
            tri = const[:, CONST["tri"][0]:CONST["tri"][0] + T]
            nf, ar = PS[0:MH, 0, 0:T], PS[0:MH, 0, T:2 * T]
            for row, with_i in ((nf, False), (ar, True)):
                nc.tensor.matmul(row, nlf[:, 0, :], tri, start=True, stop=False, **MMr)
                last = nc.tensor.matmul(row[:, P:T], nlf[:, 1, :], C("tri"), start=False, stop=not with_i, **MMr)
                if with_i:
                    for t in range(2):
                        last = nc.tensor.matmul(row[:, P * t:P * t + P], gate_if[:, t, 0:MH], ident, start=False,
                                                stop=True, **MMr)
            ac = PS[:, 7, 2 * IN_IF:2 * IN_IF + 2 * MH]
            nc.tensor.matmul(ac[:, 0:MH], C("tri"), nlf[:, 0, :], start=True, stop=False, **MMr)
            nc.tensor.matmul(ac[:, 0:MH], ident, gate_if[:, 0, 0:MH], start=False, stop=True, **MMr)
            nc.tensor.matmul(ac[:, MH:2 * MH], C("ones"), nlf[:, 0, :], start=False, stop=False, **MMr)
            nc.tensor.matmul(ac[:, MH:2 * MH], C("tri"), nlf[:, 1, :], start=False, stop=False, **MMr)
            last = nc.tensor.matmul(ac[:, MH:2 * MH], ident, gate_if[:, 1, 0:MH], start=False, stop=True, **MMr)
            last.then_inc(rows_ready, 1)

            def scores(p):
                for hd in range(2):
                    h = 2 * p + hd
                    b = HD * hd
                    s = PS[:, 4 + 2 * (p % 2) + hd, :]
                    q, k = qk_rot[b:b + HD, p, :], k_dup[b:b + HD, h // (AH // AKV), :]
                    nc.tensor.matmul(s[:, 0:P], q[:, 0:P], k[:, 0:P], start=True, stop=False, **MMr)
                    nc.tensor.matmul(s[:, P:384], q[:, P:T], k, start=False, stop=False, **MMr)
                    nc.tensor.matmul(s[:, 0:P], ident, C("win_diag"), start=False, stop=True, **MMr)
                    a = CONST["win_prev"][0]
                    last = nc.tensor.matmul(s[:, P:384], ident, const[:, a:a + T], start=False, stop=True, **MMr)
                last.then_inc(s_ready, 1)

            def transposed(p):
                pe.wait_ge(pn_done, AP_ * l + p + 1)
                if p >= 1:
                    pe.wait_ge(pt_done, AP_ * l + p)
                for hd in range(2):
                    for c in range(3):
                        last = nc.tensor.transpose(PS[:, 2 + hd, P * c:P * c + P], a_prob[p % 2][:, hd, P * c:P * c + P], ident)
                last.then_inc(pt_ready, 1)

            def outputs(p):
                pe.wait_ge(pt_done, AP_ * l + p + 1)
                if p >= 2:
                    pe.wait_ge(hid_done, hid0 + p - 1)
                for hd in range(2):
                    kv = (2 * p + hd) // (AH // AKV)
                    o = PS[HD * hd:HD * hd + HD, 1 - p % 2, 0:T]
                    v = [va_tok[:, t, HD * kv:HD * kv + HD] for t in range(2)]
                    pt = a_probT[:, hd, :]
                    nc.tensor.matmul(o[:, 0:P], v[0], pt[:, 0:P], start=True, stop=True, **MMr)
                    nc.tensor.matmul(o[:, P:T], v[0], pt[:, P:T], start=False, stop=False, **MMr)
                    last = nc.tensor.matmul(o[:, P:T], v[1], pt[:, T:384], start=False, stop=True, **MMr)
                last.then_inc(ao_ready, 1)

            pe.wait_ge(qr_done, l + 1)
            pe.wait_ge(acol_done, l + 1)
            pe.wait_ge(va_done, 3 * l + 3)
            for it in range(AP_ + 2):
                if it < AP_:
                    if it >= 2:
                        pe.wait_ge(p_done, AP_ * l + it - 1)
                    scores(it)
                if 1 <= it <= AP_:
                    transposed(it - 1)
                if it >= 2:
                    outputs(it - 2)

            pe.wait_ge(rows_done, l + 1)

            def decays(h):
                if h >= 2:
                    pe.wait_ge(w_ready, MH * l + h - 1)
                d, s = PS[:, 4 + h % 2, :], PS[:, 6 + h % 2, :]
                m = row_a[0][:, P:P + T]
                a = CONST["sel_neg"][0] + P * h
                neg = const[0:MH, a:a + P]
                nc.tensor.matmul(d[:, 0:T], neg, m, start=True, stop=False, **MMr)
                nc.tensor.matmul(d[:, T:384], neg, m[:, P:T], start=False, stop=False, **MMr)
                nc.tensor.matmul(d[:, 0:P], ident, C("m_mask"), start=False, stop=True, **MMr)
                nc.tensor.matmul(d[:, T:384], ident, C("m_mask"), start=False, stop=True, **MMr)
                b = HD * (h % 2)
                q, k = ztile[b:b + HD, 6 + h // 2, :], ztile[b:b + HD, 8 + h // 2, :]
                nc.tensor.matmul(s[:, 0:T], k[:, 0:P], q, start=True, stop=True, **MMr)
                nc.tensor.matmul(s[:, T:384], k[:, P:T], q[:, P:T], start=False, stop=True, **MMr)
                a = CONST["sel_pos"][0] + P * h
                if h >= 1:
                    pe.wait_ge(x_done, 3 * (MH * l + h))
                nc.tensor.matmul(PS[:, 3, 0:T], const[0:MH, a:a + P], row_e[:, :], start=True, stop=True,
                                 **MMr).then_inc(d_ready, 1)

            def sums(h):
                pe.wait_ge(w_ready, MH * l + h + 1)
                if h >= 1:
                    pe.wait_ge(hm_done, MH * l + h)
                nd, wt = PS[:, 2, :], m_w[h % 2]
                v = [vm_tok[:, t, P * h:P * h + P] for t in range(2)]
                nc.tensor.matmul(nd[:, 0:T], v[0], wt[:, 0:T], start=True, stop=False, **MMr)
                nc.tensor.matmul(nd[:, P:T], v[1], wt[:, T:384], start=False, stop=True, **MMr)
                nc.tensor.matmul(nd[:, T:2 * T], C("ones"), wt[:, 0:T], start=False, stop=False, **MMr)
                nc.tensor.matmul(nd[:, T + P:2 * T], C("ones"), wt[:, T:384], start=False, stop=True,
                                 **MMr).then_inc(nd_ready, 1)

            def head_mean(h):
                pe.wait_ge(hsq_done, MH * l + h + 1)
                nc.tensor.matmul(PS[:, 1, 0:T], C("mean_v"), m_sq[:, :], start=True, stop=True,
                                 **MMr).then_inc(hss_ready, 1)

            decays(0)
            for h in range(MH):
                if h + 1 < MH:
                    decays(h + 1)
                sums(h)
                head_mean(h)

        def hyb_scalar(act, l):
            g = G[f"gates{l}"]
            act.wait_ge(act_done, g.act0 + g.n)
            if l == 0:
                act.wait_ge(vec_done, 1)
                for i in range(2):
                    nc.scalar.activation(q_gain[:, i:i + 1], column("q_norm", i, 0), ACT.Copy,
                                         scale=HD ** -0.5).then_inc(gain_done, 1)
            nc.scalar.activation(qk_buf[:, :, :], ztile[:, 0:5, :], ACT.Square).then_inc(qsq_done, 1)
            act.wait_ge(gi_done, l + 1)
            nc.scalar.activation(nlf_t[:, :, :], gate_if[:, :, MH:2 * MH], ACT.Abs).then_inc(act_step, 1)
            a_count.one()
            act.wait_ge(act_step, a_count.n)
            nc.scalar.activation(nlf_t[:, :, :], nlf_t[:, :, :], ACT.Exp, scale=-1.0).then_inc(act_step, 1)
            a_count.one()
            act.wait_ge(act_step, a_count.n)
            nc.scalar.activation(nlf_t[:, :, :], nlf_t[:, :, :], ACT.Ln, bias=1.0).then_inc(soft_f, 1)
            act.wait_ge(vtm_ready, l + 1)
            nc.scalar.activation(va_tok[:, :, :].rearrange("p t d -> p (t d)"), PS[:, 1, 0:T], ACT.Copy).then_inc(va_done, 1)
            for t in range(2):
                nc.scalar.activation(vm_tok[:, t, :], PS[:, 2 + t, :], ACT.Copy).then_inc(va_done, 1)
            eps = const[:, CONST["sgn"][0] + 3:CONST["sgn"][0] + 4]
            act.wait_ge(qss_ready, l + 1)
            flat = qk_buf[:, :, :].rearrange("p a t -> p (a t)")
            nc.scalar.activation(flat[:, 0:1024].rearrange("p (a b) -> p a b", a=2), PS[:, 4:6, :], ACT.Ln, bias=eps).then_inc(act_step, 1)
            a_count.one()
            nc.scalar.activation(flat[:, 1024:1280], PS[:, 6, 0:T], ACT.Ln, bias=eps).then_inc(act_step, 1)
            a_count.one()
            act.wait_ge(act_step, a_count.n)
            nc.scalar.activation(flat, flat, ACT.Exp, scale=-0.5).then_inc(qrs_done, 1)
            for it in range(AP_ + 1):
                if it < AP_:
                    n = AP_ * l + it
                    act.wait_ge(mx_done, n + 1)
                    for hd in range(2):
                        for blk in range(2):
                            cols = slice(0, P) if blk == 0 else slice(P, 384)
                            nc.scalar.activation(a_prob[it % 2][:, hd, cols], PS[:, 4 + 2 * (it % 2) + hd, cols], ACT.Exp,
                                                 bias=neg_m[:, it, hd, blk:blk + 1],
                                                 accum_out=p_sum[:, it, hd, blk:blk + 1]).then_inc(p_part, 1)
                    nc.scalar.activation(sink_e[:, it, :, :], mx[:, it, :, :], ACT.Exp).then_inc(p_done, 1)
                if it >= 1:
                    n = AP_ * l + it - 1
                    act.wait_ge(pt_ready, n + 1)
                    if it >= 2:
                        act.wait_ge(ao_ready, n)
                    nc.scalar.activation(a_probT[:, :, :], PS[:, 2:4, 0:384], ACT.Copy).then_inc(pt_done, 1)

            def bounds(h):
                n = MH * l + h
                act.wait_ge(d_ready, n + 1)
                act.wait_ge(acol_done, l + 1)
                if h >= 2:
                    act.wait_ge(w_ready, n - 1)
                d = PS[:, 4 + h % 2, :]
                nc.scalar.activation(m_exp[h % 2][:, 0:T], d[:, 0:T], ACT.Exp, bias=a_col[:, 0, h:h + 1]).then_inc(x_done, 1)
                nc.scalar.activation(m_exp[h % 2][:, T:384], d[:, T:384], ACT.Exp, bias=a_col[:, 1, h:h + 1]).then_inc(x_done, 1)
                if h >= 2:
                    act.wait_ge(hm_done, n - 1)
                nc.scalar.activation(m_lim[h % 2][:, :], PS[:, 3, 0:T], ACT.Exp).then_inc(x_done, 1)

            bounds(0)
            for h in range(MH):
                n = MH * l + h
                if h + 1 < MH:
                    bounds(h + 1)
                act.wait_ge(hm_done, n + 1)
                if h >= 1:
                    act.wait_ge(hss_ready, n)
                nc.scalar.activation(m_sq[:, :], hm_raw[:, h % 2, :], ACT.Square).then_inc(hsq_done, 1)
                act.wait_ge(hss_ready, n + 1)
                if h >= 1:
                    act.wait_ge(hid_done, g.hid0 + 4 + h)
                nc.scalar.activation(m_rs[:, :], PS[:, 1, 0:T], ACT.Ln, bias=eps).then_inc(act_step, 1)
                a_count.one()
                act.wait_ge(act_step, a_count.n)
                nc.scalar.activation(m_rs[:, :], m_rs[:, :], ACT.Exp, scale=-0.5).then_inc(hrs_done, 1)

        def hyb_vector(dve, l):
            V = nc.vector
            g = G[f"gates{l}"]


            if l == 0:
                dve.wait_ge(ld_vec, 16 * N_VEC)
            dve.wait_ge(if_ready, l + 1)
            V.tensor_tensor(gate_if[:, :, :], PS[:, 7, 0:2 * IN_IF].rearrange("p (t f) -> p t f", t=2),
                            gate_bias[:, IN_IF * l:IN_IF * l + IN_IF].unsqueeze(1).to_broadcast([P, 2, IN_IF]),
                            ALU.add).then_inc(gi_done, 1)
            dve.wait_ge(gi_done, l + 1)
            V.tensor_scalar(nlf[:, :, :], gate_if[:, :, MH:2 * MH], -1.0, 0.0, ALU.mult, ALU.max).then_inc(dve_step, 1)
            dve.wait_ge(dve_step, v_count.one())
            dve.wait_ge(soft_f, l + 1)
            V.tensor_tensor(nlf[:, :, :], nlf[:, :, :], nlf_t[:, :, :], ALU.add).then_inc(nlf_done, 1)
            dve.wait_ge(gain_done, 2)
            dve.wait_ge(qrs_done, l + 1)
            V.scalar_tensor_tensor(out=ztile[:, 0:4, :], in0=ztile[:, 0:4, :], scalar=q_gain[:, l:l + 1], in1=qk_buf[:, 0:4, :],
                                   op0=ALU.mult, op1=ALU.mult).then_inc(qn_done, 1)
            V.scalar_tensor_tensor(out=ztile[:, 4, :], in0=ztile[:, 4, :], scalar=column("k_norm", l, 0), in1=qk_buf[:, 4, :],
                                   op0=ALU.mult, op1=ALU.mult).then_inc(qn_done, 1)
            dve.wait_ge(qn_done, 2 * l + 2)
            dve.wait_ge(if_ready, l + 1)
            V.tensor_tensor(qk_rot[:, :, :], ztile[:, 0:5, :], C("cos").unsqueeze(1).to_broadcast([P, 5, T]), ALU.mult).then_inc(dve_step, 1)
            dve.wait_ge(dve_step, v_count.one())
            dve.wait_ge(rot_ready, l + 1)
            sin = C("sin").unsqueeze(1)
            V.tensor_tensor(qk_buf[:, 0:4, :].rearrange("p (b a) t -> p b a t", b=2),
                            PS[:, 4:6, :].rearrange("p b (a t) -> p b a t", a=2),
                            sin.unsqueeze(1).to_broadcast([P, 2, 2, T]), ALU.mult).then_inc(dve_step, 1)
            dve.wait_ge(dve_step, v_count.one())
            V.tensor_tensor(qk_buf[:, 4, :], PS[:, 6, 0:T], C("sin"), ALU.mult).then_inc(dve_step, 1)
            dve.wait_ge(dve_step, v_count.one())
            V.tensor_tensor(qk_rot[:, :, :], qk_rot[:, :, :], qk_buf[:, :, :], ALU.add).then_inc(dve_step, 1)
            dve.wait_ge(dve_step, v_count.one())
            V.tensor_copy(k_dup[0:HD, 0, :], qk_rot[0:HD, 4, :])
            V.tensor_copy(k_dup[HD:P, 0, :], qk_rot[0:HD, 4, :])
            V.tensor_copy(k_dup[0:HD, 1, :], qk_rot[HD:P, 4, :])
            V.tensor_copy(k_dup[HD:P, 1, :], qk_rot[HD:P, 4, :]).then_inc(qr_done, 1)
            dve.wait_ge(rows_ready, l + 1)
            V.tensor_copy(a_col[:, :, :].rearrange("p t h -> p (t h)"),
                          PS[:, 7, 2 * IN_IF:2 * IN_IF + 2 * MH]).then_inc(acol_done, 1)
            for i in range(2):
                V.memset(row_a[i][:, 0:P], 0.0)
            V.tensor_scalar(row_a[0][:, P:P + T], PS[0:MH, 0, T:2 * T], 0.0, None, ALU.max).then_inc(dve_step, 1)
            dve.wait_ge(dve_step, v_count.one())
            for i in range(8):
                a, b = row_a[i % 2], row_a[(i + 1) % 2]
                V.tensor_tensor(b[:, P:P + T], a[:, P:P + T], a[:, P - (1 << i):P + T - (1 << i)], ALU.max).then_inc(dve_step, 1)
                dve.wait_ge(dve_step, v_count.one())
            V.tensor_tensor(row_e[:, :], PS[0:MH, 0, 0:T], row_a[0][:, P:P + T], ALU.subtract).then_inc(rows_done, 1)
            snk = sinks[:, AH * l:AH * l + AH].rearrange("p (a h) -> p a h", a=AP_)

            def normalise(p):
                n = AP_ * l + p
                dve.wait_ge(p_done, n + 1)
                dve.wait_ge(p_part, 4 * n + 4)
                V.tensor_tensor(p_inv[:, p, :, :], p_sum[:, p, :, :], sink_e[:, p, :, :], ALU.add).then_inc(dve_step, 1)
                dve.wait_ge(dve_step, v_count.one())
                V.reciprocal(p_inv[:, p, :, :], p_inv[:, p, :, :]).then_inc(dve_step, 1)
                dve.wait_ge(dve_step, v_count.one())
                for hd in range(2):
                    for blk in range(2):
                        pr = a_prob[p % 2][:, hd, 0:P] if blk == 0 else a_prob[p % 2][:, hd, P:384]
                        ins = V.tensor_scalar(pr, pr, p_inv[:, p, hd, blk:blk + 1], None, ALU.mult)
                        if hd + blk < 2:
                            ins.then_inc(dve_step, 1)
                            v_count.one()
                        else:
                            ins.then_inc(pn_done, 1)

            def head_out(p):
                n = AP_ * l + p
                dve.wait_ge(ao_ready, n + 1)
                o = PS[:, 1 - p % 2, 0:T]
                V.tensor_copy(hid_hi[:, p, :], o).then_inc(ao_hi, 1)
                dve.wait_ge(ao_hi, n + 1)
                V.tensor_tensor(hid_lo[:, p, :], o, hid_hi[:, p, :].bitcast(F32), ALU.subtract).then_inc(hid_done, 1)

            for it in range(AP_ + 2):
                if it < AP_:
                    n = AP_ * l + it
                    dve.wait_ge(s_ready, n + 1)
                    if it >= 2:
                        dve.wait_ge(pt_ready, n - 1)
                    s = PS[:, 4 + 2 * (it % 2):6 + 2 * (it % 2), :]
                    V.tensor_reduce(mx[:, it, :, 0], s[:, :, 0:P], AX, ALU.max)
                    V.tensor_reduce(mx[:, it, :, 1], s[:, :, P:384], AX, ALU.max).then_inc(dve_step, 1)
                    dve.wait_ge(dve_step, v_count.one())
                    sk = snk[:, it, :].unsqueeze(2).to_broadcast([P, 2, 2])
                    V.tensor_tensor(mx[:, it, :, :], mx[:, it, :, :], sk, ALU.max).then_inc(dve_step, 1)
                    dve.wait_ge(dve_step, v_count.one())
                    V.tensor_scalar(neg_m[:, it, :, :], mx[:, it, :, :], -1.0, None, ALU.mult).then_inc(dve_step, 1)
                    dve.wait_ge(dve_step, v_count.one())
                    V.tensor_tensor(mx[:, it, :, :], neg_m[:, it, :, :], sk, ALU.add).then_inc(mx_done, 1)
                if 1 <= it <= AP_:
                    normalise(it - 1)
                if it >= 2:
                    head_out(it - 2)

            def weights(h):
                n = MH * l + h
                dve.wait_ge(x_done, 3 * n + 2)
                if h >= 2:
                    dve.wait_ge(nd_ready, n - 1)
                V.scalar_tensor_tensor(out=m_w[h % 2][:, :], in0=PS[:, 6 + h % 2, 0:384], scalar=HD ** -0.5,
                                       in1=m_exp[h % 2][:, :], op0=ALU.mult, op1=ALU.mult).then_inc(w_ready, 1)

            weights(0)
            for h in range(MH):
                n = MH * l + h
                if h + 1 < MH:
                    weights(h + 1)
                dve.wait_ge(nd_ready, n + 1)
                dve.wait_ge(x_done, 3 * n + 3)
                V.scalar_tensor_tensor(out=m_den[:, :], in0=PS[:, 2, T:2 * T], scalar=-1.0, in1=m_lim[h % 2][:, :],
                                       op0=ALU.mult, op1=ALU.max).then_inc(dve_step, 1)
                dve.wait_ge(dve_step, v_count.one())
                V.tensor_tensor(m_den[:, :], PS[:, 2, T:2 * T], m_den[:, :], ALU.max).then_inc(dve_step, 1)
                dve.wait_ge(dve_step, v_count.one())
                V.reciprocal(m_den[:, :], m_den[:, :]).then_inc(dve_step, 1)
                dve.wait_ge(dve_step, v_count.one())
                V.tensor_tensor(hm_raw[:, h % 2, :], PS[:, 2, 0:T], m_den[:, :], ALU.mult).then_inc(hm_done, 1)
                dve.wait_ge(hm_done, n + 1)
                dve.wait_ge(hrs_done, n + 1)
                V.scalar_tensor_tensor(out=m_out[:, :], in0=hm_raw[:, h % 2, :], scalar=column("head", l, h),
                                       in1=m_rs[:, :], op0=ALU.mult, op1=ALU.mult).then_inc(dve_step, 1)
                dve.wait_ge(dve_step, v_count.one())
                V.tensor_tensor(m_out[:, :], m_out[:, :], sig_o[:, h, :], ALU.mult).then_inc(dve_step, 1)
                dve.wait_ge(dve_step, v_count.one())
                V.tensor_copy(hid_hi[:, 4 + h, :], m_out[:, :]).then_inc(hm_hi, 1)
                dve.wait_ge(hm_hi, n + 1)
                V.tensor_tensor(hid_lo[:, 4 + h, :], m_out[:, :], hid_hi[:, 4 + h, :].bitcast(F32),
                                ALU.subtract).then_inc(hid_done, 1)

        out_sb = sb("out_sb", [P, 2, D], "xc")
        out_t, out_done, stored = S("out_t"), S("out_done"), S("stored")

        def result_tensor(pe, n_res):
            pe.wait_ge(resid_done, n_res)
            pe.wait_ge(xt_done, KT)
            for t in range(2):
                for f in range(KT):
                    last = nc.tensor.transpose(PS[:, 4 + 2 * t + f // 4, (f % 4) * P:(f % 4 + 1) * P], res[:, f, P * t:P * t + P], ident)
                    if f % 4 == 3:
                        last.then_inc(out_t, 1)

        def result_scalar(act):
            for i in range(4):
                act.wait_ge(out_t, i + 1)
                nc.scalar.activation(out_sb[:, i // 2, 512 * (i % 2):512 * (i % 2) + 512], PS[:, 4 + i, :],
                                     ACT.Copy).then_inc(out_done, 1)

        def result_sync(sp):
            for i in range(4):
                sp.wait_ge(out_done, i + 1)
                t, c = i // 2, 512 * (i % 2)
                sp.dma_start(out[P * t:P * t + P, c:c + 512], out_sb[:, t, c:c + 512]).then_inc(stored, 16)
            sp.wait_ge(stored, 64)

        soft_f, p_part = S("soft_f"), S("p_part")
        block = ctx.enter_context(nc.Block())

        @block.sync
        def _(sp):
            s5_loads(sp)
            s5_toeplitz(sp)
            sp.wait_ge(k_ready, 16)
            sp.wait_ge(sout_done, NB)
            for g in gemms:
                chunk_loop(sp, g.n, 4 if g.shape == "kt4" else (RING if g.c0 == 0 else 0), 0,
                           lambda idx, k, turn: load_chunk(sp, g, idx, k))
            result_sync(sp)

        @block.gpsimd
        def _(pool):
            s5_pool(pool)
            chunk_loop(pool, n_chunks, 0, 0, lambda idx, k, turn: split_lo(pool, 0, idx, k, 1, lo_pool))

        @block.tensor
        def _(pe):
            s5_tensor(pe)
            norm = 0
            for g in gemms:
                gemm_tensor(pe, g)
                if g.evac == "resid":
                    if norm < 8 and g.name != "ff2_1":
                        norm_tensor(pe, norm)
                        norm += 1
                    if norm == 4:
                        norm_tensor(pe, norm)
                        norm += 1
                elif g.name == "v":
                    sb_tensor(pe)
                elif g.name.startswith("gates"):
                    hyb_tensor(pe, int(g.name[-1]))
            result_tensor(pe, 32)

        @block.scalar
        def _(act):
            s5_scalar(act)
            norm = 0
            for g in gemms:
                gemm_scalar(act, g)
                if g.evac == "resid":
                    if g.name != "ff2_1":
                        norm_scalar(act, norm)
                        norm += 1
                    if norm == 4:
                        norm_scalar(act, norm)
                        norm += 1
                elif g.name == "v":
                    sb_scalar(act)
                elif g.name.startswith("gates"):
                    hyb_scalar(act, int(g.name[-1]))
            result_scalar(act)

        @block.vector
        def _(dve):
            s5_vector(dve)
            norm = 0
            for g in gemms:
                gemm_vector(dve, g)
                if g.evac == "resid":
                    if g.name != "ff2_1":
                        norm_vector(dve, norm)
                        norm += 1
                    if norm == 4:
                        norm_vector(dve, norm)
                        norm += 1
                elif g.name == "v":
                    sb_vector(dve)
                elif g.name.startswith("gates"):
                    hyb_vector(dve, int(g.name[-1]))


def kernel(**inputs):
    import numpy as _np
    import concourse.bacc as _bacc
    from concourse import mybir as _mybir
    from concourse.bass_utils import run_bass_kernel_spmd as _run

    nc = _bacc.Bacc("TRN2", target_bir_lowering=False, num_devices=1)
    arrays, aps = {}, {}
    feed = {name: _np.ascontiguousarray(a) for name, a in inputs.items()}
    feed["consts"] = constants()
    for name, a in feed.items():
        arrays[f"in_{name}_dram"] = a
        aps[name] = nc.dram_tensor(f"in_{name}_dram", a.shape, _mybir.dt.from_np(a.dtype), kind="ExternalInput").ap()
    out = nc.dram_tensor("out_0_dram", (T, D), F32, kind="ExternalOutput").ap()
    stack(nc, aps, out)
    r = _run(nc, [arrays], core_ids=[0])
    return r.results[0]["out_0_dram"].reshape(1, T, D)
```

```python
from contextlib import ExitStack

import numpy as np

import concourse.bass as bass
from concourse import mybir

F32 = mybir.dt.float32
F32R = mybir.dt.float32r
I32 = mybir.dt.int32
ACT = mybir.ActivationFunctionType
ALU = mybir.AluOpType
AX = mybir.AxisListType.X
LN_EXP = "natural_log_exp_and_others"

P = 128
T = 256
D = 1024
KT = D // P
FFN = 2816
FF = 4096
ALPHA = 4.0 ** 0.25
LN_EPS, RMS_EPS = 1e-5, 1e-6
RING = 3
CH = 2048
HALF = CH // 2

SG, SH, SP, SL = 64, 16, 64, 8
SC = T // SL
SB_HEADS, HD = 16, 64
AH, AKV = 8, 2
MH = 4
IN_QKVO = 2304
IN_IF = 8
BIG = -1.0e30

_WIDTHS = [("ident", P), ("mean_d", P), ("negtri", P), ("negones", P), ("sb_keep", P), ("sb_mask", P),
           ("win_prev", P), ("win_diag", P), ("m_mask", P), ("tri", P), ("ones", P), ("mean_h", P), ("mean_v", P),
           ("rot", P), ("cos", T), ("sin", T), ("sel_neg", MH * P), ("sel_pos", MH * P), ("sgn", 8)]
CONST = {}
_at = 0
for _n, _w in _WIDTHS:
    CONST[_n] = (_at, _w)
    _at += _w
N_CONST = _at


def constants():
    c = np.zeros((P, N_CONST), np.float32)

    def put(name, value):
        at, w = CONST[name]
        c[:value.shape[0], at:at + w] = value

    i, j = np.arange(P)[:, None], np.arange(P)[None, :]
    put("ident", (i == j).astype(np.float32))
    put("mean_d", np.full((P, P), 1.0 / D, np.float32))
    put("negtri", -(i >= j).astype(np.float32))
    put("negones", np.full((P, P), -1.0, np.float32))
    put("sb_keep", (i < j).astype(np.float32))
    put("sb_mask", np.where(i < j, 0.0, BIG).astype(np.float32))
    put("win_prev", np.where(j > i, 0.0, BIG).astype(np.float32))
    put("win_diag", np.where(j <= i, 0.0, BIG).astype(np.float32))
    put("m_mask", np.where(i <= j, 0.0, BIG).astype(np.float32))
    put("tri", (i <= j).astype(np.float32))
    put("ones", np.ones((P, P), np.float32))
    put("mean_h", (i // HD == j // HD).astype(np.float32) / HD)
    put("mean_v", np.full((P, P), 1.0 / P, np.float32))
    rd = HD // 4
    half = rd // 2
    rot = np.zeros((P, P), np.float32)
    cos, sin = np.ones((P, T), np.float32), np.zeros((P, T), np.float32)
    inv_freq = np.float32(500000.0) ** (-np.arange(0, rd, 2, dtype=np.float32) / np.float32(rd))
    ang = np.arange(T, dtype=np.float32)[None, :] * inv_freq[:, None]
    for b in (0, HD):
        for f in range(half):
            rot[b + half + f, b + f] = -1.0
            rot[b + f, b + half + f] = 1.0
        cos[b:b + half], cos[b + half:b + rd] = np.cos(ang), np.cos(ang)
        sin[b:b + half], sin[b + half:b + rd] = np.sin(ang), np.sin(ang)
    put("rot", rot)
    put("cos", cos)
    put("sin", sin)
    sel = np.zeros((MH, MH * P), np.float32)
    for h in range(MH):
        sel[h, h * P:(h + 1) * P] = 1.0
    put("sel_neg", -sel)
    put("sel_pos", sel)
    sgn = np.ones((P, 8), np.float32)
    sgn[:SP, 0] = -1.0
    sgn[SP:, 1] = -1.0
    sgn[:, 2] = LN_EPS
    sgn[:, 3] = RMS_EPS
    sgn[:, 4] = 0.0
    put("sgn", sgn)
    return c


class Count:

    def __init__(self):
        self.n = 0

    def one(self):
        self.n += 1
        return self.n


class Gemm:

    def __init__(self, name, n, shape, evac, src, x=None, func=None, alpha=None, per=None, scale=None, layer=None,
                 half=False, normed=0, order=0):
        self.name, self.n, self.shape, self.evac, self.src = name, n, shape, evac, src
        self.x, self.func, self.alpha, self.per = x, func, alpha, per
        self.scale, self.layer, self.half = scale, layer, half
        self.normed, self.order = normed, order


def plan(w):

    def kt8(m, col=0):
        v = m.rearrange("(k p) n -> p k n", p=P)
        return lambda i: [v[:, :, bass.ds(i * 256 + col, 256)]]

    def pair(m, gate):
        v = m.rearrange("(k p) (two n) -> two p k n", p=P, two=2)
        return lambda i: [v[1 - gate, :, :, bass.ds(i * P, P)], v[gate, :, :, bass.ds(i * P, P)]]

    def kt2(m):
        v = m.rearrange("(c k p) n -> p c k n", k=2, p=P)
        return lambda i: [v[:, bass.ds(i, 1), :, :]]

    def branch(a, m):
        va = a.rearrange("(k p) n -> p k n", p=P)
        vm = m.rearrange("(k p) n -> p k n", p=P)
        return lambda i: [(va, vm)[i // 2][:, :, 512 * (i % 2):512 * (i % 2) + 512]]

    gs = [Gemm("glu", 8, "kt8", "gated", pair(w["ssm_w_glu"][0], 1), x=0, func=ACT.Sigmoid),
          Gemm("ssm_out", 4, "kt8", "resid", kt8(w["ssm_w_out"][0]), alpha=ALPHA),
          Gemm("gu0", 22, "kt8", "gated", pair(w["ffn_w_gu"][0], 0), x=1, func=ACT.Silu),
          Gemm("down0", 11, "kt2", "resid", kt2(w["ffn_w_down"][0]), alpha=ALPHA, per=1, normed=KT),
          Gemm("q", 4, "kt8", "copy", kt8(w["sb_w_qkv"][0]), x=2, scale=HD ** -0.5),
          Gemm("k", 4, "kt8", "copy", kt8(w["sb_w_qkv"][0], D), x=2, scale=1.0),
          Gemm("v", 4, "kt8", "copy", kt8(w["sb_w_qkv"][0], 2 * D), x=2, scale=1.0),
          Gemm("sb_out", 4, "kt8", "resid", kt8(w["sb_w_o"][0]), alpha=ALPHA, normed=2 * KT),
          Gemm("gu1", 22, "kt8", "gated", pair(w["ffn_w_gu"][1], 0), x=3, func=ACT.Silu),
          Gemm("down1", 11, "kt2", "resid", kt2(w["ffn_w_down"][1]), alpha=ALPHA, per=1, normed=3 * KT, order=1)]
    for l in range(2):
        win = w["w_in_2"][l]
        gs += [Gemm(f"in{l}", 7, "kt8", "copy", kt8(win), x=4 + 2 * l, scale=1.0),
               Gemm(f"o{l}", 2, "kt8", "sig_o", kt8(win, 1792), x=4 + 2 * l),
               Gemm(f"gates{l}", 8, "kt8", "sig_g", kt8(win, IN_QKVO + IN_IF), x=4 + 2 * l, layer=l),
               Gemm(f"mix{l}", 4, "kt4", "mix", branch(w["w_att_branch_2"][l], w["w_m_branch_2"][l]), layer=l),
               Gemm(f"out{l}", 4, "kt8", "resid", kt8(w["w_out_2"][l]), alpha=1.0, half=True, layer=l),
               Gemm(f"ff1_{l}", 16, "kt8", "relu2", kt8(w["w_ff1_2"][l]), x=5 + 2 * l),
               Gemm(f"ff2_{l}", 16, "kt2", "resid", kt2(w["w_ff2_2"][l]), alpha=1.0, per=2, order=2 + l)]
    c = bank = 0
    cnt = {"gated": 0, "act": 0, "relu": 0, "resid": 0, "hid": 0, "seq": 0}
    prev = None
    for g in gs:
        g.c0, g.bank0 = c, bank
        g.gated0, g.act0, g.relu0, g.resid0 = cnt["gated"], cnt["act"], cnt["relu"], cnt["resid"]
        g.in_hid = prev_hid0 if prev else 0
        if g.evac in ("copy", "sig_o", "sig_g"):
            cnt["act"] += g.n
        elif g.evac == "gated":
            cnt["gated"] += g.n
        elif g.evac == "relu2":
            cnt["relu"] += g.n
        elif g.evac == "resid":
            cnt["resid"] += 4
        before = cnt["hid"]
        if g.evac in ("gated", "relu2"):
            cnt["hid"] += g.n
        elif g.evac == "mix":
            cnt["hid"] += 4
        g.hid0 = before
        if g.name == "v":
            cnt["hid"] += 8
        if g.name.startswith("gates"):
            cnt["hid"] += 8
        prev_hid0, prev = before, g
        g.run0 = 0
        c += g.n
        if g.shape == "kt8":
            bank += g.n
    for a, b in zip(gs, gs[1:]):
        if a.evac in ("copy", "sig_o", "sig_g") and b.evac in ("copy", "sig_o", "sig_g"):
            b.run0 = a.run0 + a.n
    return gs, c


def stack(nc, w, out):
    gemms, n_chunks = plan(w)
    G = {g.name: g for g in gemms}
    ctx = ExitStack()
    with ctx:
        base = 16512
        fence = ctx.enter_context(nc.sbuf_tensor("fence", [P, (229344 - base) // 4 - 16], F32))
        del fence
        place = {}
        at = base
        for name, size in [("const", 4 * N_CONST), ("vec", 512), ("misc", 3072), ("raw", 4 * CH * RING),
                           ("wh", 4 * CH * RING), ("wl", 4 * CH * RING), ("res", 8192), ("xh", 8192), ("xl", 8192),
                           ("hh", 32768), ("hl", 32768), ("xc", 8192), ("sq", 4096), ("sg", 6144), ("zt", 2048),
                           ("rstd", 1024), ("extra", 10240)]:
            place[name] = at
            at += size
        assert at <= 229344 - 64, at

        def sb(name, shape, region, off=0, dt=F32):
            return nc.alloc_sbuf_tensor_at(name, shape, dt, offset=place[region] + off)

        const = sb("const", [P, N_CONST], "const")
        raw = [sb(f"raw{s}", [P, CH], "raw", 4 * CH * s) for s in range(RING)]
        w_hi = [sb(f"w_hi{s}", [P, CH], "wh", 4 * CH * s, F32R) for s in range(RING)]
        w_lo = [sb(f"w_lo{s}", [P, CH], "wl", 4 * CH * s, F32R) for s in range(RING)]
        res = sb("res", [P, KT, T], "res")
        x_hi = sb("x_hi", [P, KT, T], "xh", 0, F32R)
        x_lo = sb("x_lo", [P, KT, T], "xl", 0, F32R)
        hid_hi = sb("hid_hi", [P, 32, T], "hh", 0, F32R)
        hid_lo = sb("hid_lo", [P, 32, T], "hl", 0, F32R)
        xn = sb("xn", [P, KT, T], "xc")
        sqr = sb("sqr", [P, 2, 512], "sq")
        gate_sb = sb("gate_sb", [P, RING, 512], "sg")
        prod = sb("prod", [P, 512], "zt")
        rstd = sb("rstd", [P, T], "rstd")
        vec_rows = sb("vec_rows", [108, P], "misc")
        vec = sb("vec", [P, 108], "vec")
        PS = ctx.enter_context(nc.psum_tensor("PS", [P, 8, 512], F32))
        acc = PS[:, 4:8, :]

        def C(name, rows=P):
            a, n = CONST[name]
            return const[0:rows, a:a + n]

        def column(kind, l, k):
            first = {"ln_mix_g": 0, "ln_mix_b": 16, "ln_ffn_g": 32, "ln_ffn_b": 48, "norm_mix": 64,
                     "norm_ffn": 80}
            if kind in first:
                c = first[kind] + 8 * l + k
            else:
                c = {"head": 96 + 4 * l + k, "q_norm": 104 + l, "k_norm": 106 + l}[kind]
            return vec[:, c:c + 1]

        ident = C("ident")

        a_count, v_count = Count(), Count()
        sems = {}

        def S(name):
            if name not in sems:
                sems[name] = ctx.enter_context(nc.semaphore(name))
            return sems[name]

        raw_ready = [S(f"raw_ready{s}") for s in range(RING)]
        act_step, dve_step = S("act_step"), S("dve_step")
        hi_done, lo_dve, lo_pool = S("hi_done"), S("lo_dve"), S("lo_pool")
        chunk_done = S("chunk_done")
        sig_done, z_done = S("sig_done"), S("z_done")
        act_done, relu_done, u_done = S("act_done"), S("relu_done"), S("u_done")
        resid_done, mix_done = S("resid_done"), S("mix_done")
        gated_hi, relu_hi, hid_done = S("gated_hi"), S("relu_hi"), S("hid_done")
        xh_done, xl_done = S("xh_done"), S("xl_done")
        sigg_done, mix_ready, acc_done = S("sigg_done"), S("mix_ready"), S("acc_done")

        def chunk_loop(eng, n, head, tail, body):
            for i in range(min(head, n)):
                body(i, i % RING, i // RING)
            mid = max(n - head - tail, 0)
            turns = mid // RING
            if turns >= 2:
                with eng.Fori(0, turns) as t:
                    for k in range(RING):
                        body(t * RING + (head + k), (head + k) % RING, t + (head + k) // RING)
                start = head + turns * RING
            else:
                start = head
            for i in range(start, n):
                body(i, i % RING, i // RING)

        def load_chunk(eng, g, idx, k):
            j = g.c0 + idx
            s = (g.c0 + k) % RING
            if not isinstance(j, int) or j >= RING:
                eng.wait_ge(lo_dve, j - (RING - 1))
                eng.wait_ge(lo_pool, j - (RING - 1))
            srcs = g.src(idx)
            if g.shape == "kt2":
                src = srcs[0].rearrange("p c k n -> p (c k) n")
                parts = [src[:, 0:1, :], src[:, 1:2, :]]
                dst = raw[s][:, :].rearrange("p (k n) -> p k n", k=2)
                dsts = [dst[:, 0:1, :], dst[:, 1:2, :]]
            elif g.evac == "gated":
                parts = srcs
                dst = raw[s][:, :].rearrange("p (k m n) -> p m k n", k=8, m=2)
                dsts = [dst[:, 0], dst[:, 1]]
            else:
                kt = 8 if g.shape == "kt8" else 4
                parts = [srcs[0][:, 0:kt // 2, :], srcs[0][:, kt // 2:kt, :]]
                dst = raw[s][:, :].rearrange("p (k n) -> p k n", k=kt)
                dsts = [dst[:, 0:kt // 2, :], dst[:, kt // 2:kt, :]]
            for d, q in zip(dsts, parts):
                eng.dma_start(d, q).then_inc(raw_ready[s], 16)

        def split_hi(act, c, k, turn):
            s = (c + k) % RING
            act.wait_ge(raw_ready[s], turn * 32 + ((c + k) // RING + 1) * 32)
            nc.scalar.activation(w_hi[s][:, :], raw[s][:, :], ACT.Copy).then_inc(hi_done, 1)

        def split_lo(eng, c, idx, k, half, done):
            s = (c + k) % RING
            e = nc.vector if half == 0 else nc.gpsimd
            eng.wait_ge(hi_done, idx + (c + 1))
            cols = slice(half * HALF, (half + 1) * HALF)
            e.tensor_tensor(w_lo[s][:, cols], raw[s][:, cols], w_hi[s][:, cols].bitcast(F32),
                              ALU.subtract).then_inc(done, 1)

        def base_of(g):
            return {"gated": (z_done, g.gated0), "relu2": (relu_done, g.relu0), "resid": (resid_done, g.resid0),
                    }.get(g.evac, (act_done, g.act0))

        def gemm_head(g):
            return 3 if base_of(g)[1] == 0 else 1

        def gemm_tensor(pe, g, only=None):
            drained, first = base_of(g)

            def three(dst, lhs_hi, lhs_lo, r_hi, r_lo, start, stop):
                nc.tensor.matmul(dst, lhs_hi, r_hi, start=start, stop=False, skip_group_check=True)
                nc.tensor.matmul(dst, lhs_hi, r_lo, start=False, stop=False, skip_group_check=True)
                return nc.tensor.matmul(dst, lhs_lo, r_hi, start=False, stop=stop, skip_group_check=True)

            def body(idx, k, turn):
                s = (g.c0 + k) % RING
                head = isinstance(idx, int)
                pe.wait_ge(lo_dve, idx + (g.c0 + 1))
                pe.wait_ge(lo_pool, idx + (g.c0 + 1))
                if g.shape == "kt8":
                    bank = (g.bank0 + k) % RING
                    if g.evac == "sig_g":
                        pe.wait_ge(drained, idx + first)
                    elif not head or idx + g.run0 >= RING:
                        pe.wait_ge(drained, idx + (first - 2))
                    if g.evac == "sig_g":
                        bank = 0
                    elif g.half:
                        bank = OUT_BANKS[bank]
                    hi = w_hi[s][:, :].rearrange("p (k m n) -> p k m n", k=8, m=2)
                    lo = w_lo[s][:, :].rearrange("p (k m n) -> p k m n", k=8, m=2)
                    first_chunk = head and idx == 0
                    if first_chunk and g.half:
                        pe.wait_ge(hid_done, g.in_hid + 2)
                    order = [(kt, m) for kt in range(KT) for m in range(2)] if first_chunk else [
                        (kt, m) for m in range(2) for kt in range(KT)]
                    for kt, m in order:
                        if first_chunk and m == 0:
                            if g.x is not None:
                                pe.wait_ge(xl_done, KT * g.x + kt + 1)
                            else:
                                pe.wait_ge(hid_done, g.in_hid + (kt // 2 if g.half else kt) + 1)
                        if g.x is not None:
                            a, b = x_hi[:, kt, :], x_lo[:, kt, :]
                        else:
                            t0 = 8 if g.half else 0
                            a, b = hid_hi[:, t0 + kt, :], hid_lo[:, t0 + kt, :]
                        last = three(PS[:, bank, m * T:(m + 1) * T], hi[:, kt, m, :], lo[:, kt, m, :], a, b,
                                     kt == 0 and m == 0, kt == KT - 1)
                elif g.shape == "kt4":
                    which, half = idx // 2, idx % 2
                    if which and half == 0:
                        pe.wait_ge(act_done, G[f"gates{g.layer}"].act0 + G[f"gates{g.layer}"].n)
                    hi = w_hi[s][:, :].rearrange("p (k m n) -> p k m n", k=4, m=4)
                    lo = w_lo[s][:, :].rearrange("p (k m n) -> p k m n", k=4, m=4)
                    for m in range(4):
                        for kt in range(4):
                            if m == 0 and half == 0:
                                pe.wait_ge(hid_done, g.in_hid + 4 * which + kt + 1)
                            dst = PS[:, mix_bank(half, which, m // 2), (m % 2) * T:(m % 2 + 1) * T]
                            last = three(dst, hi[:, kt, m, :], lo[:, kt, m, :], hid_hi[:, 4 * which + kt, :],
                                         hid_lo[:, 4 * which + kt, :], kt == 0 and m % 2 == 0, kt == 3)
                        if which == 1 and m == 1:
                            last.then_inc(mix_ready, 1)
                else:
                    pe.wait_ge(hid_done, idx * 2 + (g.in_hid + 2) if g.per == 1 else idx + (g.in_hid + 1))
                    hi = w_hi[s][:, :].rearrange("p (k m n) -> p k m n", k=2, m=8)
                    lo = w_lo[s][:, :].rearrange("p (k m n) -> p k m n", k=2, m=8)
                    for kt in range(2):
                        a = hid_hi[:, bass.ds(idx * 2 + kt, 1), :].rearrange("p a t -> p (a t)")
                        b = hid_lo[:, bass.ds(idx * 2 + kt, 1), :].rearrange("p a t -> p (a t)")
                        for m in range(8):
                            last = three(acc[:, m // 2, (m % 2) * T:(m % 2 + 1) * T], hi[:, kt, m, :], lo[:, kt, m, :],
                                         a, b, head and idx == 0 and kt == 0 and m % 2 == 0,
                                         head and idx == g.n - 1 and kt == 1)
                            if head and idx == g.n - 1 and kt == 1 and m in (1, 3, 5):
                                last.then_inc(acc_done, 1)
                last.then_inc(chunk_done, 1)
                if g.half and idx >= 1:
                    norm_squares_sum(pe, 5 + 2 * g.layer, idx - 1)

            if only is not None or g.shape == "kt4":
                for i in (2, 3) if only is None else (only,):
                    body(i, i % RING, i // RING)
                return
            chunk_loop(pe, g.n, gemm_head(g) if g.shape == "kt8" else 1,
                       1 if g.shape == "kt2" else 0, body)

        def gemm_scalar(act, g, only=None):
            def body(idx, k, turn):
                bank = (g.bank0 + k) % RING
                if g.half and idx == 0:
                    nc.scalar.preload_act_table_set(LN_EXP)
                act.wait_ge(chunk_done, idx + (g.c0 + 1))
                if g.half and idx == g.n - 1:
                    norm_squares(act, 5 + 2 * g.layer, idx)
                if g.evac == "gated":
                    nc.scalar.activation(gate_sb[:, k, 0:T], PS[:, bank, T:2 * T], g.func).then_inc(sig_done, 1)
                elif g.evac == "relu2":
                    if not isinstance(idx, int) or g.relu0 + idx >= RING:
                        act.wait_ge(u_done, idx + (g.relu0 - 2))
                    nc.scalar.activation(gate_sb[:, k, :], PS[:, bank, :], ACT.Relu).then_inc(relu_done, 1)
                elif g.evac == "copy":
                    nc.scalar.activation(proj(g, idx), PS[:, bank, :], ACT.Copy, scale=g.scale).then_inc(act_done, 1)
                elif g.evac == "sig_o":
                    nc.scalar.activation(sig_o[:, bass.ds(idx * 2, 2), :].rearrange("p a t -> p (a t)"),
                                         PS[:, bank, :], ACT.Sigmoid).then_inc(act_done, 1)
                if not isinstance(idx, int) or g.c0 + idx + RING < n_chunks:
                    split_hi(act, g.c0 + RING, k, turn)
                if g.half and idx < g.n - 1:
                    norm_squares(act, 5 + 2 * g.layer, idx)

            if only is not None or g.shape == "kt4":
                for i in (2, 3) if only is None else (only,):
                    body(i, i % RING, i // RING)
                return
            chunk_loop(act, g.n, 3 if g.evac == "relu2" and g.relu0 == 0 else 0,
                       RING if g.c0 + g.n == n_chunks else 0, body)

        def gates_drain(act, g, idx):
            act.wait_ge(chunk_done, g.c0 + idx + 1)
            nc.scalar.activation(sig_g[:, 2 * idx:2 * idx + 2, :].rearrange("p a t -> p (a t)"), PS[:, 0, :],
                                 ACT.Copy).then_inc(act_done, 1)

        def gates_hi(act, g, idx):
            split_hi(act, g.c0 + RING, idx % RING, idx // RING)

        def gates_lo(dve, g, idx):
            split_lo(dve, g.c0 + RING, idx, idx % RING, 0, lo_dve)

        def gates_sigmoid(act, g):
            act.wait_ge(act_done, g.act0 + g.n)
            for t in (0, 8, 4, 12):
                v = sig_g[:, t:t + 4, :].rearrange("p a t -> p (a t)")
                nc.scalar.activation(v, v, ACT.Sigmoid).then_inc(sigg_done, 1)

        def gemm_vector(dve, g, only=None):
            def body(idx, k, turn):
                bank = (g.bank0 + k) % RING
                if g.evac == "gated":
                    n = idx + (g.gated0 + 1)
                    dve.wait_ge(sig_done, n)
                    if not isinstance(idx, int) or n > 1:
                        dve.wait_ge(hid_done, idx + g.hid0)
                    hi = hid_hi[:, bass.ds(idx, 1), :].rearrange("p a t -> p (a t)")
                    lo = hid_lo[:, bass.ds(idx, 1), :].rearrange("p a t -> p (a t)")
                    nc.vector.tensor_tensor(prod[:, 0:T], PS[:, bank, 0:T], gate_sb[:, k, 0:T],
                                            ALU.mult).then_inc(z_done, 1)
                    dve.wait_ge(z_done, n)
                    nc.vector.tensor_copy(hi, prod[:, 0:T]).then_inc(gated_hi, 1)
                    dve.wait_ge(gated_hi, n)
                    nc.vector.tensor_tensor(lo, prod[:, 0:T], hi.bitcast(F32), ALU.subtract).then_inc(hid_done, 1)
                elif g.evac == "relu2":
                    n = idx + (g.relu0 + 1)
                    dve.wait_ge(relu_done, n)
                    dve.wait_ge(hid_done, idx + g.hid0)
                    hi = hid_hi[:, bass.ds(idx * 2, 2), :].rearrange("p a t -> p (a t)")
                    lo = hid_lo[:, bass.ds(idx * 2, 2), :].rearrange("p a t -> p (a t)")
                    nc.vector.tensor_tensor(prod[:, :], gate_sb[:, k, :], gate_sb[:, k, :],
                                            ALU.mult).then_inc(u_done, 1)
                    dve.wait_ge(u_done, n)
                    nc.vector.tensor_copy(hi, prod[:, :]).then_inc(relu_hi, 1)
                    dve.wait_ge(relu_hi, n)
                    nc.vector.tensor_tensor(lo, prod[:, :], hi.bitcast(F32), ALU.subtract).then_inc(hid_done, 1)
                elif g.evac == "resid" and g.shape == "kt8":
                    dve.wait_ge(chunk_done, idx + (g.c0 + 1))
                    if isinstance(idx, int) and idx == 0 and g.normed:
                        dve.wait_ge(res_normed, g.normed)
                    if g.half:
                        bank = OUT_BANKS[bank]
                    r = res[:, bass.ds(idx * 2, 2), :].rearrange("p a t -> p (a t)")
                    nc.vector.scalar_tensor_tensor(out=r, in0=r, scalar=g.alpha, in1=PS[:, bank, :], op0=ALU.mult,
                                                   op1=ALU.add).then_inc(resid_done, 1)
                elif g.evac == "mix" and idx >= 2:
                    mix_vector(dve, g, idx - 2)
                if not isinstance(idx, int) or g.c0 + idx + RING < n_chunks:
                    if g.shape == "kt2" and isinstance(idx, int) and idx == g.n - 1:
                        sum_resid(dve, g)
                    split_lo(dve, g.c0 + RING, idx, k, 0, lo_dve)
                elif g.shape == "kt2" and idx == g.n - 1:
                    sum_resid(dve, g)

            if only is not None or g.shape == "kt4":
                for i in (2, 3) if only is None else (only,):
                    body(i, i % RING, i // RING)
                return
            chunk_loop(dve, g.n, 0,
                       RING if g.c0 + g.n == n_chunks else (1 if g.shape == "kt2" else 0), body)

        def sum_resid(dve, g):
            if g.normed:
                dve.wait_ge(res_normed, g.normed)
            for q in range(4):
                if q < 3:
                    dve.wait_ge(acc_done, 3 * g.order + q + 1)
                else:
                    dve.wait_ge(chunk_done, g.c0 + g.n)
                r = res[:, 2 * q:2 * q + 2, :].rearrange("p a t -> p (a t)")
                nc.vector.scalar_tensor_tensor(out=r, in0=r, scalar=g.alpha, in1=acc[:, q, :], op0=ALU.mult,
                                               op1=ALU.add).then_inc(resid_done, 1)

        def mix_bank(half, which, q):
            return (4 + half + 2 * q) if which == 0 else 2 * half + q

        OUT_BANKS = (4, 6, 0)

        def mix_vector(dve, g, half):
            dve.wait_ge(sigg_done, 4 * g.layer + 2 * half + 2)
            for q in range(2):
                if q == 0:
                    dve.wait_ge(mix_ready, 2 * g.layer + half + 1)
                else:
                    dve.wait_ge(chunk_done, g.c0 + half + 3)
                if half or q:
                    dve.wait_ge(hid_done, g.hid0 + 2 * half + q)
                t = 4 * half + 2 * q
                ga = sig_g[:, t:t + 2, :].rearrange("p a t -> p (a t)")
                gm = sig_g[:, 8 + t:10 + t, :].rearrange("p a t -> p (a t)")
                hi = hid_hi[:, 8 + t:10 + t, :].rearrange("p a t -> p (a t)")
                lo = hid_lo[:, 8 + t:10 + t, :].rearrange("p a t -> p (a t)")
                nc.vector.tensor_tensor(prod[:, :], PS[:, mix_bank(half, 0, q), :], ga, ALU.mult).then_inc(dve_step, 1)
                v_count.one()
                nc.vector.tensor_tensor(gate_sb[:, 0, :], PS[:, mix_bank(half, 1, q), :], gm, ALU.mult).then_inc(dve_step, 1)
                dve.wait_ge(dve_step, v_count.one())
                nc.vector.tensor_tensor(prod[:, :], prod[:, :], gate_sb[:, 0, :], ALU.add).then_inc(mix_done, 1)
                dve.wait_ge(mix_done, 4 * g.layer + 2 * half + q + 1)
                nc.vector.tensor_copy(hi, prod[:, :]).then_inc(dve_step, 1)
                dve.wait_ge(dve_step, v_count.one())
                nc.vector.tensor_tensor(lo, prod[:, :], hi.bitcast(F32), ALU.subtract).then_inc(hid_done, 1)

        mean_ready, var_ready, rstd_done = S("mean_ready"), S("var_ready"), S("rstd_done")
        centred, sq_done, sq_used = S("centred"), S("sq_done"), S("sq_used")
        scaled, res_normed = S("scaled"), S("res_normed")
        LN_VEC = [("ln_mix_g", "ln_mix_b", 0), ("ln_ffn_g", "ln_ffn_b", 0), ("ln_mix_g", "ln_mix_b", 1),
                  ("ln_ffn_g", "ln_ffn_b", 1)]
        RMS_VEC = [("norm_mix", 0), ("norm_ffn", 0), ("norm_mix", 1), ("norm_ffn", 1)]

        def x_index(n):
            return n + 1 if n < 3 else n

        def res_wait(eng, n, q):
            if n < 4:
                eng.wait_ge(resid_done, 4 * n + q + 1)
            elif n == 4:
                eng.wait_ge(res_normed, 8 * 3 + 2 * q + 2)
            else:
                eng.wait_ge(resid_done, 4 * (n - 1) + q + 1)

        def var_bank(n):
            return 4 if n < 4 else 3

        def norm_tensor(pe, n):
            if n < 4:
                for kt in range(KT):
                    if kt % 2 == 0:
                        res_wait(pe, n, kt // 2)
                    last = nc.tensor.matmul(PS[:, 3, 0:T], C("mean_d"), res[:, kt, :], start=kt == 0, stop=kt == KT - 1)
                last.then_inc(mean_ready, 1)
            for q in range(3 if n in (5, 7) else 0, 4):
                norm_squares_sum(pe, n, q)

        def norm_squares_sum(pe, n, q):
            pe.wait_ge(sq_done, 4 * n + q + 1)
            for i in range(2):
                last = nc.tensor.matmul(PS[:, var_bank(n), 0:T], C("mean_d"), sqr[:, q % 2, i * T:(i + 1) * T],
                                        start=q + i == 0, stop=q + i == 4, skip_group_check=True)
            last.then_inc(sq_used if q < 3 else var_ready, 1)

        def norm_squares(act, n, q):
            if n < 4:
                act.wait_ge(centred, 4 * n + q + 1)
            else:
                res_wait(act, n, q)
            if q >= 2:
                act.wait_ge(sq_used, 3 * n + q - 1)
            nc.scalar.activation(sqr[:, q % 2, :], (xn if n < 4 else res)[:, 2 * q:2 * q + 2, :].rearrange("p a t -> p (a t)"),
                                 ACT.Square).then_inc(sq_done, 1)

        def norm_scalar(act, n):
            if n < 4:
                nc.scalar.preload_act_table_set(LN_EXP)
            if n < 4 or n == 6:
                for q in range(4):
                    norm_squares(act, n, q)
            act.wait_ge(var_ready, n + 1)
            eps = const[:, CONST["sgn"][0] + (2 if n < 4 else 3):][:, 0:1]
            nc.scalar.activation(rstd[:, :], PS[:, var_bank(n), 0:T], ACT.Ln, bias=eps).then_inc(act_step, 1)
            a_count.one()
            act.wait_ge(act_step, a_count.n)
            nc.scalar.activation(rstd[:, :], rstd[:, :], ACT.Exp, scale=-0.5).then_inc(rstd_done, 1)
            if n in (0, 2):
                nc.scalar.preload_act_table(ACT.Silu)

            def normed(kt):
                nc.scalar.activation(res[:, kt, :], xn[:, kt, :], ACT.Identity, bias=ln_bias(n, kt)).then_inc(res_normed, 1)

            for kt in range(KT):
                act.wait_ge(scaled, KT * n + kt + 1)
                if n < 3:
                    nc.scalar.activation(x_hi[:, kt, :], xn[:, kt, :], ACT.Identity, bias=ln_bias(n, kt)).then_inc(xh_done, 1)
                elif n > 3:
                    nc.scalar.activation(x_hi[:, kt, :], xn[:, kt, :], ACT.Copy).then_inc(xh_done, 1)
                elif n == 3:
                    normed(kt)
                    if kt % 2:
                        norm_squares(act, 4, kt // 2)
            if n < 3:
                for kt in range(KT):
                    normed(kt)

        def ln_bias(n, kt):
            return column(LN_VEC[n][1], LN_VEC[n][2], kt)

        def norm_vector(dve, n):
            if n < 4:
                dve.wait_ge(mean_ready, n + 1)
                for q in range(4):
                    nc.vector.tensor_tensor(xn[:, 2 * q:2 * q + 2, :], res[:, 2 * q:2 * q + 2, :],
                                            PS[:, 3, 0:T].unsqueeze(1).to_broadcast([P, 2, T]),
                                            ALU.subtract).then_inc(centred, 1)
            dve.wait_ge(rstd_done, n + 1)
            if n < 4:
                dve.wait_ge(centred, 4 * n + 4)

            def scale(kt):
                gain = column(LN_VEC[n][0], LN_VEC[n][2], kt) if n < 4 else column(RMS_VEC[n - 4][0], RMS_VEC[n - 4][1], kt)
                nc.vector.scalar_tensor_tensor(out=xn[:, kt, :], in0=(xn if n < 4 else res)[:, kt, :], scalar=gain,
                                               in1=rstd[:, :], op0=ALU.mult, op1=ALU.mult).then_inc(scaled, 1)

            def split(kt):
                dve.wait_ge(scaled, KT * n + kt + 1)
                dve.wait_ge(xh_done, KT * x_index(n) + kt + 1)
                hi = x_hi[:, kt, :].bitcast(F32)
                if n < 4:
                    nc.vector.scalar_tensor_tensor(out=x_lo[:, kt, :], in0=xn[:, kt, :], scalar=ln_bias(n, kt), in1=hi,
                                                   op0=ALU.add, op1=ALU.subtract).then_inc(xl_done, 1)
                else:
                    nc.vector.tensor_tensor(x_lo[:, kt, :], xn[:, kt, :], hi, ALU.subtract).then_inc(xl_done, 1)

            ahead = 3
            for kt in range(KT + ahead):
                if kt < KT:
                    scale(kt)
                if kt >= ahead and n != 3:
                    split(kt - ahead)

        qkv = sb("qkv", [P, 16, T], "hh", 16 * 4 * T)
        v_feat = sb("v_feat", [P, 8, T], "hl", 16 * 4 * T)
        v_tok = sb("v_tok", [P, 2, D], "hl", 24 * 4 * T)
        sb_soft = [sb(f"sb_soft{i}", [P, 2, 384], "sg" if i == 0 else "extra", 0) for i in range(2)]
        sb_nl = [sb(f"sb_nl{i}", [P, 2, 384], "extra", 3072 * (i + 1)) for i in range(2)]
        sb_w = [sb(f"sb_w{i}", [P, 2, 384], "sg" if i == 0 else "sq", 3072 if i == 0 else 0) for i in range(2)]
        vt_ready, vt_done, z_ready, nl_done = S("vt_ready"), S("vt_done"), S("z_ready"), S("nl_done")
        soft_done, cum_ready, w_done, o_ready = S("soft_done"), S("cum_ready"), S("w_done"), S("o_ready")
        sb_hi = S("sb_hi")
        PAIRS = SB_HEADS // 2

        def z_banks(hp):
            return PS[:, 2 * (hp % 2):2 * (hp % 2) + 2, :]

        def sb_tensor(pe):
            pe.wait_ge(act_done, G["v"].act0 + G["v"].n)
            for half in range(2):
                for f in range(8):
                    last = nc.tensor.transpose(PS[:, 4 + 2 * half + f // 4, (f % 4) * P:(f % 4 + 1) * P],
                                               v_feat[:, f, half * P:(half + 1) * P], ident)
                    if f % 4 == 3:
                        last.then_inc(vt_ready, 1)

            def scores(hp):
                if hp >= 2:
                    pe.wait_ge(w_done, hp - 1)
                for hd in range(2):
                    b = HD * hd
                    z = PS[:, 2 * (hp % 2) + hd, :]
                    q, k = qkv[b:b + HD, hp, :], qkv[b:b + HD, 8 + hp, :]
                    nc.tensor.matmul(z[:, 0:T], k[:, 0:P], q, start=True, stop=False, skip_group_check=True)
                    last = nc.tensor.matmul(z[:, T:T + P], k[:, P:T], q[:, P:T], start=False, stop=False,
                                            skip_group_check=True)
                last.then_inc(z_ready, 1)

            def running_sums(hp):
                pe.wait_ge(nl_done, hp + 1)
                for hd in range(2):
                    z = PS[:, 2 * (hp % 2) + hd, :]
                    nl = sb_nl[hp % 2][:, hd, :]
                    for dst, lhs, rhs in ((z[:, 0:T], C("negtri"), nl[:, 0:T]), (z[:, P:T], C("negones"), nl[:, T:T + P]),
                                          (z[:, T:T + P], C("negtri"), nl[:, T:T + P]), (z[:, 0:P], ident, C("sb_mask")),
                                          (z[:, T:T + P], ident, C("sb_mask"))):
                        last = nc.tensor.matmul(dst, lhs, rhs, start=False, stop=True, skip_group_check=True)
                last.then_inc(cum_ready, 1)

            def outputs(hp):
                pe.wait_ge(w_done, hp + 1)
                if hp == 0:
                    pe.wait_ge(vt_done, 4)
                if hp >= 2:
                    pe.wait_ge(hid_done, G["v"].hid0 + hp - 1)
                for hd in range(2):
                    o = PS[HD * hd:HD * hd + HD, 6 + hp % 2, 0:T]
                    h = 2 * hp + hd
                    wt = sb_w[hp % 2][:, hd, :]
                    nc.tensor.matmul(o, v_tok[:, 0, HD * h:HD * h + HD], wt[:, 0:T], start=True, stop=False,
                                     skip_group_check=True)
                    last = nc.tensor.matmul(o[:, P:T], v_tok[:, 1, HD * h:HD * h + HD], wt[:, T:T + P], start=False,
                                            stop=True, skip_group_check=True)
                last.then_inc(o_ready, 1)

            for it in range(PAIRS + 2):
                if it < PAIRS:
                    scores(it)
                if 1 <= it <= PAIRS:
                    running_sums(it - 1)
                if it >= 2:
                    outputs(it - 2)

        def sb_scalar(act):
            nc.scalar.preload_act_table_set(LN_EXP)
            for i in range(4):
                act.wait_ge(vt_ready, i + 1)
                nc.scalar.activation(v_tok[:, i // 2, 512 * (i % 2):512 * (i % 2) + 512], PS[:, 4 + i, :],
                                     ACT.Copy).then_inc(vt_done, 1)
            for it in range(PAIRS + 1):
                if it < PAIRS:
                    a = sb_soft[it % 2]
                    act.wait_ge(z_ready, it + 1)
                    if it >= 2:
                        act.wait_ge(nl_done, it - 1)
                    nc.scalar.activation(a[:, :, :], z_banks(it)[:, :, 0:384], ACT.Abs).then_inc(act_step, 1)
                    a_count.one()
                    act.wait_ge(act_step, a_count.n)
                    nc.scalar.activation(a[:, :, :], a[:, :, :], ACT.Exp, scale=-1.0).then_inc(act_step, 1)
                    a_count.one()
                    act.wait_ge(act_step, a_count.n)
                    nc.scalar.activation(a[:, :, :], a[:, :, :], ACT.Ln, bias=1.0).then_inc(soft_done, 1)
                if it >= 1:
                    act.wait_ge(cum_ready, it)
                    if it >= 3:
                        act.wait_ge(o_ready, it - 2)
                    nc.scalar.activation(sb_w[(it - 1) % 2][:, :, :], z_banks(it - 1)[:, :, 0:384],
                                         ACT.Exp).then_inc(w_done, 1)

        def sb_vector(dve):
            keep = C("sb_keep").unsqueeze(1).to_broadcast([P, 2, P])
            for it in range(PAIRS + 2):
                if it < PAIRS:
                    nl = sb_nl[it % 2]
                    dve.wait_ge(soft_done, it + 1)
                    if it >= 2:
                        dve.wait_ge(cum_ready, it - 1)
                    nc.vector.scalar_tensor_tensor(out=nl[:, :, :], in0=z_banks(it)[:, :, 0:384], scalar=0.0,
                                                   in1=sb_soft[it % 2][:, :, :], op0=ALU.max, op1=ALU.add).then_inc(dve_step, 1)
                    v_count.one()
                    dve.wait_ge(dve_step, v_count.n)
                    nc.vector.tensor_tensor(nl[:, :, 0:P], nl[:, :, 0:P], keep, ALU.mult).then_inc(dve_step, 1)
                    v_count.one()
                    dve.wait_ge(dve_step, v_count.n)
                    nc.vector.tensor_tensor(nl[:, :, T:T + P], nl[:, :, T:T + P], keep, ALU.mult).then_inc(nl_done, 1)
                if it >= 2:
                    hp = it - 2
                    dve.wait_ge(o_ready, hp + 1)
                    o = PS[:, 6 + hp % 2, 0:T]
                    nc.vector.tensor_copy(hid_hi[:, hp, :], o).then_inc(sb_hi, 1)
                    dve.wait_ge(sb_hi, hp + 1)
                    nc.vector.tensor_tensor(hid_lo[:, hp, :], o, hid_hi[:, hp, :].bitcast(F32),
                                            ALU.subtract).then_inc(hid_done, 1)

        BQ = 16
        NB = SG // BQ
        x_chunk = sb("x_chunk", [SC, SL, D], "hl")
        y_chunk = sb("y_chunk", [SC, SL, D], "hl")
        toep = sb("toep", [P, SG, P], "hh")
        x_group = sb("x_group", [SC, SG, SL * SH], "hh")
        s_out = sb("s_out", [P, SG, SL + 1, SH], "wh")
        s_in = sb("s_in", [P, BQ, P], "wh", 36864)
        d_diag = sb("d_diag", [SH, SG, SH], "wh", 45056)
        b_rows = [sb(f"b_rows{i}", [SG, 2 * SP * SH], "wh", 8192 * i) for i in range(2)]
        c_rows = sb("c_rows", [P, 8, 4 * SP], "wh", 16384)
        a_rows = sb("a_rows", [SG, 4 * SP], "wh", 24576)
        tab_b = [sb(f"tab_b{i}", [P, SG, SH], "raw", 4096 * i) for i in range(2)]
        tab_c = [sb(f"tab_c{i}", [P, SG, SH], "raw", 8192 + 4096 * i) for i in range(2)]
        lag_b = [sb(f"lag_b{b}", [P, BQ, SL, SH], "hl", 8192 * b) if b else sb("lag_b0", [P, BQ, SL, SH], "raw", 16384)
                 for b in range(NB)]
        tmp_lag = sb("tmp_lag", [P, BQ, SL, SH], "hl")
        tmp_b = [sb(f"tmp_b{i}", [P, SG, SH], "raw", 16384 + 4096 * i) for i in range(2)]
        tmp = sb("tmp", [P, BQ * (SL + 1) * SH], "extra")
        kern = sb("kern", [P, BQ, P], "xh")
        terms = sb("terms", [P, SC, 2, 3, SG // 2], "hl")
        tb = sb("tb", [P, 24, SG], "xl")
        state = sb("state", [P, SG, SC], "xl")
        u_in = sb("u_in", [P, SG, SC], "xc")
        pow_re = sb("pow_re", [P, SL + 1, SG], "sq")
        pow_im = sb("pow_im", [P, SL + 1, SG], "sq", 2304)
        pow_is = sb("pow_is", [P, SL + 1, SG], "sq", 4608)
        rev_re = sb("rev_re", [P, SL, SG], "sq", 6912)
        rev_is = sb("rev_is", [P, SL, SG], "sq", 8960)
        run = sb("run", [P, SC + 1, 2, SG // 2], "extra")
        carry = sb("carry", [P, 2, 2, SG // 2], "misc", 512)
        sinks = sb("sinks", [P, 2 * AH], "misc", 2304)
        gate_bias = sb("gate_bias", [P, 2 * IN_IF], "misc", 2368)
        gelu = sb("gelu", [P, KT, T], "xc")
        w_if = [sb(f"w_if{l}", [P, KT, IN_IF], "misc", 2560 + 256 * l) for l in range(2)]
        ld_if = S("ld_if")
        ld_const, ld_vec, ld_x = S("ld_const"), S("ld_vec"), S("ld_x")
        ld_first, ld_a, ld_b, ld_c, ld_d = S("ld_first"), S("ld_a"), S("ld_b"), S("ld_c"), S("ld_d")
        tabb_done, lag_step, lag_last = S("tabb_done"), S("lag_step"), S("lag_last")
        N_VEC = 13
        vec_t, vec_done = S("vec_t"), S("vec_done")
        xt_ready, xt_done, u_ready, u_done5 = S("xt_ready"), S("xt_done"), S("u_ready"), S("s5_u_done")
        a_ready, b_ready, c_ready, a_read = S("a_ready"), S("b_ready"), S("c_ready"), S("a_read")
        dt_done, mag_done, sin_done, cos_done = S("dt_done"), S("mag_done"), S("sin_done"), S("cos_done")
        arg_mag, arg_sin, arg_cos = S("arg_mag"), S("arg_sin"), S("arg_cos")
        tabs_done, sout_done = S("tabs_done"), S("sout_done")
        e_t, e_done, ds_ready, k_ready, k_done, k_moved = (S("e_t"), S("e_done"), S("ds_ready"), S("k_ready"),
                                                           S("k_done"), S("k_moved"))
        toep_zero, din_act, din_dve, st_act, st_dve = (S("toep_zero"), S("din_act"), S("din_dve"), S("st_act"),
                                                       S("st_dve"))
        scan_p, scan_n = S("scan_p"), S("scan_n")
        y_ready, yt_ready, gelu_done = S("y_ready"), S("yt_ready"), S("gelu_done")
        y_act, y_dve = S("y_act"), S("y_dve")
        diag_done, grouped = S("diag_done"), S("grouped")

        lag_order = [NB - 1] + list(range(NB - 1))
        s5_jobs = [("inputs", NB - 1), ("inputs", 0)]
        for b in range(NB):
            s5_jobs.append(("kernels", b))
            if 1 <= b < NB - 1:
                s5_jobs.append(("inputs", b))

        def s5_loads(sp):
            sg = CONST["sgn"][0]
            sp.dma_start(const[:, 0:P], w["consts"][:, 0:P]).then_inc(ld_first, 16)
            sp.dma_start(const[:, sg:sg + 8], w["consts"][:, sg:sg + 8]).then_inc(ld_first, 16)
            for i, name in enumerate(("ssm_a_re", "ssm_a_re", "ssm_a_im", "ssm_a_im")):
                sp.dma_start(a_rows[:, SP * i:SP * i + SP], w[name][0]).then_inc(ld_a, 16)
            sp.dma_start(tb[:, 0, :], w["ssm_log_dt"][0].partition_broadcast(P)).then_inc(ld_a, 16)
            for i, name in enumerate(("ssm_c_re", "ssm_c_im", "ssm_c_im", "ssm_c_re")):
                sp.dma_start(c_rows[:, :, SP * i:SP * i + SP],
                             w[name][0].rearrange("(t g) h p -> (g h) t p", g=8)).then_inc(ld_c, 16)
            for i, pair in enumerate((("ssm_b_re", "ssm_b_im"), ("ssm_b_im", "ssm_b_re"))):
                for j, name in enumerate(pair):
                    sp.dma_start(b_rows[i][:, SP * SH * j:SP * SH * (j + 1)],
                                 w[name][0].rearrange("g p h -> g (p h)")).then_inc(ld_b, 16)
            sp.dma_start(x_chunk[:, :, :], w["x"][0].rearrange("(c t) d -> c t d", t=SL)).then_inc(ld_x, 16)
            sp.dma_start(d_diag[:, :, :].rearrange("h g k -> h (g k)"),
                         w["ssm_d"][0].partition_broadcast(SH)).then_inc(ld_d, 16)
            sp.dma_start(const[:, P:sg], w["consts"][:, P:sg]).then_inc(ld_const, 16)
            at = 0
            for name in ("ln_mix_g", "ln_mix_b", "ln_ffn_g", "ln_ffn_b", "norm_mix_2", "norm_ffn_2"):
                sp.dma_start(vec_rows[at:at + 16, :], w[name].rearrange("l (k p) -> (l k) p", p=P)).then_inc(ld_vec, 16)
                at += 16
            sp.dma_start(vec_rows[at:at + 8, :], w["m_head_norm_2"].rearrange("l (k p) -> (l k) p", p=P)).then_inc(ld_vec, 16)
            at += 8
            for name in ("att_q_norm_2", "att_k_norm_2"):
                for b in (0, HD):
                    sp.dma_start(vec_rows[at:at + 2, b:b + HD], w[name]).then_inc(ld_vec, 16)
                at += 2
            sp.dma_start(sinks[:, :], w["att_sinks_2"].rearrange("l h -> (l h)").partition_broadcast(P)).then_inc(ld_vec, 16)
            sp.dma_start(gate_bias[:, :], w["m_gate_bias_2"].rearrange("l h -> (l h)").partition_broadcast(P)).then_inc(ld_vec, 16)
            for l in range(2):
                sp.dma_start(w_if[l][:, :, :], w["w_in_2"][l].rearrange("(k p) n -> p k n", p=P)[
                    :, :, IN_QKVO:IN_QKVO + IN_IF]).then_inc(ld_if, 16)

        def s5_toeplitz(sp):
            sp.wait_ge(toep_zero, 1)
            for b in range(NB):
                sp.wait_ge(k_done, 4 * b + 4)
                for t in range(SL):
                    sp.dma_start(toep[SH * t:SH * t + SH, BQ * b:BQ * b + BQ, SH * t:P],
                                 kern[32 * b:32 * b + SH, :, 0:P - SH * t]).then_inc(k_moved, 16)

        def s5_tensor(pe):
            pe.wait_ge(ld_first, 32)
            pe.wait_ge(ld_a, 80)
            for i in range(2):
                last = nc.tensor.transpose(PS[:, 5, SG * i:SG * i + SG], a_rows[:, P * i:P * i + P], ident[0:SG, 0:SG])
            last.then_inc(a_ready, 1)
            pe.wait_ge(a_read, 2)
            pe.wait_ge(ld_c, 64)
            for i in range(2):
                for t in range(8):
                    last = nc.tensor.transpose(PS[:, 4 + 2 * i + t // 4, (t % 4) * P:(t % 4 + 1) * P],
                                               c_rows[:, t, P * i:P * i + P], ident)
            last.then_inc(c_ready, 1)
            pe.wait_ge(ld_b, 64)
            for i in range(2):
                rows = b_rows[i][:, :].rearrange("g (q h) -> g q h", h=SH)
                for h in range(SH):
                    last = nc.tensor.transpose(PS[:, 2 * i + h // 8, (h % 8) * SG:(h % 8 + 1) * SG], rows[:, :, h],
                                               ident[0:SG, 0:SG])
            last.then_inc(b_ready, 1)
            pe.wait_ge(ld_x, 16)
            pe.wait_ge(tabs_done, 2)
            for f in range(KT):
                for t in range(SL):
                    last = nc.tensor.transpose(PS[:, 4 + f // 2, (f % 2) * T + SC * t:(f % 2) * T + SC * t + SC],
                                               x_chunk[:, t, P * f:P * f + P], ident[0:SC, 0:SC])
                last.then_inc(xt_ready, 1)
            pe.wait_ge(grouped, 2)
            pe.wait_ge(xt_done, KT)
            for g in range(SG):
                last = nc.tensor.transpose(PS[:, 4 + g // 16, (g % 16) * SC:(g % 16 + 1) * SC],
                                           x_group[:, g, :], ident[0:SC, 0:SC])
                if g % 16 == 15:
                    last.then_inc(u_ready, 1)
            pe.wait_ge(ld_vec, 16 * N_VEC)
            pe.wait_ge(u_done5, 4)
            nc.tensor.transpose(PS[:, 4, 0:108], vec_rows[:, :], ident[0:108, 0:108]).then_inc(vec_t, 1)
            pe.wait_ge(vec_done, 1)

            def kernels(b):
                pe.wait_ge(sout_done, b + 1)
                pe.wait_ge(diag_done, 1)
                for q in range(4):
                    n = 4 * b + q
                    if n >= 2:
                        pe.wait_ge(k_done, n - 1)
                    for i in range(4):
                        g = BQ * b + 4 * q + i
                        nc.tensor.matmul(PS[0:SH, n % 2, P * i:P * i + P], tab_b[0][:, g, :],
                                         s_out[:, g, 0:SL, :].rearrange("p t h -> p (t h)"), start=i == 0, stop=False,
                                         skip_group_check=True)
                    lag0 = PS[0:SH, n % 2, :].rearrange("h (i c) -> h i c", i=4)[:, :, 0:SH]
                    nc.tensor.matmul(lag0, ident[0:SH, 0:SH], d_diag[:, 4 * n:4 * n + 4, :], start=False, stop=True,
                                     skip_group_check=True).then_inc(k_ready, 1)

            def inputs(at, b):
                if b < NB - 1:
                    pe.wait_ge(lag_step, 3 * b + 3)
                else:
                    pe.wait_ge(lag_last, 1)
                for q in range(4):
                    n = 4 * at + q
                    if n >= 2:
                        pe.wait_ge(e_done, n - 1)
                    for i in range(4):
                        last = nc.tensor.transpose(PS[:, 2 + n % 2, P * i:P * i + P],
                                                   lag_b[b][:, 4 * q + i, :, :].rearrange("p t h -> p (t h)"), ident)
                    last.then_inc(e_t, 1)
                for q in range(4):
                    pe.wait_ge(e_done, 4 * at + q + 1)
                    for i in range(4):
                        last = nc.tensor.matmul(PS[:, 4 + b, (4 * q + i) * SC:(4 * q + i + 1) * SC], s_in[:, 4 * q + i, :],
                                                u_in[:, BQ * b + 4 * q + i, :], start=True, stop=True, skip_group_check=True)
                    last.then_inc(ds_ready, 1)

            for job, b in s5_jobs:
                if job == "inputs":
                    inputs(lag_order.index(b), b)
                else:
                    kernels(b)
            pe.wait_ge(k_moved, 16 * SL * NB)
            pe.wait_ge(k_done, 16)
            pe.wait_ge(e_done, 16)
            for q in range(16):
                for i in range(4):
                    nc.tensor.matmul(y_bank(q)[:, P * i:P * i + P], u_in[:, 4 * q + i, :], toep[:, 4 * q + i, :],
                                     start=i == 0, stop=False, skip_group_check=True)
            pe.wait_ge(st_act, 2)
            pe.wait_ge(st_dve, 2)

            def y_features(f):
                pe.wait_ge(y_act, f + 1)
                pe.wait_ge(y_dve, f + 1)
                if f == 0:
                    pe.wait_ge(din_act, 1)
                    pe.wait_ge(din_dve, 2)
                for t in range(SL):
                    last = nc.tensor.transpose(PS[:, 4 + f // 2, (f % 2) * T + SC * t:(f % 2) * T + SC * t + SC],
                                               y_chunk[:, t, P * f:P * f + P], ident[0:SC, 0:SC])
                last.then_inc(yt_ready, 1)

            for q in range(16):
                for i in range(4):
                    g = 4 * q + i
                    last = nc.tensor.matmul(y_bank(q)[:, P * i:P * i + P], state[:, g, :],
                                            s_out[:, g, 1:SL + 1, :].rearrange("p t h -> p (t h)"), start=False, stop=True,
                                            skip_group_check=True)
                last.then_inc(y_ready, 1)
                if q % 2 and q >= 3:
                    y_features(q // 2 - 1)
            y_features(KT - 1)
            pe.wait_ge(ld_const, 16)

        def y_bank(q):
            return PS[SC * (q // 4):SC * (q // 4) + SC, q % 4, :]

        def by_token(f):
            return PS[:, 4 + f // 2, (f % 2) * T:(f % 2 + 1) * T].rearrange("p (t c) -> p c t", t=SL)

        def s5_scalar(act):
            act.wait_ge(ld_a, 80)
            act.wait_ge(ld_first, 32)
            nc.scalar.activation(tb[:, 1, :], tb[:, 0, :], ACT.Exp).then_inc(dt_done, 1)
            act.wait_ge(arg_mag, 1)
            nc.scalar.activation(tb[:, 8, :], tb[:, 4, :], ACT.Exp).then_inc(mag_done, 1)
            nc.scalar.preload_act_table(ACT.Sin)
            act.wait_ge(arg_sin, 1)
            nc.scalar.activation(tb[:, 9, :], tb[:, 7, :], ACT.Sin).then_inc(sin_done, 1)
            act.wait_ge(arg_cos, 1)
            nc.scalar.activation(tb[:, 10, :], tb[:, 11, :], ACT.Sin).then_inc(cos_done, 1)
            nc.scalar.preload_act_table(ACT.Gelu_apprx_tanh)
            sgn = const[:, CONST["sgn"][0]:CONST["sgn"][0] + 2]
            act.wait_ge(c_ready, 1)
            nc.scalar.activation(tab_c[0][:, :, :].rearrange("p g h -> p (g h)").rearrange("p (a b) -> p a b", a=2),
                                 PS[:, 4:6, :], ACT.Identity, scale=sgn[:, 1:2]).then_inc(tabs_done, 1)
            nc.scalar.activation(tab_c[1][:, :, :].rearrange("p g h -> p (g h)").rearrange("p (a b) -> p a b", a=2),
                                 PS[:, 6:8, :], ACT.Copy, scale=-1.0).then_inc(tabs_done, 1)
            act.wait_ge(ld_x, 16)
            for i in range(2):
                nc.scalar.activation(x_group[:, 32 * i:32 * i + 32, :].rearrange("c g (t h) -> c t g h", h=SH),
                                     x_chunk[:, :, 512 * i:512 * i + 512].rearrange("c t (g h) -> c t g h", h=SH),
                                     ACT.Copy).then_inc(grouped, 1)
            for f in range(KT):
                act.wait_ge(xt_ready, f // 2 * 2 + 2)
                nc.scalar.activation(res[:, f, :].rearrange("p (c t) -> p c t", t=SL), by_token(f), ACT.Copy).then_inc(xt_done, 1)
            for i in range(4):
                act.wait_ge(u_ready, i + 1)
                nc.scalar.activation(u_in[:, 16 * i:16 * i + 16, :].rearrange("p g c -> p (g c)"), PS[:, 4 + i, :],
                                     ACT.Copy).then_inc(u_done5, 1)
            act.wait_ge(vec_t, 1)
            nc.scalar.activation(vec[:, :], PS[:, 4, 0:108], ACT.Copy).then_inc(vec_done, 1)
            zero = const[:, CONST["sgn"][0] + 4:CONST["sgn"][0] + 5].unsqueeze(2).to_broadcast([P, SG, P])
            nc.scalar.activation(toep[:, :, :], zero, ACT.Copy).then_inc(toep_zero, 1)
            for job, b in s5_jobs:
                at = lag_order.index(b)
                for q in range(4):
                    if job == "kernels":
                        n = 4 * b + q
                        act.wait_ge(k_ready, n + 1)
                        nc.scalar.activation(kern[32 * b:32 * b + SH, 4 * q:4 * q + 4, :].rearrange("h g c -> h (g c)"),
                                             PS[0:SH, n % 2, :], ACT.Copy).then_inc(k_done, 1)
                    else:
                        n = 4 * at + q
                        act.wait_ge(e_t, n + 1)
                        if at >= 1:
                            act.wait_ge(ds_ready, n - 3)
                        nc.scalar.activation(s_in[:, 4 * q:4 * q + 4, :].rearrange("p g c -> p (g c)"), PS[:, 2 + n % 2, :],
                                             ACT.Copy).then_inc(e_done, 1)
            act.wait_ge(ds_ready, 16)
            ds = PS[:, 4:8, :].rearrange("p b (g two c) -> p b g two c", two=2, c=SC)
            dv = terms[:, :, :, 2, :].rearrange("p c r (b g) -> p r b g c", b=4)
            for b in range(2):
                for two in range(2):
                    for ri in range(2):
                        ins = nc.scalar.activation(dv[SP * two:SP * two + SP, ri, b], ds[SP * ri:SP * ri + SP, b, :, two, :],
                                                   ACT.Copy)
            ins.then_inc(din_act, 1)
            act.wait_ge(scan_n, SC - 1)
            st = state[:, :, :].rearrange("p (g two) c -> p two g c", two=2)
            rn = run[:, 0:SC, :, :].rearrange("p c r g -> p r g c")
            nc.scalar.activation(st[0:SP, 0], rn[0:SP, 0], ACT.Copy).then_inc(st_act, 1)
            nc.scalar.activation(st[SP:P, 1], rn[SP:P, 1], ACT.Copy).then_inc(st_act, 1)

            def mixer_out(f):
                act.wait_ge(yt_ready, f // 2 * 2 + 2)
                nc.scalar.activation(gelu[:, f, :].rearrange("p (c t) -> p c t", t=SL), by_token(f),
                                     ACT.Gelu_apprx_tanh).then_inc(gelu_done, 1)
                act.wait_ge(gelu_done, f + 1)
                if f == 0:
                    act.wait_ge(k_moved, 16 * SL * NB)
                nc.scalar.activation(x_hi[:, f, :], gelu[:, f, :], ACT.Copy).then_inc(xh_done, 1)

            for f in range(KT):
                act.wait_ge(y_ready, 2 * f + 1)
                nc.scalar.activation(*y_places(2 * f), ACT.Copy).then_inc(y_act, 1)
                if f >= 2:
                    mixer_out(f - 2)
            act.wait_ge(y_ready, 16)
            split_hi(act, 0, 0, 0)
            for f in range(KT - 2, KT):
                mixer_out(f)
            for j in range(1, RING):
                split_hi(act, 0, j, 0)

        def y_places(q):
            src = y_bank(q).rearrange("c (g t h) -> c g t h", g=4, h=SH)
            dst = y_chunk[:, :, 4 * q * SH:4 * (q + 1) * SH].rearrange("c t (g h) -> c g t h", h=SH)
            return dst, src

        def lag_tables(b, sh):
            gs = slice(BQ * b, BQ * b + BQ)
            return (tab_b[0][:, gs, :].unsqueeze(2).to_broadcast(sh), tab_b[1][:, gs, :].unsqueeze(2).to_broadcast(sh),
                    rev_re[:, :, gs].rearrange("p t g -> p g t").unsqueeze(3).to_broadcast(sh),
                    rev_is[:, :, gs].rearrange("p t g -> p g t").unsqueeze(3).to_broadcast(sh))

        def s5_pool(pool):
            Q = nc.gpsimd
            pool.wait_ge(ld_d, 16)
            pool.wait_ge(ld_first, 32)
            Q.tensor_tensor(d_diag[:, :, :], d_diag[:, :, :], ident[0:SH, 0:SH].unsqueeze(1).to_broadcast([SH, SG, SH]),
                            ALU.mult).then_inc(diag_done, 1)
            pool.wait_ge(u_ready, 4)
            pool.wait_ge(tabb_done, 2)
            for b in range(NB - 1):
                sh = [P, BQ, SL, SH]
                b_re, b_is, lag_re, lag_im = lag_tables(b, sh)
                if b >= 1:
                    pool.wait_ge(lag_step, 3 * b)
                Q.tensor_tensor(lag_b[b][:, :, :, :], b_re, lag_re, ALU.mult).then_inc(lag_step, 1)
                Q.tensor_tensor(tmp_lag[:, :, :, :], b_is, lag_im, ALU.mult).then_inc(lag_step, 1)
                pool.wait_ge(lag_step, 3 * b + 2)
                Q.tensor_tensor(lag_b[b][:, :, :, :], lag_b[b][:, :, :, :], tmp_lag[:, :, :, :], ALU.add).then_inc(lag_step, 1)

        def s5_vector(dve):
            V = nc.vector
            lr, li, dt, xm, th, kk, r = (tb[:, i, :] for i in (2, 3, 1, 4, 5, 6, 7))
            mag, sn, cs, ca, ar = (tb[:, i, :] for i in (8, 9, 10, 11, 12))


            dve.wait_ge(ld_first, 32)
            dve.wait_ge(a_ready, 1)
            V.tensor_scalar(lr, PS[:, 5, 0:SG], -1e-4, None, ALU.min).then_inc(a_read, 1)
            V.tensor_copy(li, PS[:, 5, SG:2 * SG]).then_inc(a_read, 1)
            dve.wait_ge(a_read, 2)
            dve.wait_ge(dt_done, 1)
            V.tensor_tensor(xm, lr, dt, ALU.mult).then_inc(arg_mag, 1)
            V.tensor_tensor(th, li, dt, ALU.mult).then_inc(dve_step, 1)
            dve.wait_ge(dve_step, v_count.one())
            magic = 1.5 * 2.0 ** 23
            two_pi_hi = float(np.float32(6.28125))
            two_pi_lo = float(2 * np.pi - 6.28125)
            V.tensor_scalar(kk, th, float(1 / (2 * np.pi)), magic, ALU.mult, ALU.add).then_inc(dve_step, 1)
            dve.wait_ge(dve_step, v_count.one())
            V.tensor_scalar(kk, kk, -magic, None, ALU.add).then_inc(dve_step, 1)
            dve.wait_ge(dve_step, v_count.one())
            V.scalar_tensor_tensor(out=r, in0=kk, scalar=-two_pi_hi, in1=th, op0=ALU.mult, op1=ALU.add).then_inc(dve_step, 1)
            dve.wait_ge(dve_step, v_count.one())
            V.scalar_tensor_tensor(out=r, in0=kk, scalar=-two_pi_lo, in1=r, op0=ALU.mult, op1=ALU.add).then_inc(dve_step, 1)
            dve.wait_ge(dve_step, v_count.one())
            pi = float(np.nextafter(np.float32(np.pi), np.float32(0)))
            V.tensor_scalar(r, r, pi, -pi, ALU.min, ALU.max).then_inc(arg_sin, 1)
            dve.wait_ge(arg_sin, 1)
            V.scalar_tensor_tensor(out=ar, in0=r, scalar=-1.0, in1=r, op0=ALU.mult, op1=ALU.max).then_inc(dve_step, 1)
            dve.wait_ge(dve_step, v_count.one())
            V.tensor_scalar(ca, ar, -1.0, float(np.pi / 2), ALU.mult, ALU.add).then_inc(arg_cos, 1)
            dve.wait_ge(mag_done, 1)
            dve.wait_ge(sin_done, 1)
            dve.wait_ge(cos_done, 1)
            V.memset(pow_re[:, 0, :], 1.0)
            V.memset(pow_im[:, 0, :], 0.0)
            V.tensor_tensor(pow_re[:, 1, :], mag, cs, ALU.mult).then_inc(dve_step, 1)
            dve.wait_ge(dve_step, v_count.one())
            V.tensor_tensor(pow_im[:, 1, :], mag, sn, ALU.mult).then_inc(dve_step, 1)
            dve.wait_ge(dve_step, v_count.one())
            nr, den, t0, t1, cr, ci = (tb[:, i, :] for i in (13, 14, 15, 16, 17, 18))
            cis = tb[:, 19, :]
            lb_im = pow_im[:, 1, :]
            V.tensor_scalar(nr, pow_re[:, 1, :], -1.0, None, ALU.add).then_inc(dve_step, 1)
            dve.wait_ge(dve_step, v_count.one())
            V.tensor_tensor(den, lr, lr, ALU.mult).then_inc(dve_step, 1)
            dve.wait_ge(dve_step, v_count.one())
            V.tensor_tensor(t0, li, li, ALU.mult).then_inc(dve_step, 1)
            dve.wait_ge(dve_step, v_count.one())
            V.tensor_tensor(den, den, t0, ALU.add).then_inc(dve_step, 1)
            dve.wait_ge(dve_step, v_count.one())
            V.reciprocal(den, den).then_inc(dve_step, 1)
            dve.wait_ge(dve_step, v_count.one())
            V.tensor_tensor(t0, nr, lr, ALU.mult).then_inc(dve_step, 1)
            dve.wait_ge(dve_step, v_count.one())
            V.tensor_tensor(t1, lb_im, li, ALU.mult).then_inc(dve_step, 1)
            dve.wait_ge(dve_step, v_count.one())
            V.tensor_tensor(t0, t0, t1, ALU.add).then_inc(dve_step, 1)
            dve.wait_ge(dve_step, v_count.one())
            V.tensor_tensor(cr, t0, den, ALU.mult).then_inc(dve_step, 1)
            dve.wait_ge(dve_step, v_count.one())
            V.tensor_tensor(t0, lb_im, lr, ALU.mult).then_inc(dve_step, 1)
            dve.wait_ge(dve_step, v_count.one())
            V.tensor_tensor(t1, nr, li, ALU.mult).then_inc(dve_step, 1)
            dve.wait_ge(dve_step, v_count.one())
            V.tensor_tensor(t0, t0, t1, ALU.subtract).then_inc(dve_step, 1)
            dve.wait_ge(dve_step, v_count.one())
            V.tensor_tensor(ci, t0, den, ALU.mult).then_inc(dve_step, 1)
            dve.wait_ge(dve_step, v_count.one())
            sgn = CONST["sgn"][0]
            minus_re = const[:, sgn:sgn + 1]
            V.tensor_scalar(cis, ci, minus_re, None, ALU.mult).then_inc(dve_step, 1)
            dve.wait_ge(dve_step, v_count.one())
            for lo, n in ((1, 1), (1, 2), (1, 4)):
                top = lo + n - 1
                src = slice(1, n + 1)
                dst = slice(top + 1, top + n + 1)
                br = pow_re[:, top:top + 1, :].to_broadcast([P, n, SG])
                bi = pow_im[:, top:top + 1, :].to_broadcast([P, n, SG])
                ta, tb2 = tmp[:, 0:n * SG].rearrange("p (n g) -> p n g", n=n), tmp[:, 512:512 + n * SG].rearrange(
                    "p (n g) -> p n g", n=n)
                V.tensor_tensor(ta, pow_re[:, src, :], br, ALU.mult).then_inc(dve_step, 1)
                dve.wait_ge(dve_step, v_count.one())
                V.tensor_tensor(tb2, pow_im[:, src, :], bi, ALU.mult).then_inc(dve_step, 1)
                dve.wait_ge(dve_step, v_count.one())
                V.tensor_tensor(pow_re[:, dst, :], ta, tb2, ALU.subtract).then_inc(dve_step, 1)
                dve.wait_ge(dve_step, v_count.one())
                V.tensor_tensor(ta, pow_re[:, src, :], bi, ALU.mult).then_inc(dve_step, 1)
                dve.wait_ge(dve_step, v_count.one())
                V.tensor_tensor(tb2, pow_im[:, src, :], br, ALU.mult).then_inc(dve_step, 1)
                dve.wait_ge(dve_step, v_count.one())
                V.tensor_tensor(pow_im[:, dst, :], ta, tb2, ALU.add).then_inc(dve_step, 1)
                dve.wait_ge(dve_step, v_count.one())
            V.tensor_scalar(pow_is[:, :, :], pow_im[:, :, :], minus_re, None, ALU.mult).then_inc(dve_step, 1)
            dve.wait_ge(dve_step, v_count.one())
            for j in range(SL):
                V.tensor_copy(rev_re[:, j, :], pow_re[:, SL - 1 - j, :])
                V.tensor_copy(rev_is[:, j, :], pow_is[:, SL - 1 - j, :]).then_inc(dve_step, 1)
                dve.wait_ge(dve_step, v_count.one())
            for half in range(2):
                ps = slice(SP * half, SP * half + SP)
                lre = pow_re[ps, SL, :].rearrange("p (g two) -> p two g", two=2)[:, half, :]
                lim = pow_im[ps, SL, :].rearrange("p (g two) -> p two g", two=2)[:, half, :]
                V.tensor_copy(carry[ps, 0, 0, :], lre)
                V.tensor_copy(carry[ps, 1, 1, :], lre)
                V.tensor_copy(carry[ps, 1, 0, :], lim)
                V.tensor_scalar(carry[ps, 0, 1, :], lim, -1.0, None, ALU.mult).then_inc(dve_step, 1)
                dve.wait_ge(dve_step, v_count.one())
            dve.wait_ge(b_ready, 1)
            pb = [PS[:, 2 * i:2 * i + 2, :].rearrange("p a (h g) -> p (a h) g", g=SG).rearrange("p h g -> p g h")
                  for i in range(2)]
            crb = cr.unsqueeze(2).to_broadcast([P, SG, SH])
            cib = cis.unsqueeze(2).to_broadcast([P, SG, SH])
            V.tensor_tensor(tmp_b[0][:, :, :], pb[0], crb, ALU.mult).then_inc(dve_step, 1)
            dve.wait_ge(dve_step, v_count.one())
            V.tensor_tensor(tmp_b[1][:, :, :], pb[1], cib, ALU.mult).then_inc(dve_step, 1)
            dve.wait_ge(dve_step, v_count.one())
            V.tensor_tensor(tab_b[0][:, :, :], tmp_b[0][:, :, :], tmp_b[1][:, :, :], ALU.add).then_inc(tabb_done, 1)
            dve.wait_ge(tabb_done, 1)
            V.tensor_tensor(tmp_b[0][:, :, :], pb[1], crb, ALU.mult).then_inc(dve_step, 1)
            dve.wait_ge(dve_step, v_count.one())
            V.tensor_tensor(tmp_b[1][:, :, :], pb[0], cib, ALU.mult).then_inc(dve_step, 1)
            dve.wait_ge(dve_step, v_count.one())
            V.tensor_tensor(tab_b[1][:, :, :], tmp_b[0][:, :, :], tmp_b[1][:, :, :], ALU.subtract).then_inc(tabb_done, 1)
            dve.wait_ge(tabb_done, 2)
            sh = [P, BQ, SL, SH]
            b_re, b_is, lag_re, lag_im = lag_tables(NB - 1, sh)
            tv = tmp[:, 0:BQ * SL * SH].rearrange("p (g t h) -> p g t h", g=BQ, h=SH)
            last_lag = lag_b[NB - 1][:, :, :, :]
            dve.wait_ge(u_ready, 4)
            V.tensor_tensor(last_lag, b_re, lag_re, ALU.mult).then_inc(dve_step, 1)
            v_count.one()
            V.tensor_tensor(tv, b_is, lag_im, ALU.mult).then_inc(dve_step, 1)
            dve.wait_ge(dve_step, v_count.one())
            V.tensor_tensor(last_lag, last_lag, tv, ALU.add).then_inc(lag_last, 1)
            dve.wait_ge(lag_last, 1)
            dve.wait_ge(tabs_done, 2)
            tv = tmp[:, :].rearrange("p (g t h) -> p g t h", g=BQ, h=SH)
            for b in range(NB):
                gs = slice(BQ * b, BQ * b + BQ)
                sh = [P, BQ, SL + 1, SH]
                o_re = pow_re[:, :, gs].rearrange("p t g -> p g t").unsqueeze(3).to_broadcast(sh)
                o_im = pow_im[:, :, gs].rearrange("p t g -> p g t").unsqueeze(3).to_broadcast(sh)
                so = s_out[:, gs, :, :]
                V.tensor_tensor(so, tab_c[0][:, gs, :].unsqueeze(2).to_broadcast(sh), o_re, ALU.mult).then_inc(dve_step, 1)
                v_count.one()
                V.tensor_tensor(tv, tab_c[1][:, gs, :].unsqueeze(2).to_broadcast(sh), o_im, ALU.mult).then_inc(dve_step, 1)
                dve.wait_ge(dve_step, v_count.one())
                V.tensor_tensor(so, so, tv, ALU.add).then_inc(sout_done, 1)
                dve.wait_ge(sout_done, b + 1)
            dve.wait_ge(ds_ready, 16)
            ds = PS[:, 4:8, :].rearrange("p b (g two c) -> p b g two c", two=2, c=SC)
            dv = terms[:, :, :, 2, :].rearrange("p c r (b g) -> p r b g c", b=4)
            for b in range(2, 4):
                for two in range(2):
                    for ri in range(2):
                        ins = V.tensor_copy(dv[SP * two:SP * two + SP, ri, b], ds[SP * ri:SP * ri + SP, b, :, two, :])
            ins.then_inc(din_dve, 1)
            V.memset(run[:, 0, :, :], 0.0).then_inc(din_dve, 1)
            dve.wait_ge(din_dve, 2)
            dve.wait_ge(din_act, 1)
            def advance(c):
                now = run[:, bass.ds(c, 1), :, :].to_broadcast([P, 2, 2, SG // 2])
                step = terms[:, bass.ds(c, 1), :, :, :].rearrange("p a r k g -> p (a r) k g")
                V.tensor_tensor(step[:, :, 0:2, :], now, carry[:, :, :, :], ALU.mult).then_inc(scan_p, 1)
                dve.wait_ge(scan_p, c + 1)
                V.tensor_reduce(run[:, bass.ds(c + 1, 1), :, :].rearrange("p a r g -> p (a r) g"),
                                step.rearrange("p r k g -> p r g k"), AX, ALU.add).then_inc(scan_n, 1)
                dve.wait_ge(scan_n, c + 1)

            steps = 8
            for c in range(steps - 1):
                advance(c)
            with dve.Fori(0, SC // steps - 1) as turn:
                for i in range(steps):
                    advance(turn * steps + (steps - 1 + i))
            st = state[:, :, :].rearrange("p (g two) c -> p two g c", two=2)
            rn = run[:, 0:SC, :, :].rearrange("p c r g -> p r g c")
            V.tensor_copy(st[SP:P, 0], rn[0:SP, 1]).then_inc(st_dve, 1)
            V.tensor_copy(st[0:SP, 1], rn[SP:P, 0]).then_inc(st_dve, 1)
            for q in range(1, 16, 2):
                dve.wait_ge(y_ready, q + 1)
                V.tensor_copy(*y_places(q)).then_inc(y_dve, 1)
            split_lo(dve, 0, 0, 0, 0, lo_dve)
            dve.wait_ge(y_ready, 16)
            for f in range(KT):
                dve.wait_ge(xh_done, f + 1)
                V.tensor_tensor(x_lo[:, f, :], gelu[:, f, :], x_hi[:, f, :].bitcast(F32), ALU.subtract).then_inc(xl_done, 1)
            for j in range(1, RING):
                split_lo(dve, 0, j, j, 0, lo_dve)

        ztile = sb("ztile", [P, 14, T], "hl", 16 * 4 * T)
        sig_g = sb("sig_g", [P, 16, T], "hh", 16 * 4 * T)
        sig_o = sb("sig_o", [P, MH, T], "extra", 4096)
        vm_tok = sb("vm_tok", [P, 2, 512], "extra", 0)
        hm_raw = sb("hm_raw", [P, 2, T], "extra", 8192)
        qk_rot = sb("qk_rot", [P, 5, T], "xc")
        k_dup = sb("k_dup", [P, 2, T], "xc", 5120)
        va_tok = sb("va_tok", [P, 2, P], "xc", 7168)
        qk_buf = sb("qk_buf", [P, 5, T], "sg")
        a_prob = [sb(f"a_prob{i}", [P, 2, 384], "sg", 3072 * i) for i in range(2)]
        a_probT = sb("a_probT", [P, 2, 384], "sq")
        m_exp = [sb(f"m_exp{i}", [P, 384], "sg", 1536 * i) for i in range(2)]
        m_w = [sb(f"m_w{i}", [P, 384], "sg", 3072 + 1536 * i) for i in range(2)]
        m_lim = [sb(f"m_lim{i}", [P, T], "zt", 1024 * i) for i in range(2)]
        m_den, m_sq, m_rs, m_out = (sb(n, [P, T], "sq", 1024 * i) for i, n in enumerate(("m_den", "m_sq", "m_rs", "m_out")))
        row_a = [sb(f"row_a{i}", [MH, P + T], "hh", 8192 + 1536 * i) for i in range(2)]
        row_e = sb("row_e", [MH, T], "hh", 8192 + 3072)
        gate_if = sb("gate_if", [P, 2, IN_IF], "hh", 8192 + 4096)
        nlf = sb("nlf", [P, 2, MH], "hh", 8192 + 4160)
        nlf_t = sb("nlf_t", [P, 2, MH], "hh", 8192 + 4192)
        a_col = sb("a_col", [P, 2, MH], "hh", 8192 + 4224)
        mx, neg_m, sink_e, p_sum, p_inv = (sb(n, [P, 4, 2, 2], "hh", 8192 + 4288 + 64 * i) for i, n in enumerate(
            ("mx", "neg_m", "sink_e", "p_sum", "p_inv")))
        q_gain = sb("q_gain", [P, 2], "misc", 2432)
        gain_done = S("gain_done")
        if_ready, vtm_ready, va_done = S("if_ready"), S("vtm_ready"), S("va_done")
        qsq_done, qss_ready, qrs_done, qn_done, rot_ready, qr_done = (S("qsq_done"), S("qss_ready"), S("qrs_done"),
                                                                      S("qn_done"), S("rot_ready"), S("qr_done"))
        gi_done, nlf_done, rows_ready, rows_done, acol_done = (S("gi_done"), S("nlf_done"), S("rows_ready"),
                                                               S("rows_done"), S("acol_done"))
        s_ready, mx_done, p_done, pn_done, pt_ready, pt_done, ao_ready, ao_hi = (
            S("s_ready"), S("mx_done"), S("p_done"), S("pn_done"), S("pt_ready"), S("pt_done"), S("ao_ready"), S("ao_hi"))
        d_ready, x_done, w_ready, nd_ready, hm_done, hsq_done, hss_ready, hrs_done, hm_hi = (
            S("d_ready"), S("x_done"), S("w_ready"), S("nd_ready"), S("hm_done"), S("hsq_done"), S("hss_ready"),
            S("hrs_done"), S("hm_hi"))
        AP_ = AH // 2

        def proj(g, idx):
            if g.name == "q":
                t = qkv[:, bass.ds(idx * 2, 2), :]
            elif g.name == "k":
                t = qkv[:, bass.ds(idx * 2 + 8, 2), :]
            elif g.name == "v":
                t = v_feat[:, bass.ds(idx * 2, 2), :]
            else:
                t = ztile[:, bass.ds(idx * 2, 2), :]
            return t.rearrange("p a t -> p (a t)")

        def hyb_tensor(pe, l):
            g, mix = G[f"gates{l}"], G[f"mix{l}"]
            hid0 = g.hid0
            MMr = dict(skip_group_check=True)
            pe.wait_ge(act_done, g.act0)
            if l == 0:
                pe.wait_ge(ld_if, 32)
            for t in range(2):
                for kt in range(KT):
                    last = nc.tensor.matmul(PS[:, 7, IN_IF * t:IN_IF * (t + 1)], xn[:, kt, P * t:P * t + P],
                                            w_if[l][:, kt, :], start=kt == 0, stop=kt == KT - 1, **MMr)
            last.then_inc(if_ready, 1)
            for t in range(2):
                nc.tensor.transpose(PS[:, 1, P * t:P * t + P], ztile[:, 5, P * t:P * t + P], ident)
                for h in range(MH):
                    last = nc.tensor.transpose(PS[:, 2 + t, P * h:P * h + P], ztile[:, 10 + h, P * t:P * t + P], ident)
            last.then_inc(vtm_ready, 1)
            pe.wait_ge(qsq_done, l + 1)
            flat = qk_buf[:, :, :].rearrange("p a t -> p (a t)")
            zflat = ztile[:, 0:5, :].rearrange("p a t -> p (a t)")
            for b, n in ((0, 512), (1, 512), (2, T)):
                last = nc.tensor.matmul(PS[:, 4 + b, 0:n], C("mean_h"), flat[:, 512 * b:512 * b + n], start=True, stop=True)
            last.then_inc(qss_ready, 1)
            gemm_tensor(pe, g, 0)
            pe.wait_ge(qn_done, 2 * l + 2)
            for b, n in ((0, 512), (1, 512), (2, T)):
                last = nc.tensor.matmul(PS[:, 4 + b, 0:n], C("rot"), zflat[:, 512 * b:512 * b + n], start=True, stop=True)
            last.then_inc(rot_ready, 1)
            pe.wait_ge(nlf_done, l + 1)
            pe.wait_ge(va_done, 3 * l + 3)
            tri = const[:, CONST["tri"][0]:CONST["tri"][0] + T]
            nf, ar = PS[0:MH, 2, 0:T], PS[0:MH, 2, T:2 * T]
            for row, with_i in ((nf, False), (ar, True)):
                nc.tensor.matmul(row, nlf[:, 0, :], tri, start=True, stop=False, **MMr)
                last = nc.tensor.matmul(row[:, P:T], nlf[:, 1, :], C("tri"), start=False, stop=not with_i, **MMr)
                if with_i:
                    for t in range(2):
                        last = nc.tensor.matmul(row[:, P * t:P * t + P], gate_if[:, t, 0:MH], ident, start=False,
                                                stop=True, **MMr)
            ac = PS[:, 7, 2 * IN_IF:2 * IN_IF + 2 * MH]
            nc.tensor.matmul(ac[:, 0:MH], C("tri"), nlf[:, 0, :], start=True, stop=False, **MMr)
            nc.tensor.matmul(ac[:, 0:MH], ident, gate_if[:, 0, 0:MH], start=False, stop=True, **MMr)
            nc.tensor.matmul(ac[:, MH:2 * MH], C("ones"), nlf[:, 0, :], start=False, stop=False, **MMr)
            nc.tensor.matmul(ac[:, MH:2 * MH], C("tri"), nlf[:, 1, :], start=False, stop=False, **MMr)
            last = nc.tensor.matmul(ac[:, MH:2 * MH], ident, gate_if[:, 1, 0:MH], start=False, stop=True, **MMr)
            last.then_inc(rows_ready, 1)

            def scores(p):
                for hd in range(2):
                    h = 2 * p + hd
                    b = HD * hd
                    s = PS[:, 4 + 2 * (p % 2) + hd, :]
                    q, k = qk_rot[b:b + HD, p, :], k_dup[b:b + HD, h // (AH // AKV), :]
                    nc.tensor.matmul(s[:, 0:P], q[:, 0:P], k[:, 0:P], start=True, stop=False, **MMr)
                    nc.tensor.matmul(s[:, P:384], q[:, P:T], k, start=False, stop=False, **MMr)
                    nc.tensor.matmul(s[:, 0:P], ident, C("win_diag"), start=False, stop=True, **MMr)
                    a = CONST["win_prev"][0]
                    last = nc.tensor.matmul(s[:, P:384], ident, const[:, a:a + T], start=False, stop=True, **MMr)
                last.then_inc(s_ready, 1)

            def transposed(p):
                pe.wait_ge(pn_done, AP_ * l + p + 1)
                if p >= 1:
                    pe.wait_ge(pt_done, AP_ * l + p)
                for hd in range(2):
                    for c in range(3):
                        last = nc.tensor.transpose(PS[:, 2 + hd, P * c:P * c + P], a_prob[p % 2][:, hd, P * c:P * c + P], ident)
                last.then_inc(pt_ready, 1)

            def outputs(p):
                pe.wait_ge(pt_done, AP_ * l + p + 1)
                if p >= 1:
                    pe.wait_ge(hid_done, hid0 + p)
                for hd in range(2):
                    kv = (2 * p + hd) // (AH // AKV)
                    o = PS[HD * hd:HD * hd + HD, 1, 0:T]
                    v = [va_tok[:, t, HD * kv:HD * kv + HD] for t in range(2)]
                    pt = a_probT[:, hd, :]
                    nc.tensor.matmul(o[:, 0:P], v[0], pt[:, 0:P], start=True, stop=True, **MMr)
                    nc.tensor.matmul(o[:, P:T], v[0], pt[:, P:T], start=False, stop=False, **MMr)
                    last = nc.tensor.matmul(o[:, P:T], v[1], pt[:, T:384], start=False, stop=True, **MMr)
                last.then_inc(ao_ready, 1)

            gemm_tensor(pe, g, 1)
            pe.wait_ge(qr_done, l + 1)
            pe.wait_ge(acol_done, l + 1)
            pe.wait_ge(va_done, 3 * l + 3)
            for it in range(AP_ + 2):
                if it < AP_:
                    if it >= 2:
                        pe.wait_ge(p_done, AP_ * l + it - 1)
                    scores(it)
                if 1 <= it <= AP_:
                    gemm_tensor(pe, g, it + 1)
                if 1 <= it <= AP_:
                    transposed(it - 1)
                if it >= 2:
                    outputs(it - 2)

            pe.wait_ge(rows_done, l + 1)

            def decays(h):
                if h >= 2:
                    pe.wait_ge(w_ready, MH * l + h - 1)
                d, s = PS[:, 4 + h % 2, :], PS[:, 6 + h % 2, :]
                m = row_a[0][:, P:P + T]
                a = CONST["sel_neg"][0] + P * h
                neg = const[0:MH, a:a + P]
                nc.tensor.matmul(d[:, 0:T], neg, m, start=True, stop=False, **MMr)
                nc.tensor.matmul(d[:, T:384], neg, m[:, P:T], start=False, stop=False, **MMr)
                nc.tensor.matmul(d[:, 0:P], ident, C("m_mask"), start=False, stop=True, **MMr)
                nc.tensor.matmul(d[:, T:384], ident, C("m_mask"), start=False, stop=True, **MMr)
                b = HD * (h % 2)
                q, k = ztile[b:b + HD, 6 + h // 2, :], ztile[b:b + HD, 8 + h // 2, :]
                nc.tensor.matmul(s[:, 0:T], k[:, 0:P], q, start=True, stop=True, **MMr)
                nc.tensor.matmul(s[:, T:384], k[:, P:T], q[:, P:T], start=False, stop=True, **MMr)
                a = CONST["sel_pos"][0] + P * h
                if h >= 1:
                    pe.wait_ge(x_done, 3 * (MH * l + h))
                nc.tensor.matmul(PS[:, 3, 0:T], const[0:MH, a:a + P], row_e[:, :], start=True, stop=True,
                                 **MMr).then_inc(d_ready, 1)

            def sums(h):
                pe.wait_ge(w_ready, MH * l + h + 1)
                if h >= 1:
                    pe.wait_ge(hm_done, MH * l + h)
                nd, wt = PS[:, 2, :], m_w[h % 2]
                v = [vm_tok[:, t, P * h:P * h + P] for t in range(2)]
                nc.tensor.matmul(nd[:, 0:T], v[0], wt[:, 0:T], start=True, stop=False, **MMr)
                nc.tensor.matmul(nd[:, P:T], v[1], wt[:, T:384], start=False, stop=True, **MMr)
                nc.tensor.matmul(nd[:, T:2 * T], C("ones"), wt[:, 0:T], start=False, stop=False, **MMr)
                nc.tensor.matmul(nd[:, T + P:2 * T], C("ones"), wt[:, T:384], start=False, stop=True,
                                 **MMr).then_inc(nd_ready, 1)

            def head_mean(h):
                pe.wait_ge(hsq_done, MH * l + h + 1)
                nc.tensor.matmul(PS[:, 1, 0:T], C("mean_v"), m_sq[:, :], start=True, stop=True,
                                 **MMr).then_inc(hss_ready, 1)

            decays(0)
            for h in range(MH):
                if h + 1 < MH:
                    decays(h + 1)
                sums(h)
                if h < 2:
                    gemm_tensor(pe, g, 6 + h)
                else:
                    gemm_tensor(pe, mix, h - 2)
                head_mean(h)

        def hyb_scalar(act, l):
            g, mix = G[f"gates{l}"], G[f"mix{l}"]
            nc.scalar.preload_act_table_set(LN_EXP)
            act.wait_ge(act_done, g.act0)
            if l == 0:
                act.wait_ge(vec_done, 1)
                for i in range(2):
                    nc.scalar.activation(q_gain[:, i:i + 1], column("q_norm", i, 0), ACT.Copy,
                                         scale=HD ** -0.5).then_inc(gain_done, 1)
            nc.scalar.activation(qk_buf[:, :, :], ztile[:, 0:5, :], ACT.Square).then_inc(qsq_done, 1)
            act.wait_ge(gi_done, l + 1)
            nc.scalar.activation(nlf_t[:, :, :], gate_if[:, :, MH:2 * MH], ACT.Abs).then_inc(act_step, 1)
            a_count.one()
            act.wait_ge(act_step, a_count.n)
            nc.scalar.activation(nlf_t[:, :, :], nlf_t[:, :, :], ACT.Exp, scale=-1.0).then_inc(act_step, 1)
            a_count.one()
            act.wait_ge(act_step, a_count.n)
            nc.scalar.activation(nlf_t[:, :, :], nlf_t[:, :, :], ACT.Ln, bias=1.0).then_inc(soft_f, 1)
            act.wait_ge(vtm_ready, l + 1)
            nc.scalar.activation(va_tok[:, :, :].rearrange("p t d -> p (t d)"), PS[:, 1, 0:T], ACT.Copy).then_inc(va_done, 1)
            for t in range(2):
                nc.scalar.activation(vm_tok[:, t, :], PS[:, 2 + t, :], ACT.Copy).then_inc(va_done, 1)
            eps = const[:, CONST["sgn"][0] + 3:CONST["sgn"][0] + 4]
            act.wait_ge(qss_ready, l + 1)
            flat = qk_buf[:, :, :].rearrange("p a t -> p (a t)")
            nc.scalar.activation(flat[:, 0:1024].rearrange("p (a b) -> p a b", a=2), PS[:, 4:6, :], ACT.Ln, bias=eps).then_inc(act_step, 1)
            a_count.one()
            nc.scalar.activation(flat[:, 1024:1280], PS[:, 6, 0:T], ACT.Ln, bias=eps).then_inc(act_step, 1)
            a_count.one()
            act.wait_ge(act_step, a_count.n)
            nc.scalar.activation(flat, flat, ACT.Exp, scale=-0.5).then_inc(qrs_done, 1)
            for i in range(2):
                gates_drain(act, g, i)
                gates_hi(act, g, i)
            for it in range(AP_ + 1):
                if it < AP_:
                    n = AP_ * l + it
                    act.wait_ge(mx_done, n + 1)
                    for hd in range(2):
                        for blk in range(2):
                            cols = slice(0, P) if blk == 0 else slice(P, 384)
                            nc.scalar.activation(a_prob[it % 2][:, hd, cols], PS[:, 4 + 2 * (it % 2) + hd, cols], ACT.Exp,
                                                 bias=neg_m[:, it, hd, blk:blk + 1],
                                                 accum_out=p_sum[:, it, hd, blk:blk + 1]).then_inc(p_part, 1)
                    nc.scalar.activation(sink_e[:, it, :, :], mx[:, it, :, :], ACT.Exp).then_inc(p_done, 1)
                if 1 <= it <= AP_:
                    gates_drain(act, g, it + 1)
                if it >= 1:
                    n = AP_ * l + it - 1
                    act.wait_ge(pt_ready, n + 1)
                    if it >= 2:
                        act.wait_ge(ao_ready, n)
                    nc.scalar.activation(a_probT[:, :, :], PS[:, 2:4, 0:384], ACT.Copy).then_inc(pt_done, 1)
                if 1 <= it <= AP_:
                    gates_hi(act, g, it + 1)

            def bounds(h):
                n = MH * l + h
                act.wait_ge(d_ready, n + 1)
                act.wait_ge(acol_done, l + 1)
                if h >= 2:
                    act.wait_ge(w_ready, n - 1)
                d = PS[:, 4 + h % 2, :]
                nc.scalar.activation(m_exp[h % 2][:, 0:T], d[:, 0:T], ACT.Exp, bias=a_col[:, 0, h:h + 1]).then_inc(x_done, 1)
                nc.scalar.activation(m_exp[h % 2][:, T:384], d[:, T:384], ACT.Exp, bias=a_col[:, 1, h:h + 1]).then_inc(x_done, 1)
                if h >= 2:
                    act.wait_ge(hm_done, n - 1)
                nc.scalar.activation(m_lim[h % 2][:, :], PS[:, 3, 0:T], ACT.Exp).then_inc(x_done, 1)

            bounds(0)
            for h in range(MH):
                n = MH * l + h
                if h + 1 < MH:
                    bounds(h + 1)
                act.wait_ge(hm_done, n + 1)
                if h >= 1:
                    act.wait_ge(hss_ready, n)
                nc.scalar.activation(m_sq[:, :], hm_raw[:, h % 2, :], ACT.Square).then_inc(hsq_done, 1)
                if h < 2:
                    gates_drain(act, g, 6 + h)
                act.wait_ge(hss_ready, n + 1)
                if h >= 1:
                    act.wait_ge(hid_done, g.hid0 + 4 + h)
                nc.scalar.activation(m_rs[:, :], PS[:, 1, 0:T], ACT.Ln, bias=eps).then_inc(act_step, 1)
                a_count.one()
                act.wait_ge(act_step, a_count.n)
                nc.scalar.activation(m_rs[:, :], m_rs[:, :], ACT.Exp, scale=-0.5).then_inc(hrs_done, 1)
                if h < 2:
                    gates_hi(act, g, 6 + h)
                else:
                    gemm_scalar(act, mix, h - 2)
            gates_sigmoid(act, g)

        def hyb_vector(dve, l):
            V = nc.vector
            g, mix = G[f"gates{l}"], G[f"mix{l}"]


            if l == 0:
                dve.wait_ge(ld_vec, 16 * N_VEC)
            dve.wait_ge(if_ready, l + 1)
            V.tensor_tensor(gate_if[:, :, :], PS[:, 7, 0:2 * IN_IF].rearrange("p (t f) -> p t f", t=2),
                            gate_bias[:, IN_IF * l:IN_IF * l + IN_IF].unsqueeze(1).to_broadcast([P, 2, IN_IF]),
                            ALU.add).then_inc(gi_done, 1)
            dve.wait_ge(gi_done, l + 1)
            V.tensor_scalar(nlf[:, :, :], gate_if[:, :, MH:2 * MH], -1.0, 0.0, ALU.mult, ALU.max).then_inc(dve_step, 1)
            dve.wait_ge(dve_step, v_count.one())
            dve.wait_ge(soft_f, l + 1)
            V.tensor_tensor(nlf[:, :, :], nlf[:, :, :], nlf_t[:, :, :], ALU.add).then_inc(nlf_done, 1)
            dve.wait_ge(gain_done, 2)
            dve.wait_ge(qrs_done, l + 1)
            V.scalar_tensor_tensor(out=ztile[:, 0:4, :], in0=ztile[:, 0:4, :], scalar=q_gain[:, l:l + 1], in1=qk_buf[:, 0:4, :],
                                   op0=ALU.mult, op1=ALU.mult).then_inc(qn_done, 1)
            V.scalar_tensor_tensor(out=ztile[:, 4, :], in0=ztile[:, 4, :], scalar=column("k_norm", l, 0), in1=qk_buf[:, 4, :],
                                   op0=ALU.mult, op1=ALU.mult).then_inc(qn_done, 1)
            dve.wait_ge(qn_done, 2 * l + 2)
            dve.wait_ge(if_ready, l + 1)
            V.tensor_tensor(qk_rot[:, :, :], ztile[:, 0:5, :], C("cos").unsqueeze(1).to_broadcast([P, 5, T]), ALU.mult).then_inc(dve_step, 1)
            dve.wait_ge(dve_step, v_count.one())
            dve.wait_ge(rot_ready, l + 1)
            sin = C("sin").unsqueeze(1)
            V.tensor_tensor(qk_buf[:, 0:4, :].rearrange("p (b a) t -> p b a t", b=2),
                            PS[:, 4:6, :].rearrange("p b (a t) -> p b a t", a=2),
                            sin.unsqueeze(1).to_broadcast([P, 2, 2, T]), ALU.mult).then_inc(dve_step, 1)
            dve.wait_ge(dve_step, v_count.one())
            V.tensor_tensor(qk_buf[:, 4, :], PS[:, 6, 0:T], C("sin"), ALU.mult).then_inc(dve_step, 1)
            dve.wait_ge(dve_step, v_count.one())
            V.tensor_tensor(qk_rot[:, :, :], qk_rot[:, :, :], qk_buf[:, :, :], ALU.add).then_inc(dve_step, 1)
            dve.wait_ge(dve_step, v_count.one())
            V.tensor_copy(k_dup[0:HD, 0, :], qk_rot[0:HD, 4, :])
            V.tensor_copy(k_dup[HD:P, 0, :], qk_rot[0:HD, 4, :])
            V.tensor_copy(k_dup[0:HD, 1, :], qk_rot[HD:P, 4, :])
            V.tensor_copy(k_dup[HD:P, 1, :], qk_rot[HD:P, 4, :]).then_inc(qr_done, 1)
            gates_lo(dve, g, 0)
            dve.wait_ge(rows_ready, l + 1)
            V.tensor_copy(a_col[:, :, :].rearrange("p t h -> p (t h)"),
                          PS[:, 7, 2 * IN_IF:2 * IN_IF + 2 * MH]).then_inc(acol_done, 1)
            for i in range(2):
                V.memset(row_a[i][:, 0:P], 0.0)
            V.tensor_scalar(row_a[0][:, P:P + T], PS[0:MH, 2, T:2 * T], 0.0, None, ALU.max).then_inc(dve_step, 1)
            dve.wait_ge(dve_step, v_count.one())
            for i in range(8):
                a, b = row_a[i % 2], row_a[(i + 1) % 2]
                V.tensor_tensor(b[:, P:P + T], a[:, P:P + T], a[:, P - (1 << i):P + T - (1 << i)], ALU.max).then_inc(dve_step, 1)
                dve.wait_ge(dve_step, v_count.one())
            V.tensor_tensor(row_e[:, :], PS[0:MH, 2, 0:T], row_a[0][:, P:P + T], ALU.subtract).then_inc(rows_done, 1)
            gates_lo(dve, g, 1)
            snk = sinks[:, AH * l:AH * l + AH].rearrange("p (a h) -> p a h", a=AP_)

            def normalise(p):
                n = AP_ * l + p
                dve.wait_ge(p_done, n + 1)
                dve.wait_ge(p_part, 4 * n + 4)
                V.tensor_tensor(p_inv[:, p, :, :], p_sum[:, p, :, :], sink_e[:, p, :, :], ALU.add).then_inc(dve_step, 1)
                dve.wait_ge(dve_step, v_count.one())
                V.reciprocal(p_inv[:, p, :, :], p_inv[:, p, :, :]).then_inc(dve_step, 1)
                dve.wait_ge(dve_step, v_count.one())
                for hd in range(2):
                    for blk in range(2):
                        pr = a_prob[p % 2][:, hd, 0:P] if blk == 0 else a_prob[p % 2][:, hd, P:384]
                        ins = V.tensor_scalar(pr, pr, p_inv[:, p, hd, blk:blk + 1], None, ALU.mult)
                        if hd + blk < 2:
                            ins.then_inc(dve_step, 1)
                            v_count.one()
                        else:
                            ins.then_inc(pn_done, 1)

            def head_out(p):
                n = AP_ * l + p
                dve.wait_ge(ao_ready, n + 1)
                o = PS[:, 1, 0:T]
                V.tensor_copy(hid_hi[:, p, :], o).then_inc(ao_hi, 1)
                dve.wait_ge(ao_hi, n + 1)
                V.tensor_tensor(hid_lo[:, p, :], o, hid_hi[:, p, :].bitcast(F32), ALU.subtract).then_inc(hid_done, 1)

            for it in range(AP_ + 2):
                if it < AP_:
                    n = AP_ * l + it
                    dve.wait_ge(s_ready, n + 1)
                    if it >= 2:
                        dve.wait_ge(pt_ready, n - 1)
                    s = PS[:, 4 + 2 * (it % 2):6 + 2 * (it % 2), :]
                    V.tensor_reduce(mx[:, it, :, 0], s[:, :, 0:P], AX, ALU.max)
                    V.tensor_reduce(mx[:, it, :, 1], s[:, :, P:384], AX, ALU.max).then_inc(dve_step, 1)
                    dve.wait_ge(dve_step, v_count.one())
                    sk = snk[:, it, :].unsqueeze(2).to_broadcast([P, 2, 2])
                    V.tensor_tensor(mx[:, it, :, :], mx[:, it, :, :], sk, ALU.max).then_inc(dve_step, 1)
                    dve.wait_ge(dve_step, v_count.one())
                    V.tensor_scalar(neg_m[:, it, :, :], mx[:, it, :, :], -1.0, None, ALU.mult).then_inc(dve_step, 1)
                    dve.wait_ge(dve_step, v_count.one())
                    V.tensor_tensor(mx[:, it, :, :], neg_m[:, it, :, :], sk, ALU.add).then_inc(mx_done, 1)
                if 1 <= it <= AP_:
                    normalise(it - 1)
                if it >= 2:
                    head_out(it - 2)
                if 1 <= it <= AP_:
                    gates_lo(dve, g, it + 1)

            def weights(h):
                n = MH * l + h
                dve.wait_ge(x_done, 3 * n + 2)
                if h >= 2:
                    dve.wait_ge(nd_ready, n - 1)
                V.scalar_tensor_tensor(out=m_w[h % 2][:, :], in0=PS[:, 6 + h % 2, 0:384], scalar=HD ** -0.5,
                                       in1=m_exp[h % 2][:, :], op0=ALU.mult, op1=ALU.mult).then_inc(w_ready, 1)

            weights(0)
            for h in range(MH):
                n = MH * l + h
                if h + 1 < MH:
                    weights(h + 1)
                dve.wait_ge(nd_ready, n + 1)
                dve.wait_ge(x_done, 3 * n + 3)
                V.scalar_tensor_tensor(out=m_den[:, :], in0=PS[:, 2, T:2 * T], scalar=-1.0, in1=m_lim[h % 2][:, :],
                                       op0=ALU.mult, op1=ALU.max).then_inc(dve_step, 1)
                dve.wait_ge(dve_step, v_count.one())
                V.tensor_tensor(m_den[:, :], PS[:, 2, T:2 * T], m_den[:, :], ALU.max).then_inc(dve_step, 1)
                dve.wait_ge(dve_step, v_count.one())
                V.reciprocal(m_den[:, :], m_den[:, :]).then_inc(dve_step, 1)
                dve.wait_ge(dve_step, v_count.one())
                V.tensor_tensor(hm_raw[:, h % 2, :], PS[:, 2, 0:T], m_den[:, :], ALU.mult).then_inc(hm_done, 1)
                dve.wait_ge(hm_done, n + 1)
                dve.wait_ge(hrs_done, n + 1)
                V.scalar_tensor_tensor(out=m_out[:, :], in0=hm_raw[:, h % 2, :], scalar=column("head", l, h),
                                       in1=m_rs[:, :], op0=ALU.mult, op1=ALU.mult).then_inc(dve_step, 1)
                dve.wait_ge(dve_step, v_count.one())
                V.tensor_tensor(m_out[:, :], m_out[:, :], sig_o[:, h, :], ALU.mult).then_inc(dve_step, 1)
                dve.wait_ge(dve_step, v_count.one())
                V.tensor_copy(hid_hi[:, 4 + h, :], m_out[:, :]).then_inc(hm_hi, 1)
                dve.wait_ge(hm_hi, n + 1)
                V.tensor_tensor(hid_lo[:, 4 + h, :], m_out[:, :], hid_hi[:, 4 + h, :].bitcast(F32),
                                ALU.subtract).then_inc(hid_done, 1)
                if h < 2:
                    gates_lo(dve, g, 6 + h)
                else:
                    gemm_vector(dve, mix, h - 2)

        out_sb = sb("out_sb", [P, 2, D], "xc")
        out_t, out_done, stored = S("out_t"), S("out_done"), S("stored")

        def result_tensor(pe, n_res):
            pe.wait_ge(resid_done, n_res)
            pe.wait_ge(xt_done, KT)
            for t in range(2):
                for f in range(KT):
                    last = nc.tensor.transpose(PS[:, 4 + 2 * t + f // 4, (f % 4) * P:(f % 4 + 1) * P], res[:, f, P * t:P * t + P], ident)
                    if f % 4 == 3:
                        last.then_inc(out_t, 1)

        def result_scalar(act):
            for i in range(4):
                act.wait_ge(out_t, i + 1)
                nc.scalar.activation(out_sb[:, i // 2, 512 * (i % 2):512 * (i % 2) + 512], PS[:, 4 + i, :],
                                     ACT.Copy).then_inc(out_done, 1)

        def result_sync(sp):
            for i in range(4):
                sp.wait_ge(out_done, i + 1)
                t, c = i // 2, 512 * (i % 2)
                sp.dma_start(out[P * t:P * t + P, c:c + 512], out_sb[:, t, c:c + 512]).then_inc(stored, 16)
            sp.wait_ge(stored, 64)

        soft_f, p_part = S("soft_f"), S("p_part")
        block = ctx.enter_context(nc.Block())

        @block.sync
        def _(sp):
            s5_loads(sp)
            s5_toeplitz(sp)
            sp.wait_ge(k_ready, 16)
            sp.wait_ge(e_t, 16)
            sp.wait_ge(sout_done, NB)
            for g in gemms:
                chunk_loop(sp, g.n, 4 if g.shape == "kt4" else (RING if g.c0 == 0 else 0), 0,
                           lambda idx, k, turn: load_chunk(sp, g, idx, k))
            result_sync(sp)

        @block.gpsimd
        def _(pool):
            s5_pool(pool)
            chunk_loop(pool, n_chunks, 0, 0, lambda idx, k, turn: split_lo(pool, 0, idx, k, 1, lo_pool))

        @block.tensor
        def _(pe):
            s5_tensor(pe)
            norm = 0
            for g in gemms:
                if g.evac == "sig_g":
                    hyb_tensor(pe, g.layer)
                    continue
                gemm_tensor(pe, g)
                if g.evac == "resid":
                    if norm < 8 and g.name != "ff2_1":
                        norm_tensor(pe, norm)
                        norm += 1
                    if norm == 4:
                        norm_tensor(pe, norm)
                        norm += 1
                elif g.name == "v":
                    sb_tensor(pe)
            result_tensor(pe, 32)

        @block.scalar
        def _(act):
            s5_scalar(act)
            norm = 0
            for g in gemms:
                if g.evac == "sig_g":
                    hyb_scalar(act, g.layer)
                    continue
                gemm_scalar(act, g)
                if g.evac == "resid":
                    if g.name != "ff2_1":
                        norm_scalar(act, norm)
                        norm += 1
                    if norm == 4:
                        norm_scalar(act, norm)
                        norm += 1
                elif g.name == "v":
                    sb_scalar(act)
            result_scalar(act)

        @block.vector
        def _(dve):
            s5_vector(dve)
            norm = 0
            for g in gemms:
                if g.evac == "sig_g":
                    hyb_vector(dve, g.layer)
                    continue
                gemm_vector(dve, g)
                if g.evac == "resid":
                    if g.name != "ff2_1":
                        norm_vector(dve, norm)
                        norm += 1
                    if norm == 4:
                        norm_vector(dve, norm)
                        norm += 1
                elif g.name == "v":
                    sb_vector(dve)


def kernel(**inputs):
    import numpy as _np
    import concourse.bacc as _bacc
    from concourse import mybir as _mybir
    from concourse.bass_utils import run_bass_kernel_spmd as _run

    nc = _bacc.Bacc("TRN2", target_bir_lowering=False, num_devices=1)
    arrays, aps = {}, {}
    feed = {name: _np.ascontiguousarray(a) for name, a in inputs.items()}
    feed["consts"] = constants()
    for name, a in feed.items():
        arrays[f"in_{name}_dram"] = a
        aps[name] = nc.dram_tensor(f"in_{name}_dram", a.shape, _mybir.dt.from_np(a.dtype), kind="ExternalInput").ap()
    out = nc.dram_tensor("out_0_dram", (T, D), F32, kind="ExternalOutput").ap()
    stack(nc, aps, out)
    r = _run(nc, [arrays], core_ids=[0])
    return r.results[0]["out_0_dram"].reshape(1, T, D)
```
